# Optimizing a Trainium2 kernel written in Bass

```python
import numpy as np
import jax
import jax.numpy as jnp
from jax import lax

D_MODEL = 1024
BATCH = 1
SEQ = 256
DEPTH = 2

CHUNK = 64
D_MIX = D_MODEL
N_SUB = 3
EPS = 1e-6
D_FF = ((8 * D_MODEL // 3 + 127) // 128) * 128

M_HEADS = 4
M_DQK = D_MODEL // 16
M_DV = D_MODEL // 8
M_WIDTH = M_HEADS * M_DV
GATE_CAP = 15.0

CONV_WIDTH = D_MODEL // 4
CONV_K = 3

A_HEADS = 4
A_KV_HEADS = 2
A_GROUP = A_HEADS // A_KV_HEADS
A_DH = D_MODEL // 16
A_WIDTH = A_HEADS * A_DH
WINDOW = 128
WIN_CHUNKS = WINDOW // CHUNK
N_BUCKETS = 32
MAX_DISTANCE = 128

SPLIT_SIZES = (M_HEADS * M_DQK, M_HEADS * M_DQK, M_WIDTH, M_HEADS, M_HEADS, M_WIDTH,
               CONV_WIDTH, CONV_WIDTH, CONV_WIDTH,
               A_HEADS * A_DH, A_KV_HEADS * A_DH, A_KV_HEADS * A_DH)
P_IN = sum(SPLIT_SIZES)

kernel_name = 'hybrid_mlstm_conv_swa_block'

def rmsnorm(x, g):
    xf = x.astype(jnp.float32)
    y = xf * lax.rsqrt(jnp.mean(xf * xf, axis=-1, keepdims=True) + EPS)
    return (y * g.astype(jnp.float32)).astype(x.dtype)

def swiglu(h, wg, wu, wd):
    return (jax.nn.silu(h @ wg) * (h @ wu)) @ wd

def soft_cap(t):
    return GATE_CAP * jnp.tanh(t / GATE_CAP)

def mlstm_chunkwise(q, k, v, i_pre, f_pre):
    f32 = jnp.float32
    B, H, S, dk = q.shape
    dv = v.shape[-1]
    L = CHUNK
    N = S // L
    q = q.astype(f32).reshape(B, H, N, L, dk) * (dk ** -0.5)
    k = k.astype(f32).reshape(B, H, N, L, dk)
    v = v.astype(f32).reshape(B, H, N, L, dv)
    logi = i_pre.astype(f32).reshape(B, H, N, L)
    g = jnp.cumsum(jax.nn.log_sigmoid(f_pre.astype(f32)).reshape(B, H, N, L), axis=-1)
    g_end = g[..., -1]
    w_end = g_end[..., None] - g + logi
    m_loc = jnp.max(w_end, axis=-1)
    e = jnp.exp(w_end - m_loc[..., None])
    dC = jnp.einsum('bhnlk,bhnlv->bhnkv', e[..., None] * k, v)
    dn = jnp.einsum('bhnl,bhnlk->bhnk', e, k)

    def step(carry, inp):
        C, n, m = carry
        dC_j, dn_j, ml_j, G_j = inp
        m_new = jnp.maximum(G_j + m, ml_j)
        a = jnp.exp(G_j + m - m_new)
        b = jnp.exp(ml_j - m_new)
        C_new = a[..., None, None] * C + b[..., None, None] * dC_j
        n_new = a[..., None] * n + b[..., None] * dn_j
        return (C_new, n_new, m_new), (C, n, m)

    init = (jnp.zeros((B, H, dk, dv), f32), jnp.zeros((B, H, dk), f32),
            jnp.full((B, H), -jnp.inf, f32))
    xs = (jnp.moveaxis(dC, 2, 0), jnp.moveaxis(dn, 2, 0),
          jnp.moveaxis(m_loc, 2, 0), jnp.moveaxis(g_end, 2, 0))
    _, (C_prev, n_prev, m_prev) = lax.scan(step, init, xs)
    C_prev = jnp.moveaxis(C_prev, 0, 2)
    n_prev = jnp.moveaxis(n_prev, 0, 2)
    m_prev = jnp.moveaxis(m_prev, 0, 2)

    causal = jnp.tril(jnp.ones((L, L), dtype=bool))
    log_d = jnp.where(causal, g[..., :, None] - g[..., None, :] + logi[..., None, :], -jnp.inf)
    log_inter = g + m_prev[..., None]
    m_t = jnp.maximum(log_inter, jnp.max(log_d, axis=-1))
    d = jnp.exp(log_d - m_t[..., None])
    s = jnp.einsum('bhntd,bhnsd->bhnts', q, k) * d
    w_inter = jnp.exp(log_inter - m_t)
    num = (jnp.einsum('bhnts,bhnsv->bhntv', s, v)
           + w_inter[..., None] * jnp.einsum('bhntk,bhnkv->bhntv', q, C_prev))
    den = jnp.sum(s, axis=-1) + w_inter * jnp.einsum('bhntk,bhnk->bhnt', q, n_prev)
    h = num / jnp.maximum(jnp.abs(den), jnp.exp(-m_t))[..., None]
    return h.reshape(B, H, S, dv)

def gated_short_conv(bg, cg, xc, w):
    u = cg * xc
    y = lax.conv_general_dilated(u, w[:, None, :].astype(u.dtype), window_strides=(1,),
                                 padding=[(CONV_K - 1, 0)],
                                 dimension_numbers=('NWC', 'WIO', 'NWC'),
                                 feature_group_count=u.shape[-1])
    return bg * y

def t5_bucket_ids():
    qpos = np.arange(CHUNK)[:, None] + (WIN_CHUNKS - 1) * CHUNK
    kpos = np.arange(WIN_CHUNKS * CHUNK)[None, :]
    rel = kpos - qpos
    nb = N_BUCKETS // 2
    max_exact = nb // 2
    n = np.abs(rel)
    large = max_exact + (np.log(np.maximum(n, 1) / max_exact)
                         / np.log(MAX_DISTANCE / max_exact) * (nb - max_exact)).astype(np.int32)
    large = np.minimum(large, nb - 1)
    return ((rel > 0).astype(np.int32) * nb + np.where(n < max_exact, n, large)).astype(np.int32)

def band(t):
    N = t.shape[1]
    pad = jnp.pad(t, ((0, 0), (WIN_CHUNKS - 1, 0), (0, 0), (0, 0), (0, 0)))
    return jnp.concatenate([pad[:, w:w + N] for w in range(WIN_CHUNKS)], axis=2)

def swa_sink_attention(q, k, v, sinks, rel_table):
    f32 = jnp.float32
    B, S, _ = q.shape
    L = CHUNK
    N = S // L
    WL = WIN_CHUNKS * L
    q = q.reshape(B, N, L, A_KV_HEADS, A_GROUP, A_DH)
    kb = band(k.reshape(B, N, L, A_KV_HEADS, A_DH))
    vb = band(v.reshape(B, N, L, A_KV_HEADS, A_DH))
    s = jnp.einsum('bnqhgd,bnkhd->bnhgqk', q, kb).astype(f32) * (A_DH ** -0.5)
    bias = rel_table.astype(f32)[t5_bucket_ids()]
    bias = jnp.transpose(bias, (2, 0, 1)).reshape(A_KV_HEADS, A_GROUP, L, WL)
    key_chunk = np.arange(N)[:, None] - (WIN_CHUNKS - 1) + (np.arange(WL) // L)[None, :]
    valid = jnp.asarray(key_chunk >= 0)
    s = jnp.where(valid[None, :, None, None, None, :], s + bias, -jnp.inf)
    sink = sinks.astype(f32).reshape(A_KV_HEADS, A_GROUP)[None, None, :, :, None, None]
    m = jnp.maximum(jnp.max(s, axis=-1, keepdims=True), sink)
    p = jnp.exp(s - m)
    p = p / (jnp.sum(p, axis=-1, keepdims=True) + jnp.exp(sink - m))
    o = jnp.einsum('bnhgqk,bnkhd->bnqhgd', p.astype(vb.dtype), vb)
    return o.reshape(B, S, A_WIDTH)

def hybrid_mixer(h, w_in, ig_b, fg_b, head_gain, conv_w, sinks, rel_table, w_out):
    B, S, _ = h.shape
    proj = h @ w_in
    split_points = np.cumsum(SPLIT_SIZES)[:-1].tolist()
    mq, mk, mv, mi, mf, mo, cb, cc, cx, aq, ak, av = jnp.split(proj, split_points, axis=-1)

    def to_heads(t, dh):
        return t.reshape(B, S, -1, dh).transpose(0, 2, 1, 3)
    i_pre = soft_cap(mi.astype(jnp.float32) + ig_b.astype(jnp.float32)).transpose(0, 2, 1)
    f_pre = soft_cap(mf.astype(jnp.float32) + fg_b.astype(jnp.float32)).transpose(0, 2, 1)
    hm = mlstm_chunkwise(to_heads(mq, M_DQK), to_heads(mk, M_DQK), to_heads(mv, M_DV), i_pre, f_pre)
    hm = hm * lax.rsqrt(jnp.mean(hm * hm, axis=-1, keepdims=True) + EPS)
    hm = hm.transpose(0, 2, 1, 3).reshape(B, S, M_WIDTH) * head_gain.astype(jnp.float32)
    out_m = (jax.nn.sigmoid(mo.astype(jnp.float32)) * hm).astype(h.dtype)

    out_c = gated_short_conv(cb, cc, cx, conv_w).astype(h.dtype)

    out_a = swa_sink_attention(aq, ak, av, sinks, rel_table).astype(h.dtype)

    return jnp.concatenate([out_m, out_c, out_a], axis=-1) @ w_out

def modulated_sublayer(x, fn, mods_i, g_pre, g_post, res_w):
    shift = mods_i[:, 0, None, :]
    scale = mods_i[:, 1, None, :]
    gate = mods_i[:, 2, None, :]
    h = rmsnorm(x, g_pre) * (1 + scale) + shift
    y = rmsnorm(fn(h), g_post)
    return x + res_w * (1 + gate) * y

def setup_inputs(seed: int = 0) -> dict:
    key = jax.random.key(seed)
    ks = jax.random.split(key, 18)
    f32 = jnp.float32
    D = D_MODEL

    def nrm(k, shape, scale):
        return jax.random.normal(k, shape, f32) * scale

    return {
        'x': nrm(ks[0], (BATCH, SEQ, D), 1.0),
        'c': nrm(ks[1], (BATCH, D), 1.0),
        'ada_w': nrm(ks[2], (DEPTH, D, N_SUB * 3 * D), 0.5 * D ** -0.5),
        'ada_b': nrm(ks[3], (DEPTH, N_SUB * 3 * D), 0.01),
        'norm_pre': 1.0 + nrm(ks[4], (DEPTH, N_SUB, D), 0.05),
        'norm_post': 1.0 + nrm(ks[5], (DEPTH, N_SUB, D), 0.05),
        'ffn_w_gate': nrm(ks[6], (DEPTH, 2, D, D_FF), D ** -0.5),
        'ffn_w_up': nrm(ks[7], (DEPTH, 2, D, D_FF), D ** -0.5),
        'ffn_w_down': nrm(ks[8], (DEPTH, 2, D_FF, D), D_FF ** -0.5),
        'w_in': nrm(ks[9], (DEPTH, D, P_IN), D ** -0.5),
        'mlstm_igate_bias': nrm(ks[10], (DEPTH, M_HEADS), 0.1),
        'mlstm_fgate_bias': jnp.linspace(3.0, 6.0, M_HEADS, dtype=f32)[None, :]
                            + nrm(ks[11], (DEPTH, M_HEADS), 0.1),
        'mlstm_head_norm': 1.0 + nrm(ks[12], (DEPTH, M_WIDTH), 0.05),
        'conv_w': nrm(ks[13], (DEPTH, CONV_K, CONV_WIDTH), CONV_K ** -0.5),
        'attn_sinks': nrm(ks[14], (DEPTH, A_HEADS), 0.5),
        'rel_bias_table': nrm(ks[15], (N_BUCKETS, A_HEADS), 0.5),
        'w_out': nrm(ks[16], (DEPTH, D_MIX, D), D_MIX ** -0.5),
    }

def reference(x, c, ada_w, ada_b, norm_pre, norm_post, ffn_w_gate, ffn_w_up, ffn_w_down,
              w_in, mlstm_igate_bias, mlstm_fgate_bias, mlstm_head_norm, conv_w,
              attn_sinks, rel_bias_table, w_out):
    B = x.shape[0]
    for l in range(DEPTH):
        mods = (jax.nn.silu(c) @ ada_w[l] + ada_b[l]).reshape(B, N_SUB, 3, D_MODEL)
        x = modulated_sublayer(
            x, lambda h: swiglu(h, ffn_w_gate[l, 0], ffn_w_up[l, 0], ffn_w_down[l, 0]),
            mods[:, 0], norm_pre[l, 0], norm_post[l, 0], 0.5)
        x = modulated_sublayer(
            x, lambda h: hybrid_mixer(h, w_in[l], mlstm_igate_bias[l], mlstm_fgate_bias[l],
                                      mlstm_head_norm[l], conv_w[l], attn_sinks[l],
                                      rel_bias_table, w_out[l]),
            mods[:, 1], norm_pre[l, 1], norm_post[l, 1], 1.0)
        x = modulated_sublayer(
            x, lambda h: swiglu(h, ffn_w_gate[l, 1], ffn_w_up[l, 1], ffn_w_down[l, 1]),
            mods[:, 2], norm_pre[l, 2], norm_post[l, 2], 0.5)
    return x


_drawn_inputs = setup_inputs


def setup_inputs(seed=0):
    import zlib

    import numpy as np

    out = dict(_drawn_inputs(seed))
    spreads = {}
    factors = {'mlstm_igate_bias': 64.0, 'attn_sinks': 8.0}
    for name, (base, spread) in spreads.items():
        noise = np.random.default_rng([zlib.crc32(name.encode()), seed]).standard_normal(out[name].shape)
        drawn = base * np.exp(spread * noise) if base else spread * noise
        out[name] = jnp.asarray(drawn.astype(out[name].dtype))
    for name, factor in factors.items():
        out[name] = (out[name] * factor).astype(out[name].dtype)
    return out
```

```python
from contextlib import ExitStack

import numpy as np

import concourse.bass as bass
from concourse import mybir

F32 = mybir.dt.float32
F32R = mybir.dt.float32r
ALU = mybir.AluOpType
ACT = mybir.ActivationFunctionType
AX_X = mybir.AxisListType.X

P = 128
D = 1024
S = 256
DEPTH = 2
KT = D // P
D_FF = 2816
PC = 256
NF = D_FF // PC
N_SUB = 3
EPS = 1e-6
CAP = 15.0
MH, DQK, DV = 4, 64, 128
AH, AKV, AG, DH = 4, 2, 2, 64
CHUNK = 64
NCH = S // CHUNK
N_BUCKETS, MAX_DISTANCE = 32, 128
P_IN = 2824
COL_GATES = 1024
MASKED = -1e30
CREDIT = 1

IN_COLS = dict(mq=0, mk=256, aq=2312, akv=2568, mv0=512, mv1=768, mo0=1032, mo1=1288, cc=1800, cx=2056, cb=1544)
IN_ORDER = ["mq", "mk", "aq", "akv", "mv0", "mv1", "mo0", "mo1", "cc", "cx", "cb"]
N_IN = len(IN_ORDER)
N_OUT = D // PC
N_READ = N_IN - 1
N_MIX = N_IN + N_OUT
MIX_USES = N_MIX // 3
USES = 2 * NF + MIX_USES
MIX0 = NF
FFB0 = NF + MIX_USES
G, U, DN = 0, 1, 2

NA = N_SUB * 3 * D // PC
EARLY = NF
A0, B0 = (EARLY + 1) // 2, EARLY // 2
A_USES, B_USES = NF + 2, NF + 1 + NF

BK_GATE, BK_UP, BK_B, BK_A = 4, 5, 6, 7

C_ID, C_CAP, C_HOT, C_SELI, C_SELF, C_NM, C_NG = 0, 128, 384, 576, 580, 584, 1096
C_ALL = 1608


def constant_table():
    c = np.zeros((P, C_ALL), np.float32)
    c[:, C_ID:C_ID + P] = np.eye(P)
    c[:, C_CAP:C_CAP + P] = np.where(np.arange(P)[:, None] <= np.arange(P)[None, :], 0.0, MASKED)
    rel = np.arange(3 * CHUNK - 1) - (2 * CHUNK - 1)
    nb = N_BUCKETS // 2
    exact = nb // 2
    n = np.abs(rel)
    large = exact + (np.log(np.maximum(n, 1) / exact) / np.log(MAX_DISTANCE / exact) * (nb - exact)).astype(np.int32)
    bucket = (rel > 0).astype(np.int32) * nb + np.where(n < exact, n, np.minimum(large, nb - 1))
    c[bucket, C_HOT + np.arange(rel.size)] = 1.0
    for h in range(MH):
        c[h, C_SELI + h] = CAP
        c[MH + h, C_SELF + h] = -1.0
        c[h, C_NM + h * P:C_NM + (h + 1) * P] = -1.0
        c[MH + h, C_NG + h * P:C_NG + (h + 1) * P] = -1.0
    return c


def build(nc, x, c, ada_w, ada_b, norm_pre, norm_post, w_gate, w_up, w_down, w_in, ig_b, fg_b, head_norm,
          conv_w, sinks, rel_table, w_out, consts, out):
    gate_rows = w_gate.rearrange("l s d f -> (l s d) f")
    up_rows = w_up.rearrange("l s d f -> (l s d) f")
    down_rows = w_down.rearrange("l s f d -> (l s f) d")
    in_rows = w_in.rearrange("l d f -> (l d) f")
    out_rows = w_out.rearrange("l d f -> (l d) f")
    ada_rows = ada_w.rearrange("l d f -> (l d) f")
    skew = nc.dram_tensor("skew", (P, AG * 3 * CHUNK), F32, kind="Internal").ap()

    with ExitStack() as ctx:
        def sb(name, shape, dt=F32):
            return ctx.enter_context(nc.sbuf_tensor(name, shape, dt))

        def sem(name):
            return ctx.enter_context(nc.semaphore(name))

        ps = ctx.enter_context(nc.psum_tensor("ps", [P, 8, 512], F32))

        raw = [sb(f"raw{s}", [P, KT * PC]) for s in range(3)]
        hi = [sb(f"hi{s}", [P, KT * PC], F32R) for s in range(3)]
        lo = [sb(f"lo{s}", [P, KT * PC], F32R) for s in range(3)]
        ada_raw = [sb(f"ada_raw{s}", [P, KT, PC]) for s in range(2)]
        ada_acc = [sb(f"ada_acc{s}", [P, PC]) for s in range(2)]
        xT = sb("xT", [P, KT, S])
        a_hi = sb("a_hi", [P, KT, S], F32R)
        a_lo = sb("a_lo", [P, KT, S], F32R)
        sq = sb("sq", [P, KT, S])
        tmp = sb("tmp", [P, KT, S])
        h32 = sb("h32", [P, KT, S])
        std = sb("std", [P, S])
        rstd = sb("rstd", [P, S])
        ffn_tmp = sb("ffn_tmp", [P, 2, 2 * S])
        silu_g, glu = ffn_tmp[:, 0, :], ffn_tmp[:, 1, :]
        u_hi = sb("u_hi", [P, 2, S], F32R)
        u_lo = sb("u_lo", [P, 2, S], F32R)
        cst = sb("cst", [P, C_ALL])
        ones = sb("ones", [P, S])
        zeros = sb("zeros", [P, P])
        m_hi = sb("m_hi", [P, KT - 2, S], F32R)
        m_lo = sb("m_lo", [P, KT - 2, S], F32R)
        eps = sb("eps", [P, 1])
        rows = sb("rows", [P, 3, P])
        cols = sb("cols", [P, 3 * P])
        adab = sb("adab", [P, (DEPTH + 1) * 72])
        c_col = sb("c_col", [P, KT])
        mods = sb("mods", [P, 72])
        mod_a = sb("mod_a", [P, KT])
        mod_c = sb("mod_c", [P, KT])
        tab = sb("tab", [N_BUCKETS, AH])
        tabx = sb("tabx", [N_BUCKETS, AG, AKV, CHUNK])
        bias = sb("bias", [P, AG, NCH, 2 * CHUNK])
        sink = sb("sink", [P, DEPTH, AG])
        sink8 = sb("sink8", [P, AG, NCH])
        gb = sb("gb", [2 * MH, DEPTH])
        gb15 = sb("gb15", [2 * MH, DEPTH])
        wg = sb("wg", [P, KT, 2 * MH])
        qT = sb("qT", [P, 2, S])
        kT = sb("kT", [P, 2, S])
        trow, bias1 = qT[:, :, 0:3 * CHUNK], kT[:, :, 0:2 * CHUNK]
        vm = sb("vm", [P, 2, MH * DV])
        aqT = sb("aqT", [P, AG, S])
        akT = sb("akT", [P, S])
        av = sb("av", [P, 3, P])
        th_o, yc, cc_s = h32[:, 0:4, :], h32[:, 4:6, :], sq[:, 4:6, :]
        hm, sc = tmp[:, 4:8, :], tmp[:, 0:4, :].rearrange("p k s -> p (k s)").rearrange("p (r n) -> p r n", n=P)
        pT = ffn_tmp[:].rearrange("p k s -> p (k s)").rearrange("p (r n) -> p r n", n=P)
        th = sb("th", [2 * MH, S])
        sp = sb("sp", [2 * MH, S])
        sp2 = sb("sp2", [2 * MH, S])
        gsum = sb("gsum", [2 * MH, S])
        arow = sb("arow", [MH, S])
        mrow = sb("mrow", [MH, S])
        acol = sb("acol", [P, 2, MH])
        floor = sb("floor", [P, S])
        ecap = sb("ecap", [P, 3 * P])
        edec = sb("edec", [P, 3 * P])
        pm = sb("pm", [P, 3 * P])
        dd = sb("dd", [P, S])
        rd = sb("rd", [P, S])
        mx = sb("mx", [P, 3, AG * NCH])
        sums = sb("sums", [P, 4, AG * NCH])
        up_s = sb("up_s", [P, 2, S + 2])

        ident = cst[:, C_ID:C_ID + P]
        pre_col = P + 72
        HEAD, CONV, CC = 2 * P, 2 * P + 8, 2 * P + 20

        def mix_tile(parts, k0):
            if k0 == 4:
                return (u_hi if parts == "hi" else u_lo)[:]
            t = m_hi if parts == "hi" else m_lo
            k1 = k0 if k0 < 4 else k0 - 2
            return t[:, k1:k1 + 2, :]

        raw_loaded = [sem(f"raw_loaded{s}") for s in range(3)]
        hi_ready = [sem(f"hi_ready{s}") for s in range(3)]
        lo_ready = [sem(f"lo_ready{s}") for s in range(3)]
        panel_used = [sem(f"panel_used{s}") for s in range(3)]
        ada_loaded = [sem(f"ada_loaded{s}") for s in range(2)]
        ada_link = [sem(f"ada_link{s}") for s in range(2)]
        ada_summed = [sem(f"ada_summed{s}") for s in range(2)]
        ada_turned = [sem(f"ada_turned{s}") for s in range(2)]
        mods_ready = [sem(f"mods_ready{s}") for s in range(2)]
        consts_in, c_in, x_in, small_in, ones_set, tab_in = (sem(n) for n in
            ("consts_in", "c_in", "x_in", "small_in", "ones_set", "tab_in"))
        cols_turned, cols_ready, silu_c_ready, x_turned, x_ready = (sem(n) for n in
            ("cols_turned", "cols_ready", "silu_c_ready", "x_turned", "x_ready"))
        prep, tabx_ready, t_rows, t_rows_out, skew_out, skew_in, bias_ready = (sem(n) for n in
            ("prep", "tabx_ready", "t_rows", "t_rows_out", "skew_out", "skew_in", "bias_ready"))
        y_done, ysq_ready, ysum_ready, ystd_ready, post_link, x_tile, xsq_ready, xsum_ready, xstd_ready = (
            sem(n) for n in ("y_done", "ysq_ready", "ysum_ready", "ystd_ready", "post_link", "x_tile",
                             "xsq_ready", "xsum_ready", "xstd_ready"))
        pre_link, t_ready, h_hi, h_lo, h_f32 = (sem(n) for n in ("pre_link", "t_ready", "h_hi", "h_lo", "h_f32"))
        y_scaled, rx_ready, sm_link, pr_link = (sem(n) for n in ("y_scaled", "rx_ready", "sm_link", "pr_link"))
        silu_ready, glu_ready, u_hi_ready, u_lo_ready = (sem(n) for n in (
            "silu_ready", "glu_ready", "u_hi_ready", "u_lo_ready"))
        wg_in = sem("wg_in")
        gates_done, th_ready, ez_ready, sp_ready, g_ready, a_done, arow_ready, m_ready = (sem(n) for n in (
            "gates_done", "th_ready", "ez_ready", "sp_ready", "g_ready", "a_done", "arow_ready", "m_ready"))
        proj_read = sem("proj_read")
        av_ready = sem("av_ready")
        scores_done, s_link, smax_ready, probs_exp, sink_exp, probs_ready = (sem(n) for n in (
            "scores_done", "s_link", "smax_ready", "probs_exp", "sink_exp", "probs_ready"))
        probs_turned, pT_ready, attn_done, attn_read = (sem(n) for n in (
            "probs_turned", "pT_ready", "attn_done", "attn_read"))
        decay_done, qk_done, floor_ready, cap_ready, dec_ready, pm_ready, num_done, hm_link, hm_ready, hmsq_ready = (
            sem(n) for n in ("decay_done", "qk_done", "floor_ready", "cap_ready", "dec_ready", "pm_ready",
                             "num_done", "hm_link", "hm_ready", "hmsq_ready"))
        hmsum_done, hmstd_ready, out_link, mix_f32, mix_hi, mix_lo, conv_link = (sem(n) for n in (
            "hmsum_done", "hmstd_ready", "out_link", "mix_f32", "mix_hi", "mix_lo", "conv_link"))
        o_turned, o_ready, out_stored = sem("o_turned"), sem("o_ready"), sem("out_stored")

        block = ctx.enter_context(nc.Block())

        def panel(t, s):
            return t[s][:].rearrange("p (k n) -> p k n", n=PC)

        def rowpanel(t, s):
            return t[s][:].rearrange("p (k n) -> p k n", n=D)

        def by_group(t, g, turned):
            v = panel(t, 2)
            if turned:
                return v.rearrange("p k (g v d) -> p k g v d", v=AKV, g=AG)[:, :, g, :, :]
            return v.rearrange("p k (v g d) -> p k v g d", v=AKV, g=AG)[:, :, :, g, :]

        def mix_used(eng, l, m):
            eng.wait_ge(panel_used[m % 3], CREDIT + USES * l + (MIX0 + m // 3 + 1))

        @block.sync
        def _(sp_e):
            def load(s, l, n, dst, src):
                sp_e.wait_ge(lo_ready[s], CREDIT + USES * l + n)
                sp_e.dma_start(dst, src).then_inc(raw_loaded[s], 16)

            def wide(rows_, r0, c0):
                return rows_[bass.ds(r0, D), bass.ds(c0, PC)].rearrange("(k p) n -> p k n", p=P)

            def load_gate(l, ffn, n0, i, now=None):
                src = wide(gate_rows, l * (2 * D) + ffn * D, i * PC)
                load(G, l if now is None else now, n0 + i if now is None else USES, panel(raw, G), src)

            def load_up(l, ffn, n0, i, now=None):
                src = wide(up_rows, l * (2 * D) + ffn * D, i * PC)
                load(U, l if now is None else now, n0 + i if now is None else USES, panel(raw, U), src)

            def load_down(l, ffn, n0, i):
                src = down_rows[bass.ds(l * (2 * D_FF) + ffn * D_FF + i * PC, PC), :].rearrange("(k p) n -> p k n", p=P)
                load(DN, l, n0 + i, rowpanel(raw, DN), src)

            def load_ada(s, use, layer, q):
                sp_e.wait_ge(ada_summed[s], CREDIT + use)
                sp_e.dma_start(ada_raw[s][:], wide(ada_rows, layer * D, q * PC)).then_inc(ada_loaded[s], 16)

            sp_e.dma_start(rows[0:72, 0, :], ada_b[0].rearrange("(r n) -> r n", n=P)).then_inc(c_in, 16)
            sp_e.dma_start(rows[72:120, 0, :], norm_pre.rearrange("l s (r n) -> (l s r) n", n=P)).then_inc(c_in, 16)
            sp_e.dma_start(rows[0:72, 1, :], ada_b[1].rearrange("(r n) -> r n", n=P)).then_inc(c_in, 16)
            sp_e.dma_start(rows[72:120, 1, :], norm_post.rearrange("l s (r n) -> (l s r) n", n=P)).then_inc(c_in, 16)
            sp_e.dma_start(rows[0:8, 2, :], head_norm.rearrange("l (r n) -> (l r) n", n=P)).then_inc(c_in, 16)
            sp_e.dma_start(rows[8:20, 2, :], conv_w.rearrange("l k (r n) -> (l k r) n", n=P)).then_inc(c_in, 16)
            sp_e.dma_start(rows[20:28, 2, :], c.rearrange("b (r n) -> (b r) n", n=P)).then_inc(c_in, 16)
            sp_e.dma_start(cst[:], consts).then_inc(consts_in, 16)
            for q in range(4):
                load_ada(q % 2, q // 2, 0, q)
            xv = x.rearrange("b (t p) d -> (b p) t d", p=P)
            sp_e.dma_start(tmp[:].rearrange("p k s -> p (k s)").rearrange("p (t d) -> p t d", t=2), xv).then_inc(x_in, 16)
            for q in range(4, EARLY):
                load_ada(q % 2, q // 2, 0, q)
                if q == 4:
                    sp_e.dma_start(panel(raw, G), wide(gate_rows, 0, 0)).then_inc(raw_loaded[G], 16)
                if q == 6:
                    sp_e.dma_start(panel(raw, U), wide(up_rows, 0, 0)).then_inc(raw_loaded[U], 16)

            with sp_e.Fori(0, DEPTH) as l:
                after = (l + 1) % DEPTH

                def ffn_loads(ffn, n0, first):
                    with sp_e.Fori(0, NF - 1) as i:
                        load_gate(l, ffn, n0, i + 1)
                        if first:
                            load_ada(0, A_USES * l + (A0 + i), l, EARLY + 2 * i)
                        load_down(l, ffn, n0, i)
                        load_up(l, ffn, n0, i + 1)
                        if first:
                            load_ada(1, B_USES * l + (B0 + i), l, EARLY + 1 + 2 * i)
                        else:
                            load_ada(1, B_USES * l + (B0 + NF + 1 + i), after, i)

                def load_mix(m):
                    src = wide(in_rows, l * D, IN_COLS[IN_ORDER[m]]) if m < N_IN else \
                        wide(out_rows, l * D, (m - N_IN) * PC)
                    load(m % 3, l, MIX0 + m // 3, panel(raw, m % 3), src)

                ffn_loads(0, 0, True)
                load_mix(0)
                load_ada(0, A_USES * l + (A0 + NF - 1), l, EARLY + 2 * (NF - 1))
                load_down(l, 0, 0, NF - 1)
                load_mix(1)
                load_ada(1, B_USES * l + (B0 + NF - 1), l, EARLY + 1 + 2 * (NF - 1))
                load_mix(2)
                sp_e.wait_ge(gates_done, CREDIT + l)
                sp_e.dma_start(wg[:], in_rows[bass.ds(l * D, D), COL_GATES:COL_GATES + 2 * MH]
                               .rearrange("(k p) n -> p k n", p=P)).then_inc(wg_in, 16)
                for m in range(3, N_MIX):
                    load_mix(m)
                    if m == 7:
                        load_ada(0, A_USES * l + (A0 + NF), l, NA - 3)
                    if m == 9:
                        load_ada(1, B_USES * l + (B0 + NF), l, NA - 2)
                    if m == 11:
                        load_ada(0, A_USES * l + (A0 + NF + 1), l, NA - 1)
                load_gate(l, 1, FFB0, 0)
                load_up(l, 1, FFB0, 0)
                ffn_loads(1, FFB0, False)
                load_gate(after, 0, 0, 0, l)
                load_down(l, 1, FFB0, NF - 1)
                load_up(after, 0, 0, 0, l)
                load_ada(1, B_USES * l + (B0 + NF + NF), after, NF - 1)
            for t in range(2):
                sp_e.wait_ge(o_ready, 2 * (t + 1))
                sp_e.dma_start(out[0, t * P:(t + 1) * P, :], tmp[:, 4 * t:4 * t + 4, :].rearrange("p k s -> p (k s)")) \
                    .then_inc(out_stored, 16)
            sp_e.wait_ge(out_stored, 32)
            for s in (G, U):
                sp_e.wait_ge(raw_loaded[s], 16 * (DEPTH * USES + 1))

        @block.gpsimd
        def _(pool):
            nc.gpsimd.memset(ones[:], 1.0).then_inc(ones_set, 1)
            nc.gpsimd.memset(zeros[:], 0.0).then_inc(ones_set, 1)
            nc.gpsimd.memset(eps[:], EPS).then_inc(ones_set, 1)
            nc.gpsimd.memset(up_s[:], 0.0).then_inc(ones_set, 1)
            pool.dma_start(tab[:], rel_table).then_inc(tab_in, 16)
            with nc.allow_non_contiguous_dma(reason="a few words of gate biases and sinks"):
                pool.dma_start(gb[0:MH, :], ig_b.rearrange("l h -> h l")).then_inc(small_in, 16)
                pool.dma_start(gb[MH:2 * MH, :], fg_b.rearrange("l h -> h l")).then_inc(small_in, 16)
                for kv in range(AKV):
                    pool.dma_start(sink[kv * CHUNK:(kv + 1) * CHUNK, :, :],
                                   sinks[:, kv * AG:(kv + 1) * AG].rearrange("(o l) g -> o l g", o=1)
                                   .to_broadcast([CHUNK, DEPTH, AG])).then_inc(small_in, 16)
            pool.wait_ge(tab_in, 16)
            for g in range(AG):
                for kv in range(AKV):
                    nc.gpsimd.tensor_copy(tabx[:, g, kv, :], tab[:, kv * AG + g:kv * AG + g + 1]
                                          .to_broadcast([N_BUCKETS, CHUNK])).then_inc(tabx_ready, 1)
            pool.wait_ge(t_rows_out, 1)
            pool.dma_start(skew.rearrange("p (g r) -> p g r", g=AG), trow).then_inc(skew_out, 16)
            pool.wait_ge(skew_out, 16)
            W = AG * 3 * CHUNK
            for kv in range(AKV):
                o = kv * CHUNK * W + CHUNK - 1
                src = skew.rearrange("p r -> (p r)")[o:o + CHUNK * (W - 1)] if o + CHUNK * (W - 1) <= P * W else None
                v = src.rearrange("(q r) -> q r", r=W - 1)
                for g in range(AG):
                    pool.dma_start(bias1[kv * CHUNK:(kv + 1) * CHUNK, g, :],
                                   v[:, g * 3 * CHUNK:g * 3 * CHUNK + 2 * CHUNK]).then_inc(skew_in, 16)
            pool.wait_ge(skew_in, 64)
            for g in range(AG):
                for j in range(1, NCH):
                    nc.gpsimd.tensor_copy(bias[:, g, j, :], bias1[:, g, :]).then_inc(bias_ready, 1)
                nc.gpsimd.tensor_copy(bias[:, g, 0, 0:CHUNK], bias1[:, g, CHUNK:]).then_inc(bias_ready, 1)
                nc.gpsimd.memset(bias[:, g, 0, CHUNK:], MASKED).then_inc(bias_ready, 1)

        @block.scalar
        def _(act):
            def split(s, l, n):
                act.wait_ge(raw_loaded[s], 16 * (USES * l + n + 1))
                act.wait_ge(panel_used[s], CREDIT + USES * l + n)
                nc.scalar.activation(hi[s][:], raw[s][:], ACT.Copy).then_inc(hi_ready[s], 1)

            def split_aq(l):
                act.wait_ge(raw_loaded[2], 16 * (USES * l + MIX0 + 1))
                act.wait_ge(panel_used[2], CREDIT + USES * l + MIX0)
                for g in range(AG):
                    last = nc.scalar.activation(by_group(hi, g, True), by_group(raw, g, False), ACT.Copy)
                last.then_inc(hi_ready[2], 1)

            for signal in (silu_ready, floor_ready, dec_ready):
                act.sem_inc(signal, CREDIT)
            act.wait_ge(cols_ready, 3)
            nc.scalar.activation(c_col[:], cols[:, CC:CC + KT], ACT.Silu).then_inc(silu_c_ready, 1)
            split(G, 0, 0)
            split(U, 0, 0)

            with act.Fori(0, DEPTH) as l:
                def post(sub):
                    r = 3 * l + sub
                    for b in range(4):
                        if sub == 1:
                            mix_used(act, l, N_IN + b)
                        elif b < 3:
                            act.wait_ge(y_done, 3 * (2 * l + sub // 2) + b + 1)
                        else:
                            act.wait_ge(panel_used[DN], CREDIT + USES * l + (NF if sub == 0 else USES))
                        nc.scalar.activation(sq[:, 2 * b:2 * b + 2, :].rearrange("p k s -> p (k s)"), ps[:, b, :],
                                             ACT.Square).then_inc(ysq_ready, 1)
                    act.wait_ge(ysum_ready, CREDIT + r + 1)
                    act.wait_ge(rx_ready, r + 1)
                    nc.scalar.activation(std[:], ps[:, BK_B, 0:S], ACT.Sqrt, bias=eps[:], scale=1.0 / D) \
                        .then_inc(ystd_ready, 1)

                def pre(sub, mixer):
                    r = 3 * l + sub
                    for b in range(4):
                        act.wait_ge(x_tile, 4 * r + b + 1)
                        act.wait_ge(ysum_ready, CREDIT + r)
                        nc.scalar.activation(sq[:, 2 * b:2 * b + 2, :], xT[:, 2 * b:2 * b + 2, :], ACT.Square) \
                            .then_inc(xsq_ready, 1)
                    act.wait_ge(xsum_ready, r + 1)
                    act.wait_ge(post_link, CREDIT + r)
                    nc.scalar.activation(std[:], ps[:, BK_A, 0:S], ACT.Sqrt, bias=eps[:], scale=1.0 / D) \
                        .then_inc(xstd_ready, 1)
                    for k in range(KT):
                        act.wait_ge(t_ready, KT * r + k + 1)
                        shift = mods[:, (3 * sub) * KT + k:(3 * sub) * KT + k + 1]
                        nc.scalar.activation(a_hi[:, k, :], tmp[:, k, :], ACT.Identity, bias=shift).then_inc(h_hi, 1)
                        if mixer:
                            nc.scalar.activation(h32[:, k, :], tmp[:, k, :], ACT.Identity, bias=shift) \
                                .then_inc(h_f32, 1)

                def silu(f, n0, i):
                    act.wait_ge(panel_used[G], CREDIT + USES * l + (n0 + 1) + i)
                    act.wait_ge(glu_ready, CREDIT + f + i)
                    nc.scalar.activation(silu_g, ps[:, BK_GATE, :], ACT.Silu).then_inc(silu_ready, 1)

                def high_u(f, n0, i):
                    act.wait_ge(glu_ready, CREDIT + f + i + 1)
                    act.wait_ge(panel_used[DN], CREDIT + USES * l + n0 + i)
                    nc.scalar.activation(u_hi[:].rearrange("p k s -> p (k s)"), glu, ACT.Copy).then_inc(u_hi_ready, 1)

                def ffn(ffn_, n0):
                    f = l * (2 * NF) + ffn_ * NF
                    silu(f, n0, 0)
                    split(G, l, n0 + 1)
                    with act.Fori(0, NF - 1) as i:
                        split(DN, l, n0 + i)
                        high_u(f, n0, i)
                        split(U, l, n0 + 1 + i)
                        silu(f, n0, i + 1)
                        split(G, l, n0 + 2 + i)
                    split(DN, l, n0 + NF - 1)
                    high_u(f, n0, NF - 1)
                    split(U, l, n0 + NF)

                pre(0, False)
                ffn(0, 0)
                post(0)
                pre(1, True)
                split_aq(l)

                def evac(m, dst, func=ACT.Copy, scale=1.0, bank=None, view=None):
                    mix_used(act, l, m)
                    src = ps[:, BK_GATE + m % 2, :] if view is None else view
                    nc.scalar.activation(dst, src, func, scale=scale).then_inc(proj_read, 1)

                def next_split(m):
                    split(m % 3, l, MIX0 + m // 3)

                act.wait_ge(gates_done, CREDIT + l + 1)
                nc.scalar.activation(th[:], ps[0:2 * MH, BK_B, 0:S], ACT.Tanh, bias=gb15[:, bass.ds(l, 1)],
                                     scale=1.0 / CAP).then_inc(th_ready, 1)
                act.wait_ge(th_ready, l + 1)
                nc.scalar.activation(sp[:], th[:], ACT.Exp, scale=-CAP).then_inc(ez_ready, 1)
                act.wait_ge(ez_ready, l + 1)
                nc.scalar.activation(sp2[:], sp[:], ACT.Ln, bias=1.0).then_inc(sp_ready, 1)
                act.wait_ge(bias_ready, AG * (NCH + 1))
                evac(0, qT[:].rearrange("p k s -> p (k s)"))
                next_split(3)
                evac(1, kT[:].rearrange("p k s -> p (k s)"))
                next_split(4)
                evac(2, aqT[:].rearrange("p k s -> p (k s)"))
                next_split(5)
                evac(3, akT[:], view=ps[:, BK_UP, 0:S])
                nc.scalar.activation(av[:].rearrange("p w d -> p (w d)"), ps[:, BK_A, 0:3 * P], ACT.Copy) \
                    .then_inc(av_ready, 1)
                next_split(6)
                evac(4, vm[:, :, 0:PC], view=ps[:, BK_GATE, :].rearrange("p (t d) -> p t d", t=2))

                def decay(h):
                    act.wait_ge(decay_done, MH * l + h + 1)
                    act.wait_ge(hm_link, CREDIT + 3 * (MH * l + h))
                    nc.scalar.activation(floor[:], ps[:, 2, S:2 * S], ACT.Exp).then_inc(floor_ready, 1)
                    act.wait_ge(cap_ready, CREDIT + 2 * (MH * l + h + 1))
                    nc.scalar.activation(edec[:], ecap[:], ACT.Exp).then_inc(dec_ready, 1)

                def square_head(h):
                    act.wait_ge(hm_ready, CREDIT + MH * l + h + 1)
                    nc.scalar.activation(sq[:, h, :], hm[:, h, :], ACT.Square).then_inc(hmsq_ready, 1)

                decay(0)
                next_split(7)
                act.wait_ge(smax_ready, l + 1)
                for r in range(AG * NCH):
                    nc.scalar.activation(sc[:, r, :], sc[:, r, :], ACT.Exp, bias=mx[:, 2, r:r + 1],
                                         accum_out=sums[:, 0, r:r + 1]).then_inc(probs_exp, 1)
                nc.scalar.activation(sums[:, 1, :], mx[:, 1, :], ACT.Exp).then_inc(sink_exp, 1)
                evac(5, vm[:, :, PC:2 * PC], view=ps[:, BK_UP, :].rearrange("p (t d) -> p t d", t=2))
                decay(1)
                square_head(0)
                next_split(8)
                evac(6, th_o[:, 0:2, :].rearrange("p k s -> p (k s)"), ACT.Tanh, 0.5)
                decay(2)
                square_head(1)
                next_split(9)
                evac(7, th_o[:, 2:4, :].rearrange("p k s -> p (k s)"), ACT.Tanh, 0.5)
                decay(3)
                square_head(2)
                next_split(10)
                evac(8, cc_s.rearrange("p k s -> p (k s)"))
                square_head(3)
                next_split(11)
                next_split(12)
                for b in range(2):
                    act.wait_ge(hmsum_done, 2 * l + b + 1)
                    nc.scalar.activation(tmp[:, 2 * b:2 * b + 2, :].rearrange("p k s -> p (k s)"), ps[:, b, :],
                                         ACT.Sqrt, bias=eps[:], scale=1.0 / DV).then_inc(hmstd_ready, 1)
                for n, k0 in enumerate((6, 0, 2, 4)):
                    act.wait_ge(mix_f32, 4 * l + n + 1)
                    nc.scalar.activation(mix_tile("hi", k0), h32[:, k0:k0 + 2, :], ACT.Copy).then_inc(mix_hi, 1)
                for m in range(13, N_MIX + 2):
                    next_split(m)
                post(1)
                pre(2, False)
                ffn(1, FFB0)
                post(2)

            for t in range(2):
                for b in range(2):
                    act.wait_ge(o_turned, 2 * t + b + 1)
                    nc.scalar.activation(tmp[:, 4 * t + 2 * b:4 * t + 2 * b + 2, :].rearrange("p k s -> p (k s)"),
                                         ps[:, 4 + 2 * t + b, :], ACT.Copy) \
                        .then_inc(o_ready, 1)

        @block.vector
        def _(dve):
            def split(s, l, n):
                dve.wait_ge(hi_ready[s], USES * l + n + 1)
                nc.vector.tensor_tensor(lo[s][:], raw[s][:], hi[s][:].bitcast(F32), ALU.subtract) \
                    .then_inc(lo_ready[s], 1)

            def split_aq(l):
                dve.wait_ge(hi_ready[2], USES * l + MIX0 + 1)
                for g in range(AG):
                    last = nc.vector.tensor_tensor(by_group(lo, g, True), by_group(raw, g, False),
                                                   by_group(hi, g, True).bitcast(F32), ALU.subtract)
                last.then_inc(lo_ready[2], 1)

            def ada_sum(s, use):
                dve.wait_ge(ada_loaded[s], 16 * (use + 1))
                dve.wait_ge(ada_turned[s], CREDIT + use)
                acc = ada_acc[s][:]
                nc.vector.tensor_scalar(acc, ada_raw[s][:, 0, :], c_col[:, 0:1], None, ALU.mult) \
                    .then_inc(ada_link[s], 1)
                for k in range(1, KT):
                    dve.wait_ge(ada_link[s], (KT - 1) * use + k)
                    nc.vector.scalar_tensor_tensor(acc, ada_raw[s][:, k, :], c_col[:, k:k + 1], acc, ALU.mult, ALU.add) \
                        .then_inc(ada_link[s] if k < KT - 1 else ada_summed[s], 1)

            def ada_mods(s, use, q, b):
                dve.wait_ge(ada_turned[s], CREDIT + use + 1)
                nc.vector.tensor_tensor(mods[:, bass.ds(2 * q, 2)], ps[:, BK_B if s else BK_A, 0:2],
                                        adab[:, bass.ds(72 * b + 2 * q, 2)], ALU.add).then_inc(mods_ready[s], 1)

            for signal in (*lo_ready, *ada_summed, *mods_ready, glu_ready, u_lo_ready, post_link, hm_link, cap_ready,
                           pm_ready, hm_ready):
                dve.sem_inc(signal, CREDIT)
            for g in range(3):
                dve.wait_ge(cols_turned, g + 1)
                n = 28 if g == 2 else 120
                nc.vector.tensor_copy(cols[:, g * P:g * P + n], ps[:, g, 0:n]).then_inc(cols_ready, 1)
            dve.wait_ge(cols_ready, 3)
            for b in range(DEPTH + 1):
                src = cols[:, (b % DEPTH) * P:(b % DEPTH) * P + 72]
                nc.vector.tensor_copy(adab[:, 72 * b:72 * b + 72], src).then_inc(prep, 1)
            dve.wait_ge(small_in, 64)
            nc.vector.tensor_scalar(gb15[:], gb[:], 1.0 / CAP, None, ALU.mult).then_inc(prep, 1)
            dve.wait_ge(prep, DEPTH + 2)
            dve.wait_ge(silu_c_ready, 1)
            for q in range(EARLY):
                ada_sum(q % 2, q // 2)
                if q >= 1:
                    ada_mods((q - 1) % 2, (q - 1) // 2, q - 1, 0)
                if q == 4:
                    for b in range(4):
                        dve.wait_ge(x_turned, b + 1)
                        nc.vector.tensor_copy(xT[:, 2 * b:2 * b + 2, :].rearrange("p k s -> p (k s)"), ps[:, b, :]) \
                            .then_inc(x_tile, 1)
            ada_mods((EARLY - 1) % 2, (EARLY - 1) // 2, EARLY - 1, 0)
            split(G, 0, 0)
            split(U, 0, 0)
            dve.wait_ge(t_rows, 1)
            nc.vector.tensor_copy(trow, ps[:, 4, 0:AG * 3 * CHUNK].rearrange("p (g r) -> p g r", g=AG)) \
                .then_inc(t_rows_out, 1)

            with dve.Fori(0, DEPTH) as l:
                def post(sub, w):
                    r = 3 * l + sub
                    gate = mods[:, (3 * sub + 2) * KT:(3 * sub + 3) * KT]
                    gp = cols[:, bass.ds(P + 72 + (3 * l + sub) * KT, KT)]
                    dve.wait_ge(mods_ready[0], CREDIT + A_USES * l + A0 + (NF if sub == 0 else A_USES))
                    dve.wait_ge(mods_ready[1], CREDIT + B_USES * l + B0 + (NF if sub == 0 else NF + 1))
                    nc.vector.scalar_tensor_tensor(mod_c[:], gate, 1.0, gp, ALU.add, ALU.mult).then_inc(pre_link, 1)
                    dve.wait_ge(pre_link, 3 * r + 2)
                    nc.vector.tensor_scalar(mod_c[:], mod_c[:], w, None, ALU.mult).then_inc(pre_link, 1)
                    dve.wait_ge(ystd_ready, r + 1)
                    nc.vector.reciprocal(rstd[:], std[:]).then_inc(post_link, 1)
                    dve.wait_ge(post_link, CREDIT + r + 1)
                    dve.wait_ge(pre_link, 3 * r + 3)
                    for b in range(4):
                        for k in (2 * b, 2 * b + 1):
                            last = nc.vector.scalar_tensor_tensor(tmp[:, k, :], ps[:, b, (k % 2) * S:(k % 2 + 1) * S],
                                                                  mod_c[:, k:k + 1], rstd[:], ALU.mult, ALU.mult)
                            last.then_inc(y_scaled, 1)
                        dve.wait_ge(y_scaled, 8 * r + 2 * b + 2)
                        nc.vector.tensor_tensor(xT[:, 2 * b:2 * b + 2, :], xT[:, 2 * b:2 * b + 2, :],
                                                tmp[:, 2 * b:2 * b + 2, :], ALU.add).then_inc(x_tile, 1)

                def pre(sub):
                    r = 3 * l + sub
                    gp = cols[:, bass.ds(72 + (3 * l + sub) * KT, KT)]
                    scale = mods[:, (3 * sub + 1) * KT:(3 * sub + 2) * KT]
                    dve.wait_ge(mods_ready[0], CREDIT + A_USES * l + A0 + (0 if sub == 0 else NF))
                    dve.wait_ge(mods_ready[1], CREDIT + B_USES * l + B0 + (0 if sub == 0 else NF))
                    nc.vector.scalar_tensor_tensor(mod_a[:], scale, 1.0, gp, ALU.add, ALU.mult).then_inc(pre_link, 1)
                    dve.wait_ge(xstd_ready, r + 1)
                    nc.vector.reciprocal(rstd[:], std[:]).then_inc(rx_ready, 1)
                    dve.wait_ge(rx_ready, r + 1)
                    dve.wait_ge(pre_link, 3 * r + 1)
                    def low(k):
                        shift = mods[:, (3 * sub) * KT + k:(3 * sub) * KT + k + 1]
                        dve.wait_ge(h_hi, KT * r + k + 1)
                        nc.vector.scalar_tensor_tensor(a_lo[:, k, :], tmp[:, k, :], shift,
                                                       a_hi[:, k, :].bitcast(F32), ALU.add, ALU.subtract) \
                            .then_inc(h_lo, 1)
                    for k in range(KT):
                        nc.vector.scalar_tensor_tensor(tmp[:, k, :], xT[:, k, :], mod_a[:, k:k + 1], rstd[:],
                                                       ALU.mult, ALU.mult).then_inc(t_ready, 1)
                        if k >= 2:
                            low(k - 2)
                    low(KT - 2)
                    low(KT - 1)

                def mult_up(f, n0, i):
                    dve.wait_ge(panel_used[U], CREDIT + USES * l + (n0 + 1) + i)
                    dve.wait_ge(silu_ready, CREDIT + f + i + 1)
                    dve.wait_ge(u_lo_ready, CREDIT + f + i)
                    nc.vector.tensor_tensor(glu, ps[:, BK_UP, :], silu_g, ALU.mult).then_inc(glu_ready, 1)

                def low_u(f, i):
                    dve.wait_ge(u_hi_ready, f + i + 1)
                    nc.vector.tensor_tensor(u_lo[:].rearrange("p k s -> p (k s)"), glu,
                                            u_hi[:].bitcast(F32).rearrange("p k s -> p (k s)"), ALU.subtract) \
                        .then_inc(u_lo_ready, 1)

                def ffn(ffn_, n0, first):
                    f = l * (2 * NF) + ffn_ * NF
                    split(G, l, n0 + 1)
                    with dve.Fori(0, NF - 1) as i:
                        if first:
                            ada_sum(0, A_USES * l + (A0 + i))
                        split(DN, l, n0 + i)
                        mult_up(f, n0, i)
                        split(U, l, n0 + 1 + i)
                        low_u(f, i)
                        if first:
                            ada_mods(0, A_USES * l + (A0 + i), 2 * i + EARLY, l)
                            ada_sum(1, B_USES * l + (B0 + i))
                        else:
                            ada_sum(1, B_USES * l + (B0 + NF + 1 + i))
                        split(G, l, n0 + 2 + i)
                        if first:
                            ada_mods(1, B_USES * l + (B0 + i), 2 * i + (EARLY + 1), l)
                        else:
                            ada_mods(1, B_USES * l + (B0 + NF + 1 + i), i, l + 1)
                    if first:
                        ada_sum(0, A_USES * l + (A0 + NF - 1))
                    split(DN, l, n0 + NF - 1)
                    mult_up(f, n0, NF - 1)
                    low_u(f, NF - 1)
                    split(U, l, n0 + NF)
                    if first:
                        ada_mods(0, A_USES * l + (A0 + NF - 1), NA - 5, l)
                        ada_sum(1, B_USES * l + (B0 + NF - 1))
                        ada_mods(1, B_USES * l + (B0 + NF - 1), NA - 4, l)
                    else:
                        ada_sum(1, B_USES * l + (B0 + NF + NF))
                        ada_mods(1, B_USES * l + (B0 + NF + NF), NF - 1, l + 1)

                pre(0)
                ffn(0, 0, True)
                post(0, 0.5)
                pre(1)
                split_aq(l)

                def next_split(m):
                    split(m % 3, l, MIX0 + m // 3)

                dve.wait_ge(sp_ready, l + 1)
                nc.vector.tensor_tensor_scan(gsum[:], ones[0:2 * MH, :], sp2[:], 0.0, ALU.mult, ALU.subtract) \
                    .then_inc(g_ready, 1)
                next_split(3)
                next_split(4)
                for g in range(AG):
                    nc.vector.tensor_copy(sink8[:, g, :], sink[:, bass.ds(l, 1), g:g + 1]
                                          .rearrange("p a b -> p (a b)").to_broadcast([P, NCH])).then_inc(s_link, 1)
                dve.wait_ge(a_done, l + 1)
                nc.vector.tensor_copy(arow[:], ps[0:MH, BK_B, 0:S]).then_inc(arow_ready, 1)
                nc.vector.tensor_copy(acol[:].rearrange("p t h -> p (t h)"), ps[:, BK_B, S:S + 2 * MH]) \
                    .then_inc(arow_ready, 1)
                dve.wait_ge(arow_ready, 2 * l + 2)
                nc.vector.tensor_tensor_scan(mrow[:], arow[:], arow[:], MASKED, ALU.max, ALU.max).then_inc(m_ready, 1)
                next_split(5)
                next_split(6)

                dve.wait_ge(bias_ready, AG * (NCH + 1))
                dve.wait_ge(scores_done, l + 1)
                for g in range(AG):
                    nc.vector.scalar_tensor_tensor(
                        sc[:, g * NCH:(g + 1) * NCH, :].rearrange("p j k -> p (j k)"), ps[:, g, :], DH ** -0.5,
                        bias[:, g, :, :].rearrange("p j k -> p (j k)"), ALU.mult, ALU.add).then_inc(s_link, 1)
                base = 6 * l + 4
                dve.wait_ge(s_link, base)
                nc.vector.tensor_reduce(mx[:, 0, :], sc, AX_X, ALU.max).then_inc(s_link, 1)
                dve.wait_ge(s_link, base + 1)
                sk = sink8[:].rearrange("p g j -> p (g j)")
                nc.vector.tensor_tensor(mx[:, 0, :], mx[:, 0, :], sk, ALU.max).then_inc(s_link, 1)
                dve.wait_ge(s_link, base + 2)
                nc.vector.tensor_tensor(mx[:, 1, :], sk, mx[:, 0, :], ALU.subtract).then_inc(sm_link, 1)
                nc.vector.tensor_scalar(mx[:, 2, :], mx[:, 0, :], -1.0, None, ALU.mult).then_inc(smax_ready, 1)

                def decay(h):
                    dve.wait_ge(floor_ready, CREDIT + MH * l + h + 1)
                    dve.wait_ge(dec_ready, CREDIT + MH * l + h)
                    cap = cst[:, C_CAP:C_CAP + S]
                    nc.vector.scalar_tensor_tensor(ecap[:, 0:S], ps[:, 2, 0:S], acol[:, 0, h:h + 1], cap,
                                                   ALU.add, ALU.min).then_inc(cap_ready, 1)
                    nc.vector.scalar_tensor_tensor(ecap[:, S:S + P], ps[:, 2, P:S], acol[:, 1, h:h + 1], cap[:, 0:P],
                                                   ALU.add, ALU.min).then_inc(cap_ready, 1)

                def weigh(h):
                    dve.wait_ge(dec_ready, CREDIT + MH * l + h + 1)
                    dve.wait_ge(qk_done, MH * l + h + 1)
                    dve.wait_ge(num_done, CREDIT + MH * l + h)
                    nc.vector.scalar_tensor_tensor(pm[:], ps[:, 3, 0:3 * P], DQK ** -0.5, edec[:], ALU.mult, ALU.mult) \
                        .then_inc(pm_ready, 1)

                def head_out(h):
                    dve.wait_ge(num_done, CREDIT + MH * l + h + 1)
                    dve.wait_ge(floor_ready, CREDIT + MH * l + h + 1)
                    n = 3 * (MH * l + h)
                    den = ps[:, BK_B, S:2 * S]
                    nc.vector.scalar_tensor_tensor(dd[:], den, -1.0, floor[:], ALU.mult, ALU.max).then_inc(hm_link, 1)
                    dve.wait_ge(hm_link, CREDIT + n + 1)
                    nc.vector.tensor_tensor(dd[:], dd[:], den, ALU.max).then_inc(hm_link, 1)
                    dve.wait_ge(hm_link, CREDIT + n + 2)
                    nc.vector.reciprocal(rd[:], dd[:]).then_inc(hm_link, 1)
                    dve.wait_ge(hm_link, CREDIT + n + 3)
                    nc.vector.tensor_tensor(hm[:, h, :], ps[:, BK_B, 0:S], rd[:], ALU.mult).then_inc(hm_ready, 1)

                decay(0)
                weigh(0)
                next_split(7)
                ada_sum(0, A_USES * l + (A0 + NF))
                dve.wait_ge(probs_exp, AG * NCH * (l + 1))
                dve.wait_ge(sink_exp, l + 1)
                nc.vector.tensor_tensor(sums[:, 2, :], sums[:, 0, :], sums[:, 1, :], ALU.add).then_inc(pr_link, 1)
                dve.wait_ge(pr_link, 2 * l + 1)
                nc.vector.reciprocal(sums[:, 3, :], sums[:, 2, :]).then_inc(pr_link, 1)
                dve.wait_ge(pr_link, 2 * l + 2)
                nc.vector.tensor_tensor(sc, sc, sums[:, 3, :].rearrange("p (r o) -> p r o", o=1)
                                        .to_broadcast([P, AG * NCH, P]), ALU.mult).then_inc(probs_ready, 1)
                head_out(0)
                decay(1)
                weigh(1)
                next_split(8)
                head_out(1)
                decay(2)
                weigh(2)
                for b in range(2):
                    dve.wait_ge(probs_turned, 2 * l + b + 1)
                    nc.vector.tensor_copy(pT[:, 4 * b:4 * b + 4, :].rearrange("p r q -> p (r q)"), ps[:, b, :]) \
                        .then_inc(pT_ready, 1)
                ada_mods(0, A_USES * l + (A0 + NF), NA - 3, l)
                next_split(9)
                head_out(2)
                decay(3)
                weigh(3)
                dve.wait_ge(attn_done, l + 1)
                nc.vector.tensor_copy(h32[:, 6:8, :].rearrange("p k s -> p (k s)"), ps[:, BK_A, :]) \
                    .then_inc(mix_f32, 1)
                ada_sum(1, B_USES * l + (B0 + NF))
                next_split(10)
                head_out(3)
                next_split(11)
                dve.wait_ge(proj_read, N_READ * l + 9)
                mix_used(dve, l, 9)
                nc.vector.tensor_tensor(up_s[:, :, 2:], ps[:, BK_UP, :].rearrange("p (k s) -> p k s", k=2), cc_s,
                                        ALU.mult).then_inc(proj_read, 1)
                dve.wait_ge(proj_read, N_READ * l + 10)
                for k in range(2):
                    def tap(t):
                        return cols[:, bass.ds(CONV + 6 * l + 2 * t + k, 1)]
                    nc.vector.tensor_scalar(yc[:, k, :], up_s[:, k, 0:S], tap(0), None, ALU.mult).then_inc(conv_link, 1)
                for t in (1, 2):
                    for k in range(2):
                        dve.wait_ge(conv_link, 6 * l + 2 * (t - 1) + k + 1)
                        nc.vector.scalar_tensor_tensor(yc[:, k, :], up_s[:, k, t:t + S],
                                                       cols[:, bass.ds(CONV + 6 * l + 2 * t + k, 1)], yc[:, k, :],
                                                       ALU.mult, ALU.add).then_inc(conv_link, 1)
                ada_sum(0, A_USES * l + (A0 + NF + 1))
                next_split(12)
                ada_mods(1, B_USES * l + (B0 + NF), NA - 2, l)
                for b in range(2):
                    sl = slice(2 * b, 2 * b + 2)
                    dve.wait_ge(hmstd_ready, 2 * l + b + 1)
                    n = 8 * l + 4 * b
                    nc.vector.reciprocal(tmp[:, sl, :], tmp[:, sl, :]).then_inc(out_link, 1)
                    dve.wait_ge(out_link, n + 1)
                    nc.vector.tensor_tensor(hm[:, sl, :], hm[:, sl, :], tmp[:, sl, :], ALU.mult).then_inc(out_link, 1)
                    nc.vector.tensor_scalar(th_o[:, sl, :], th_o[:, sl, :], 0.5, 0.5, ALU.mult, ALU.add) \
                        .then_inc(out_link, 1)
                    dve.wait_ge(out_link, n + 3)
                    nc.vector.tensor_tensor(hm[:, sl, :], hm[:, sl, :], th_o[:, sl, :], ALU.mult).then_inc(out_link, 1)
                    dve.wait_ge(out_link, n + 4)
                    for h in (2 * b, 2 * b + 1):
                        last = nc.vector.tensor_scalar(h32[:, h, :], hm[:, h, :], cols[:, bass.ds(HEAD + MH * l + h, 1)],
                                                       None, ALU.mult)
                    last.then_inc(mix_f32, 1)

                def low_mix(n, k0):
                    dve.wait_ge(mix_hi, 4 * l + n + 1)
                    nc.vector.tensor_tensor(mix_tile("lo", k0), h32[:, k0:k0 + 2, :],
                                            mix_tile("hi", k0).bitcast(F32), ALU.subtract).then_inc(mix_lo, 1)

                low_mix(0, 6)
                low_mix(1, 0)
                low_mix(2, 2)
                mix_used(dve, l, 10)
                dve.wait_ge(conv_link, 6 * l + 6)
                nc.vector.tensor_tensor(h32[:, 4:6, :].rearrange("p k s -> p (k s)"), ps[:, BK_GATE, :],
                                        yc.rearrange("p k s -> p (k s)"), ALU.mult).then_inc(mix_f32, 1)
                low_mix(3, 4)
                ada_mods(0, A_USES * l + (A0 + NF + 1), NA - 1, l)
                for m in range(13, N_MIX + 2):
                    next_split(m)
                post(1, 1.0)
                pre(2)
                ffn(1, FFB0, False)
                post(2, 0.5)

        @block.tensor
        def _(pe):
            def take(s, l, n):
                pe.wait_ge(lo_ready[s], CREDIT + USES * l + n + 1)

            def product(dst, w_hi, w_lo, b_hi, b_lo, first, last):
                nc.tensor.matmul(dst, w_hi, b_hi, start=first, stop=False, skip_group_check=True)
                nc.tensor.matmul(dst, w_hi, b_lo, start=False, stop=False, skip_group_check=True)
                return nc.tensor.matmul(dst, w_lo, b_hi, start=False, stop=last, skip_group_check=True)

            def ada_turn(s, use):
                pe.wait_ge(ada_summed[s], CREDIT + use + 1)
                pe.wait_ge(mods_ready[s], CREDIT + use)
                for j in range(2):
                    last = nc.tensor.matmul(ps[:, BK_B if s else BK_A, j:j + 1], ada_acc[s][:, j * P:(j + 1) * P],
                                            ones[:, 0:1], start=True, stop=True)
                last.then_inc(ada_turned[s], 1)

            for signal in (*panel_used, *ada_turned, gates_done, ysum_ready, num_done):
                pe.sem_inc(signal, CREDIT)
            pe.wait_ge(consts_in, 16)
            pe.wait_ge(c_in, 7 * 16)
            for g in range(3):
                n = 28 if g == 2 else 120
                nc.tensor.transpose(ps[:, g, 0:n], rows[0:n, g, :], ident[0:n, 0:n]).then_inc(cols_turned, 1)
            pe.wait_ge(ones_set, 4)
            pe.wait_ge(tabx_ready, 4)
            for g in range(AG):
                last = nc.tensor.matmul(ps[:, 4, g * 192:(g + 1) * 192],
                                        tabx[:, g, :, :].rearrange("b k q -> b (k q)"),
                                        cst[0:N_BUCKETS, C_HOT:C_HOT + 192], start=True, stop=True)
            last.then_inc(t_rows, 1)
            for q in range(EARLY):
                ada_turn(q % 2, q // 2)
                if q == 1:
                    pe.wait_ge(x_in, 16)
                    pe.wait_ge(cols_ready, 3)
                    xt = tmp[:].rearrange("p k s -> p (k s)").rearrange("p (t d) -> p t d", t=2)
                    for k in range(KT):
                        for t in range(2):
                            last = nc.tensor.transpose(ps[:, k // 2, (k % 2) * S + t * P:(k % 2) * S + (t + 1) * P],
                                                       xt[:, t, k * P:(k + 1) * P], ident)
                        if k % 2:
                            last.then_inc(x_turned, 1)
            pe.wait_ge(t_rows_out, 1)

            with pe.Fori(0, DEPTH) as l:
                def sum_squares(bank, ready, n0, done):
                    for k in range(KT):
                        if k % 2 == 0:
                            pe.wait_ge(ready, n0 + k // 2 + 1)
                        last = nc.tensor.matmul(ps[:, bank, 0:S], ones[:, 0:P], sq[:, k, :], start=(k == 0),
                                                stop=(k == KT - 1))
                    last.then_inc(done, 1)

                def pre(sub):
                    r = 3 * l + sub
                    pe.wait_ge(mods_ready[0], CREDIT + A_USES * l + A0 + (0 if sub == 0 else NF if sub == 1 else A_USES))
                    sum_squares(BK_A, xsq_ready, 4 * r, xsum_ready)

                def post(sub):
                    r = 3 * l + sub
                    pe.wait_ge(mods_ready[1], CREDIT + B_USES * l + B0 + (NF, NF + 1, B_USES)[sub])
                    sum_squares(BK_B, ysq_ready, 4 * r, ysum_ready)

                def wide_tile(bank, s, j, r=None):
                    for k in range(KT):
                        if r is not None and j == 0:
                            pe.wait_ge(h_lo, KT * r + k + 1)
                        last = product(ps[:, bank, j * S:(j + 1) * S], panel(hi, s)[:, k, j * P:(j + 1) * P],
                                       panel(lo, s)[:, k, j * P:(j + 1) * P], a_hi[:, k, :], a_lo[:, k, :],
                                       k == 0, k == KT - 1)
                    return last

                def gate(f, n0, i, r=None):
                    take(G, l, n0 + i)
                    pe.wait_ge(silu_ready, CREDIT + f + i)
                    for j in range(2):
                        last = wide_tile(BK_GATE, G, j, r)
                    last.then_inc(panel_used[G], 1)

                def up(f, n0, i):
                    take(U, l, n0 + i)
                    pe.wait_ge(glu_ready, CREDIT + f + i)
                    for j in range(2):
                        last = wide_tile(BK_UP, U, j)
                    last.then_inc(panel_used[U], 1)

                def down(f, n0, i, final, middle):
                    take(DN, l, n0 + i)
                    pe.wait_ge(u_lo_ready, CREDIT + f + i + 1)
                    for m in range(KT):
                        if m == 6:
                            middle()
                        for a in range(2):
                            last = product(ps[:, m // 2, (m % 2) * S:(m % 2 + 1) * S],
                                           rowpanel(hi, DN)[:, a, m * P:(m + 1) * P],
                                           rowpanel(lo, DN)[:, a, m * P:(m + 1) * P],
                                           u_hi[:, a, :], u_lo[:, a, :], False, final and a == 1)
                        if final and m in (1, 3, 5):
                            last.then_inc(y_done, 1)
                    last.then_inc(panel_used[DN], 1)

                def ffn(ffn_, n0, first, sub):
                    f = l * (2 * NF) + ffn_ * NF
                    b0 = B0 if first else B0 + NF + 1

                    gate(f, n0, 0, 3 * l + sub)
                    for b in range(4):
                        nc.tensor.matmul(ps[:, b, 0:1], zeros[:], ones[:, 0:1], start=True, stop=False,
                                         skip_group_check=True)
                    with pe.Fori(0, NF - 1) as i:
                        up(f, n0, i)
                        if first:
                            ada_turn(0, A_USES * l + (A0 + i))
                        gate(f, n0, i + 1)
                        down(f, n0, i, False, lambda: ada_turn(1, B_USES * l + (b0 + i)))
                    up(f, n0, NF - 1)
                    if first:
                        ada_turn(0, A_USES * l + (A0 + NF - 1))
                    down(f, n0, NF - 1, True, lambda: None)
                    ada_turn(1, B_USES * l + (b0 + NF - 1))

                def mix_take(m):
                    take(m % 3, l, MIX0 + m // 3)
                    if m >= 2:
                        pe.wait_ge(proj_read, N_READ * l + (m - 1))

                def mix_release(m, last):
                    last.then_inc(panel_used[m % 3], 1)

                def project(m, r=None):
                    mix_take(m)
                    for j in range(2):
                        last = wide_tile(BK_GATE + m % 2, m % 3, j, r)
                    mix_release(m, last)

                def project_tokens(m):
                    mix_take(m)
                    for t in range(2):
                        for k in range(KT):
                            tok = slice(t * P, (t + 1) * P)
                            last = product(ps[:, BK_GATE + m % 2, t * PC:(t + 1) * PC], a_hi[:, k, tok], a_lo[:, k, tok],
                                           panel(hi, m % 3)[:, k, :], panel(lo, m % 3)[:, k, :], k == 0, k == KT - 1)
                    mix_release(m, last)

                def gates():
                    pe.wait_ge(wg_in, 16 * (l + 1))
                    for k in range(KT):
                        pe.wait_ge(h_f32, KT * l + k + 1)
                        last = nc.tensor.matmul(ps[0:2 * MH, BK_B, 0:S], wg[:, k, :], h32[:, k, :], start=(k == 0),
                                                stop=(k == KT - 1))
                    last.then_inc(gates_done, 1)

                def project_aq():
                    mix_take(2)
                    for g in range(AG):
                        for k in range(KT):
                            w = [panel(t, 2)[:, k, g * P:(g + 1) * P] for t in (hi, lo)]
                            last = product(ps[:, BK_GATE, g * S:(g + 1) * S], w[0], w[1], a_hi[:, k, :], a_lo[:, k, :],
                                           k == 0, k == KT - 1)
                    mix_release(2, last)

                def project_akv():
                    mix_take(3)
                    wide_tile(BK_UP, 0, 0)
                    for w in range(3):
                        tok = slice(w * CHUNK, w * CHUNK + P)
                        for k in range(KT):
                            last = product(ps[:, BK_A, w * P:(w + 1) * P], a_hi[:, k, tok], a_lo[:, k, tok],
                                           panel(hi, 0)[:, k, P:2 * P], panel(lo, 0)[:, k, P:2 * P], k == 0,
                                           k == KT - 1)
                    mix_release(3, last)

                def log_weights():
                    pe.wait_ge(g_ready, l + 1)
                    sel_i, sel_f = cst[0:2 * MH, C_SELI:C_SELI + MH], cst[0:2 * MH, C_SELF:C_SELF + MH]
                    for t in range(2):
                        o = ps[:, BK_B, S + t * MH:S + (t + 1) * MH]
                        nc.tensor.matmul(o, th[:, t * P:(t + 1) * P], sel_i, start=True, stop=False)
                        nc.tensor.matmul(o, gsum[:, t * P:(t + 1) * P], sel_f, start=False, stop=True)
                    nc.tensor.matmul(ps[0:MH, BK_B, 0:S], sel_i, th[:], start=True, stop=False)
                    nc.tensor.matmul(ps[0:MH, BK_B, 0:S], sel_f, gsum[:], start=False, stop=True).then_inc(a_done, 1)

                def scores():
                    for g in range(AG):
                        for j in range(NCH):
                            k0 = max(j - 1, 0) * CHUNK
                            for kv in range(AKV):
                                pr = slice(kv * DH, (kv + 1) * DH)
                                last = nc.tensor.matmul(ps[pr, g, j * P:(j + 1) * P],
                                                        aqT[pr, g, j * CHUNK:(j + 1) * CHUNK], akT[pr, k0:k0 + P],
                                                        start=True, stop=True)
                    last.then_inc(scores_done, 1)

                def decay_and_qk(h):
                    pe.wait_ge(m_ready, l + 1)
                    pe.wait_ge(floor_ready, CREDIT + MH * l + h)
                    pe.wait_ge(cap_ready, CREDIT + 2 * (MH * l + h))
                    neg_m = cst[0:MH, C_NM + h * P:C_NM + (h + 1) * P]
                    neg_g = cst[0:2 * MH, C_NG + h * P:C_NG + (h + 1) * P]
                    nc.tensor.matmul(ps[:, 2, 0:S], neg_m, mrow[:], start=True, stop=True)
                    nc.tensor.matmul(ps[:, 2, S:2 * S], neg_g, gsum[:], start=True, stop=False)
                    nc.tensor.matmul(ps[:, 2, S:2 * S], neg_m, mrow[:], start=False, stop=True).then_inc(decay_done, 1)
                    pe.wait_ge(pm_ready, CREDIT + MH * l + h)
                    pr = slice((h % 2) * DQK, (h % 2 + 1) * DQK)
                    nc.tensor.matmul(ps[:, 3, 0:S], kT[pr, h // 2, 0:P], qT[pr, h // 2, :], start=True, stop=True)
                    nc.tensor.matmul(ps[:, 3, S:S + P], kT[pr, h // 2, P:S], qT[pr, h // 2, P:S], start=True,
                                     stop=True).then_inc(qk_done, 1)

                def numerator(h):
                    pe.wait_ge(pm_ready, CREDIT + MH * l + h + 1)
                    pe.wait_ge(hm_ready, CREDIT + MH * l + h)
                    pe.wait_ge(arow_ready, 2 * l + 2)
                    for o, w0, w1 in ((0, vm[:, 0, h * DV:(h + 1) * DV], vm[:, 1, h * DV:(h + 1) * DV]),
                                      (S, ones[:, 0:P], ones[:, 0:P])):
                        nc.tensor.matmul(ps[:, BK_B, o:o + S], w0, pm[:, 0:S], start=True, stop=False)
                        last = nc.tensor.matmul(ps[:, BK_B, o + P:o + S], w1, pm[:, S:S + P], start=False, stop=True)
                    last.then_inc(num_done, 1)

                def turn_probs():
                    pe.wait_ge(probs_ready, l + 1)
                    for r in range(AG * NCH):
                        last = nc.tensor.transpose(ps[:, r // 4, (r % 4) * P:(r % 4 + 1) * P], sc[:, r, :], ident)
                        if r % 4 == 3:
                            last.then_inc(probs_turned, 1)

                def attend():
                    pe.wait_ge(pT_ready, 2 * l + 2)
                    pe.wait_ge(mods_ready[0], CREDIT + A_USES * l + (A0 + NF + 1))
                    for g in range(AG):
                        for j in range(NCH):
                            for kv in range(AKV):
                                last = nc.tensor.matmul(
                                    ps[g * DH:(g + 1) * DH, BK_A, kv * S + j * CHUNK:kv * S + (j + 1) * CHUNK],
                                    av[:, max(j - 1, 0), kv * DH:(kv + 1) * DH],
                                    pT[:, g * NCH + j, kv * CHUNK:(kv + 1) * CHUNK], start=True, stop=True)
                    last.then_inc(attn_done, 1)

                def mix_out(b):
                    m = N_IN + b
                    take(m % 3, l, MIX0 + m // 3)
                    for j in range(2):
                        for n, k in enumerate((6, 7, 0, 1, 2, 3, 4, 5)):
                            if b == 0 and j == 0 and n % 2 == 0:
                                pe.wait_ge(mix_lo, 4 * l + n // 2 + 1)
                            last = product(ps[:, b, j * S:(j + 1) * S], panel(hi, m % 3)[:, k, j * P:(j + 1) * P],
                                           panel(lo, m % 3)[:, k, j * P:(j + 1) * P],
                                           mix_tile("hi", k - k % 2)[:, k % 2, :], mix_tile("lo", k - k % 2)[:, k % 2, :],
                                           n == 0, n == KT - 1)
                    mix_release(m, last)

                pre(0)
                ffn(0, 0, True, 0)
                post(0)
                pre(1)
                project(0, 3 * l + 1)
                gates()
                project(1)
                project_aq()
                log_weights()
                project_akv()
                project_tokens(4)
                pe.wait_ge(proj_read, N_READ * l + 4)
                decay_and_qk(0)
                scores()
                project_tokens(5)
                pe.wait_ge(proj_read, N_READ * l + 5)
                numerator(0)
                decay_and_qk(1)
                project(6)
                numerator(1)
                decay_and_qk(2)
                turn_probs()
                project(7)
                numerator(2)
                decay_and_qk(3)
                ada_turn(0, A_USES * l + (A0 + NF))
                attend()
                project(8)
                numerator(3)
                project(9)
                for b in range(2):
                    pe.wait_ge(hmsq_ready, MH * l + 2 * b + 2)
                    nc.tensor.matmul(ps[:, b, :], ones[:, 0:P], sq[:, 2 * b:2 * b + 2, :].rearrange("p k s -> p (k s)"),
                                     start=True, stop=True).then_inc(hmsum_done, 1)
                ada_turn(1, B_USES * l + (B0 + NF))
                project(10)
                pe.wait_ge(mix_f32, 4 * l + 1)
                ada_turn(0, A_USES * l + (A0 + NF + 1))
                pe.wait_ge(hmstd_ready, 2 * l + 2)
                for b in range(N_OUT):
                    mix_out(b)
                post(1)
                pre(2)
                ffn(1, FFB0, False, 2)
                post(2)

            pe.wait_ge(mods_ready[1], CREDIT + B_USES * DEPTH + B0)
            pe.wait_ge(ystd_ready, 3 * DEPTH)
            for b in range(4):
                pe.wait_ge(x_tile, 4 * (3 * DEPTH + 1))
                t = b // 2
                for k in range(4 * (b % 2), 4 * (b % 2) + 4):
                    last = nc.tensor.transpose(ps[:, 4 + b, (k % 4) * P:(k % 4 + 1) * P], xT[:, k, t * P:(t + 1) * P],
                                               ident)
                last.then_inc(o_turned, 1)


_INS = ["x", "c", "ada_w", "ada_b", "norm_pre", "norm_post", "ffn_w_gate", "ffn_w_up", "ffn_w_down", "w_in",
        "mlstm_igate_bias", "mlstm_fgate_bias", "mlstm_head_norm", "conv_w", "attn_sinks", "rel_bias_table", "w_out"]


def kernel(**inputs):
    import concourse.bacc as bacc
    from concourse.bass_utils import run_bass_kernel_spmd

    nc = bacc.Bacc("TRN2", target_bir_lowering=False, num_devices=1)
    arrays, args = {}, []
    for name in _INS + ["constants"]:
        a = constant_table() if name == "constants" else np.ascontiguousarray(inputs[name])
        arrays[f"in_{name}"] = a
        args.append(nc.dram_tensor(f"in_{name}", a.shape, mybir.dt.from_np(a.dtype), kind="ExternalInput").ap())
    args.append(nc.dram_tensor("out_x", (1, S, D), F32, kind="ExternalOutput").ap())
    build(nc, *args)
    r = run_bass_kernel_spmd(nc, [arrays], core_ids=[0])
    return r.results[0]["out_x"]
```

```python
from contextlib import ExitStack

import numpy as np

import concourse.bass as bass
from concourse import mybir

F32 = mybir.dt.float32
F32R = mybir.dt.float32r
ALU = mybir.AluOpType
ACT = mybir.ActivationFunctionType
AX_X = mybir.AxisListType.X

P = 128
D = 1024
S = 256
DEPTH = 2
KT = D // P
D_FF = 2816
PC = 256
NF = D_FF // PC
N_SUB = 3
EPS = 1e-6
CAP = 15.0
MH, DQK, DV = 4, 64, 128
AH, AKV, AG, DH = 4, 2, 2, 64
CHUNK = 64
NCH = S // CHUNK
N_BUCKETS, MAX_DISTANCE = 32, 128
P_IN = 2824
COL_GATES = 1024
MASKED = -1e30
CREDIT = 1

IN_COLS = dict(mq=0, mk=256, aq=2312, akv=2568, mv0=512, mv1=768, mo0=1032, mo1=1288, cc=1800, cx=2056, cb=1544)
IN_ORDER = ["mq", "mk", "aq", "akv", "mv0", "mv1", "cc", "cx", "cb", "mo0", "mo1"]
N_IN = len(IN_ORDER)
N_OUT = D // PC
N_READ = N_IN - 1
N_MIX = N_IN + N_OUT
MIX_USES = N_MIX // 3
USES = 2 * NF + MIX_USES
MIX0 = NF
FFB0 = NF + MIX_USES
G, U, DN = 0, 1, 2

UK, UC = KT // 2, 512
UT = UC // P
N_BLK = 3 * N_SUB * D // UC
PRO_BLK, THIRD = 2 * D // UC, N_BLK // 3
MCOLS = 3 * N_SUB * KT
WRAP = MCOLS

BK_GATE, BK_UP, BK_B, BK_A = 4, 5, 6, 7
WARM = 7
TURN_AT = 400

C_ID, C_CAP, C_HOT, C_SELI, C_SELF, C_NM, C_NG = 0, 128, 384, 576, 580, 584, 1096
C_ALL = 1608


def constant_table():
    c = np.zeros((P, C_ALL), np.float32)
    c[:, C_ID:C_ID + P] = np.eye(P)
    c[:, C_CAP:C_CAP + P] = np.where(np.arange(P)[:, None] <= np.arange(P)[None, :], 0.0, MASKED)
    rel = np.arange(3 * CHUNK - 1) - (2 * CHUNK - 1)
    nb = N_BUCKETS // 2
    exact = nb // 2
    n = np.abs(rel)
    large = exact + (np.log(np.maximum(n, 1) / exact) / np.log(MAX_DISTANCE / exact) * (nb - exact)).astype(np.int32)
    bucket = (rel > 0).astype(np.int32) * nb + np.where(n < exact, n, np.minimum(large, nb - 1))
    c[bucket, C_HOT + np.arange(rel.size)] = 1.0
    for h in range(MH):
        c[h, C_SELI + h] = CAP
        c[MH + h, C_SELF + h] = -1.0
        c[h, C_NM + h * P:C_NM + (h + 1) * P] = -1.0
        c[MH + h, C_NG + h * P:C_NG + (h + 1) * P] = -1.0
    return c


def build(nc, x, c, ada_w, ada_b, norm_pre, norm_post, w_gate, w_up, w_down, w_in, ig_b, fg_b, head_norm,
          conv_w, sinks, rel_table, w_out, consts, out):
    gate_rows = w_gate.rearrange("l s d f -> (l s d) f")
    up_rows = w_up.rearrange("l s d f -> (l s d) f")
    down_rows = w_down.rearrange("l s f d -> (l s f) d")
    in_rows = w_in.rearrange("l d f -> (l d) f")
    out_rows = w_out.rearrange("l d f -> (l d) f")
    ada_rows = ada_w.rearrange("l d f -> (l d) f")
    skew = nc.dram_tensor("skew", (P, AG * 3 * CHUNK), F32, kind="Internal").ap()

    with ExitStack() as ctx:
        def sb(name, shape, dt=F32):
            return ctx.enter_context(nc.sbuf_tensor(name, shape, dt))

        def sem(name):
            return ctx.enter_context(nc.semaphore(name))

        ps = ctx.enter_context(nc.psum_tensor("ps", [P, 8, 512], F32))

        raw = [sb(f"raw{s}", [P, KT * PC]) for s in range(3)]
        hi = [sb(f"hi{s}", [P, KT * PC], F32R) for s in range(3)]
        lo = [sb(f"lo{s}", [P, KT * PC], F32R) for s in range(3)]
        ada_raw = [sb(f"ada_raw{s}", [P, UK, UC]) for s in range(2)]
        ada_acc = sb("ada_acc", [P, 2, UC])
        xT = sb("xT", [P, KT, S])
        a_hi = sb("a_hi", [P, KT, S], F32R)
        a_lo = sb("a_lo", [P, KT, S], F32R)
        sq = sb("sq", [P, KT, S])
        tmp = sb("tmp", [P, KT, S])
        h32 = sb("h32", [P, KT, S])
        std = sb("std", [P, S])
        rstd = sb("rstd", [P, S])
        ffn_tmp = sb("ffn_tmp", [P, 2, 2 * S])
        silu_g, glu = ffn_tmp[:, 0, :], ffn_tmp[:, 1, :]
        u_hi = sb("u_hi", [P, 2, S], F32R)
        u_lo = sb("u_lo", [P, 2, S], F32R)
        cst = sb("cst", [P, C_ALL])
        ones = sb("ones", [P, S])
        zeros = sb("zeros", [P, P])
        m_hi = sb("m_hi", [P, KT - 2, S], F32R)
        m_lo = sb("m_lo", [P, KT - 2, S], F32R)
        eps = sb("eps", [P, 1])
        rows = sb("rows", [P, 3, P])
        cols = sb("cols", [P, 3 * P])
        adab = sb("adab", [P, (DEPTH + 1) * 72])
        c_col = sb("c_col", [P, KT])
        mods = sb("mods", [P, WRAP + 2 * KT])
        warm = sb("warm", [P, 1])
        mod_a = sb("mod_a", [P, KT])
        mod_c = sb("mod_c", [P, KT])
        tab = sb("tab", [N_BUCKETS, AH])
        bias = sb("bias", [P, AG, NCH, 2 * CHUNK])
        sink = sb("sink", [P, DEPTH, AG])
        sink8 = sb("sink8", [P, AG, NCH])
        half_gain = sb("half_gain", [P, DEPTH * MH])
        gb = sb("gb", [2 * MH, DEPTH])
        gb15 = sb("gb15", [2 * MH, DEPTH])
        wg = sb("wg", [P, KT, 2 * MH])
        qT = sb("qT", [P, 2, S])
        kT = sb("kT", [P, 2, S])
        trow, bias1 = qT[:, :, 0:3 * CHUNK], kT[:, :, 0:2 * CHUNK]
        vm = sb("vm", [P, 2, MH * DV])
        aqT = sb("aqT", [P, AG, S])
        akT = sb("akT", [P, S])
        av = sb("av", [P, 3, P])
        th_o, yc, cc_s = h32[:, 0:4, :], h32[:, 4:6, :], sq[:, 4:6, :]
        hm, sc = tmp[:, 4:8, :], tmp[:, 0:4, :].rearrange("p k s -> p (k s)").rearrange("p (r n) -> p r n", n=P)
        qe = [sq[:, 6, :], sq[:, 7, :], std[:], rstd[:]]
        pT = ffn_tmp[:].rearrange("p k s -> p (k s)").rearrange("p (r n) -> p r n", n=P)
        th = sb("th", [2 * MH, S])
        sp = sb("sp", [2 * MH, S])
        sp2 = sb("sp2", [2 * MH, S])
        gsum = sb("gsum", [2 * MH, S])
        arow = sb("arow", [MH, S])
        mrow = sb("mrow", [MH, S])
        acol = sb("acol", [P, 2, MH])
        floor = sb("floor", [P, S])
        ecap = sb("ecap", [P, 3 * P])
        edec = sb("edec", [P, 3 * P])
        tabx = ecap[0:N_BUCKETS, 0:AG * AKV * CHUNK].rearrange("b (g k q) -> b g k q", g=AG, k=AKV)
        pm = sb("pm", [P, 3 * P])
        dd = sb("dd", [P, S])
        qden = sb("qden", [P, 2, S])
        mx = sb("mx", [P, 3, AG * NCH])
        sums = sb("sums", [P, 4, AG * NCH])
        up_s = sb("up_s", [P, 2, S + 2])

        ident = cst[:, C_ID:C_ID + P]
        pre_col = P + 72
        HEAD, CONV, CC = 2 * P, 2 * P + 8, 2 * P + 20

        def mix_tile(parts, k0):
            if k0 == 4:
                return (u_hi if parts == "hi" else u_lo)[:]
            t = m_hi if parts == "hi" else m_lo
            k1 = k0 if k0 < 4 else k0 - 2
            return t[:, k1:k1 + 2, :]

        raw_loaded = [sem(f"raw_loaded{s}") for s in range(3)]
        hi_ready = [sem(f"hi_ready{s}") for s in range(3)]
        lo_ready = [sem(f"lo_ready{s}") for s in range(3)]
        panel_used = [sem(f"panel_used{s}") for s in range(3)]
        ada_loaded = [sem(f"ada_loaded{s}") for s in range(2)]
        ada_steps = sem("ada_steps")
        ada_turned = sem("ada_turned")
        mods_ready = sem("mods_ready")
        warmed = sem("warmed")
        consts_in, c_in, x_in, small_in, ones_set, tab_in = (sem(n) for n in
            ("consts_in", "c_in", "x_in", "small_in", "ones_set", "tab_in"))
        cols_turned, cols_ready, silu_c_ready, x_turned, x_ready = (sem(n) for n in
            ("cols_turned", "cols_ready", "silu_c_ready", "x_turned", "x_ready"))
        prep, tabx_ready, t_rows, t_rows_out, skew_out, skew_in, bias_ready = (sem(n) for n in
            ("prep", "tabx_ready", "t_rows", "t_rows_out", "skew_out", "skew_in", "bias_ready"))
        y_done, ysq_ready, ysum_ready, ystd_ready, post_link, x_tile, xsq_ready, xsum_ready, xstd_ready = (
            sem(n) for n in ("y_done", "ysq_ready", "ysum_ready", "ystd_ready", "post_link", "x_tile",
                             "xsq_ready", "xsum_ready", "xstd_ready"))
        pre_link, t_ready, h_hi, h_lo, h_f32 = (sem(n) for n in ("pre_link", "t_ready", "h_hi", "h_lo", "h_f32"))
        y_scaled, rx_ready, sm_link, pr_link = (sem(n) for n in ("y_scaled", "rx_ready", "sm_link", "pr_link"))
        silu_ready, glu_ready, u_hi_ready, u_lo_ready = (sem(n) for n in (
            "silu_ready", "glu_ready", "u_hi_ready", "u_lo_ready"))
        wg_in = sem("wg_in")
        gates_done, th_ready, ez_ready, sp_ready, g_ready, a_done, arow_ready, m_ready = (sem(n) for n in (
            "gates_done", "th_ready", "ez_ready", "sp_ready", "g_ready", "a_done", "arow_ready", "m_ready"))
        proj_read = sem("proj_read")
        av_ready = sem("av_ready")
        scores_done, s_link, smax_ready, probs_exp, sink_exp, probs_ready = (sem(n) for n in (
            "scores_done", "s_link", "smax_ready", "probs_exp", "sink_exp", "probs_ready"))
        probs_turned, pT_ready, attn_done, attn_read = (sem(n) for n in (
            "probs_turned", "pT_ready", "attn_done", "attn_read"))
        decay_done, qk_done, floor_ready, cap_ready, dec_ready, pm_ready, num_done, hm_link, hm_ready, hmsq_ready = (
            sem(n) for n in ("decay_done", "qk_done", "floor_ready", "cap_ready", "dec_ready", "pm_ready",
                             "num_done", "hm_link", "hm_ready", "hmsq_ready"))
        hmsum_done, hmstd_ready, out_link, mix_f32, mix_hi, mix_lo, conv_link = (sem(n) for n in (
            "hmsum_done", "hmstd_ready", "out_link", "mix_f32", "mix_hi", "mix_lo", "conv_link"))
        o_turned, o_ready, out_stored = sem("o_turned"), sem("o_ready"), sem("out_stored")

        pro_loaded = [sem(f"pro_loaded{s}") for s in range(4)]
        block = ctx.enter_context(nc.Block())
        pro_raw = [ada_raw[0][:], ada_raw[1][:], raw[DN][:].rearrange("p (k n) -> p k n", n=UC),
                   h32[:].rearrange("p k s -> p (k s)").rearrange("p (k n) -> p k n", n=UC)]

        def panel(t, s):
            return t[s][:].rearrange("p (k n) -> p k n", n=PC)

        def rowpanel(t, s):
            return t[s][:].rearrange("p (k n) -> p k n", n=D)

        def by_group(t, g, turned):
            v = panel(t, 2)
            if turned:
                return v.rearrange("p k (g v d) -> p k g v d", v=AKV, g=AG)[:, :, g, :, :]
            return v.rearrange("p k (v g d) -> p k v g d", v=AKV, g=AG)[:, :, :, g, :]

        def block_no(l, third, b=0):
            return N_BLK * l + (PRO_BLK + THIRD * third) + b

        def shift_at(sub):
            return WRAP if sub == 0 else 3 * sub * KT

        def steps(blk, s, k):
            return (2 * UK) * (blk + 1) + (UK * s + k)

        def mod_col(third, b):
            return PRO_BLK * UT + THIRD * UT * third + UT * b

        def mix_used(eng, l, m):
            eng.wait_ge(panel_used[m % 3], CREDIT + USES * l + (MIX0 + m // 3 + 1))

        @block.sync
        def _(sp_e):
            def load(s, l, n, dst, src):
                sp_e.wait_ge(lo_ready[s], CREDIT + USES * l + n)
                sp_e.dma_start(dst, src).then_inc(raw_loaded[s], 16)

            def wide(rows_, r0, c0):
                return rows_[bass.ds(r0, D), bass.ds(c0, PC)].rearrange("(k p) n -> p k n", p=P)

            def load_gate(l, ffn, n0, i, now=None):
                src = wide(gate_rows, l * (2 * D) + ffn * D, i * PC)
                load(G, l if now is None else now, n0 + i if now is None else USES, panel(raw, G), src)

            def load_up(l, ffn, n0, i, now=None):
                src = wide(up_rows, l * (2 * D) + ffn * D, i * PC)
                load(U, l if now is None else now, n0 + i if now is None else USES, panel(raw, U), src)

            def load_down(l, ffn, n0, i):
                src = down_rows[bass.ds(l * (2 * D_FF) + ffn * D_FF + i * PC, PC), :].rearrange("(k p) n -> p k n", p=P)
                load(DN, l, n0 + i, rowpanel(raw, DN), src)

            def load_ada(s, blk, layer, c):
                sp_e.wait_ge(ada_steps, steps(blk - 1, s, UK))
                src = ada_rows[bass.ds(layer * D + s * (UK * P), UK * P), bass.ds(c, UC)]
                sp_e.dma_start(ada_raw[s][:], src.rearrange("(k p) n -> p k n", p=P)).then_inc(ada_loaded[s], 16)

            sp_e.dma_start(rows[0:72, 0, :], ada_b[0].rearrange("(r n) -> r n", n=P)).then_inc(c_in, 16)
            sp_e.dma_start(rows[72:120, 0, :], norm_pre.rearrange("l s (r n) -> (l s r) n", n=P)).then_inc(c_in, 16)
            sp_e.dma_start(rows[0:72, 1, :], ada_b[1].rearrange("(r n) -> r n", n=P)).then_inc(c_in, 16)
            sp_e.dma_start(rows[72:120, 1, :], norm_post.rearrange("l s (r n) -> (l s r) n", n=P)).then_inc(c_in, 16)
            sp_e.dma_start(rows[0:8, 2, :], head_norm.rearrange("l (r n) -> (l r) n", n=P)).then_inc(c_in, 16)
            sp_e.dma_start(rows[8:20, 2, :], conv_w.rearrange("l k (r n) -> (l k r) n", n=P)).then_inc(c_in, 16)
            sp_e.dma_start(rows[20:28, 2, :], c.rearrange("b (r n) -> (b r) n", n=P)).then_inc(c_in, 16)
            sp_e.dma_start(cst[:, 0:C_HOT], consts[:, 0:C_HOT]).then_inc(consts_in, 16)
            sp_e.dma_start(cst[0:N_BUCKETS, C_HOT:], consts[0:N_BUCKETS, C_HOT:]).then_inc(consts_in, 16)
            xv = x.rearrange("b (t p) d -> (b p) t d", p=P)
            for n in range(2 * PRO_BLK):
                b, s, i = n // 2, n % 2, n % 4
                if n >= 4:
                    sp_e.wait_ge(ada_steps, steps(b - 2, s, UK))
                src = ada_rows[s * UK * P:(s + 1) * UK * P, b * UC:(b + 1) * UC].rearrange("(k p) n -> p k n", p=P)
                sp_e.dma_start(pro_raw[i], src).then_inc(pro_loaded[i], 16)
                if n == 0:
                    sp_e.dma_start(tmp[:].rearrange("p k s -> p (k s)").rearrange("p (t d) -> p t d", t=2), xv) \
                        .then_inc(x_in, 16)
                if n == 4:
                    sp_e.dma_start(panel(raw, G), wide(gate_rows, 0, 0)).then_inc(raw_loaded[G], 16)
                if n == 6:
                    sp_e.dma_start(panel(raw, U), wide(up_rows, 0, 0)).then_inc(raw_loaded[U], 16)

            with sp_e.Fori(0, DEPTH) as l:
                after = (l + 1) % DEPTH

                def ffn_loads(ffn, n0, third):
                    for s in range(2):
                        load_ada(s, block_no(l, third), l, (PRO_BLK + THIRD * third) * UC)
                    if third == 2:
                        two_steps(ffn, n0, third, 0, l, (PRO_BLK + THIRD * third + 1) * UC)
                        with sp_e.Fori(1, (NF - 1) // 2) as j:
                            two_steps(ffn, n0, third, j, after, (j - 1) * UC)
                    else:
                        with sp_e.Fori(0, (NF - 1) // 2) as j:
                            two_steps(ffn, n0, third, j, l, j * UC + (PRO_BLK + THIRD * third + 1) * UC)

                def two_steps(ffn, n0, third, j, layer, c):
                    for step in range(2):
                        i = 2 * j + step
                        load_gate(l, ffn, n0, i + 1)
                        load_down(l, ffn, n0, i)
                        load_up(l, ffn, n0, i + 1)
                        load_ada(step, block_no(l, third, 1 + j), layer, c)

                def load_mix(m):
                    src = wide(in_rows, l * D, IN_COLS[IN_ORDER[m]]) if m < N_IN else \
                        wide(out_rows, l * D, (m - N_IN) * PC)
                    load(m % 3, l, MIX0 + m // 3, panel(raw, m % 3), src)

                def mixer_ada(u):
                    b, s = u // 2, u % 2
                    load_ada(s, block_no(l, 1, b), l, (PRO_BLK + THIRD + b) * UC)

                ffn_loads(0, 0, 0)
                load_mix(0)
                load_down(l, 0, 0, NF - 1)
                mixer_ada(0)
                load_mix(1)
                mixer_ada(1)
                load_mix(2)
                sp_e.wait_ge(gates_done, CREDIT + l)
                sp_e.dma_start(wg[:], in_rows[bass.ds(l * D, D), COL_GATES:COL_GATES + 2 * MH]
                               .rearrange("(k p) n -> p k n", p=P)).then_inc(wg_in, 16)
                mixer_ada(2)
                mixer_ada(3)
                between = {6: (4,), 7: (5,), 8: (6, 7), 10: (8, 9), 12: (10, 11)}
                for m in range(3, N_MIX):
                    load_mix(m)
                    for u in between.get(m, ()):
                        mixer_ada(u)
                load_gate(l, 1, FFB0, 0)
                load_up(l, 1, FFB0, 0)
                ffn_loads(1, FFB0, 2)
                load_gate(after, 0, 0, 0, l)
                load_down(l, 1, FFB0, NF - 1)
                load_up(after, 0, 0, 0, l)
            for t in range(2):
                sp_e.wait_ge(o_ready, 2 * (t + 1))
                sp_e.dma_start(out[0, t * P:(t + 1) * P, :], tmp[:, 4 * t:4 * t + 4, :].rearrange("p k s -> p (k s)")) \
                    .then_inc(out_stored, 16)
            sp_e.wait_ge(out_stored, 32)
            for s in (G, U):
                sp_e.wait_ge(raw_loaded[s], 16 * (DEPTH * USES + 1))

        @block.gpsimd
        def _(pool):
            nc.gpsimd.memset(ones[:], 1.0).then_inc(ones_set, 1)
            nc.gpsimd.memset(zeros[:], 0.0).then_inc(ones_set, 1)
            nc.gpsimd.memset(eps[:], EPS).then_inc(ones_set, 1)
            nc.gpsimd.memset(up_s[:], 0.0).then_inc(ones_set, 1)
            pool.dma_start(tab[:], rel_table).then_inc(tab_in, 16)
            with nc.allow_non_contiguous_dma(reason="a few words of gate biases and sinks"):
                pool.dma_start(gb[0:MH, :], ig_b.rearrange("l h -> h l")).then_inc(small_in, 16)
                pool.dma_start(gb[MH:2 * MH, :], fg_b.rearrange("l h -> h l")).then_inc(small_in, 16)
                for kv in range(AKV):
                    pool.dma_start(sink[kv * CHUNK:(kv + 1) * CHUNK, :, :],
                                   sinks[:, kv * AG:(kv + 1) * AG].rearrange("(o l) g -> o l g", o=1)
                                   .to_broadcast([CHUNK, DEPTH, AG])).then_inc(small_in, 16)
            pool.wait_ge(tab_in, 16)
            for g in range(AG):
                for kv in range(AKV):
                    nc.gpsimd.tensor_copy(tabx[:, g, kv, :], tab[:, kv * AG + g:kv * AG + g + 1]
                                          .to_broadcast([N_BUCKETS, CHUNK])).then_inc(tabx_ready, 1)
            pool.wait_ge(t_rows_out, 1)
            pool.dma_start(skew.rearrange("p (g r) -> p g r", g=AG), trow).then_inc(skew_out, 16)
            pool.wait_ge(skew_out, 16)
            W = AG * 3 * CHUNK
            for kv in range(AKV):
                o = kv * CHUNK * W + CHUNK - 1
                src = skew.rearrange("p r -> (p r)")[o:o + CHUNK * (W - 1)] if o + CHUNK * (W - 1) <= P * W else None
                v = src.rearrange("(q r) -> q r", r=W - 1)
                for g in range(AG):
                    pool.dma_start(bias1[kv * CHUNK:(kv + 1) * CHUNK, g, :],
                                   v[:, g * 3 * CHUNK:g * 3 * CHUNK + 2 * CHUNK]).then_inc(skew_in, 16)
            pool.wait_ge(skew_in, 64)
            for g in range(AG):
                for j in range(1, NCH):
                    nc.gpsimd.tensor_copy(bias[:, g, j, :], bias1[:, g, :]).then_inc(bias_ready, 1)
                nc.gpsimd.tensor_copy(bias[:, g, 0, 0:CHUNK], bias1[:, g, CHUNK:]).then_inc(bias_ready, 1)
                nc.gpsimd.memset(bias[:, g, 0, CHUNK:], MASKED).then_inc(bias_ready, 1)

        @block.scalar
        def _(act):
            def split(s, l, n):
                act.wait_ge(raw_loaded[s], 16 * (USES * l + n + 1))
                act.wait_ge(panel_used[s], CREDIT + USES * l + n)
                nc.scalar.activation(hi[s][:], raw[s][:], ACT.Copy).then_inc(hi_ready[s], 1)

            def split_aq(l):
                act.wait_ge(raw_loaded[2], 16 * (USES * l + MIX0 + 1))
                act.wait_ge(panel_used[2], CREDIT + USES * l + MIX0)
                for g in range(AG):
                    last = nc.scalar.activation(by_group(hi, g, True), by_group(raw, g, False), ACT.Copy)
                last.then_inc(hi_ready[2], 1)

            act.wait_ge(ones_set, 4)
            for signal in (silu_ready, floor_ready, dec_ready, warmed, hmsq_ready):
                act.sem_inc(signal, CREDIT)
            act.wait_ge(cols_ready, 3)
            nc.scalar.activation(c_col[:], cols[:, CC:CC + KT], ACT.Silu).then_inc(silu_c_ready, 1)
            split(G, 0, 0)
            split(U, 0, 0)

            with act.Fori(0, DEPTH) as l:
                def post(sub):
                    r = 3 * l + sub
                    act.wait_ge(warmed, r + 1)
                    nc.scalar.activation(warm[:], eps[:], ACT.Sqrt).then_inc(warmed, 1)
                    for b in range(4):
                        if sub == 1:
                            mix_used(act, l, N_IN + b)
                        elif b < 3:
                            act.wait_ge(y_done, 3 * (2 * l + sub // 2) + b + 1)
                        else:
                            act.wait_ge(panel_used[DN], CREDIT + USES * l + (NF if sub == 0 else USES))
                        nc.scalar.activation(sq[:, 2 * b:2 * b + 2, :].rearrange("p k s -> p (k s)"), ps[:, b, :],
                                             ACT.Square).then_inc(ysq_ready, 1)
                    act.wait_ge(ysum_ready, CREDIT + r + 1)
                    act.wait_ge(rx_ready, r + 1)
                    nc.scalar.activation(std[:], ps[:, BK_B, 0:S], ACT.Sqrt, bias=eps[:], scale=1.0 / D) \
                        .then_inc(ystd_ready, 1)

                def pre(sub, mixer):
                    r = 3 * l + sub
                    for b in range(4):
                        act.wait_ge(x_tile, 4 * r + b + 1)
                        act.wait_ge(ysum_ready, CREDIT + r)
                        nc.scalar.activation(sq[:, 2 * b:2 * b + 2, :], xT[:, 2 * b:2 * b + 2, :], ACT.Square) \
                            .then_inc(xsq_ready, 1)
                    act.wait_ge(xsum_ready, r + 1)
                    act.wait_ge(post_link, CREDIT + r)
                    nc.scalar.activation(std[:], ps[:, BK_A, 0:S], ACT.Sqrt, bias=eps[:], scale=1.0 / D) \
                        .then_inc(xstd_ready, 1)
                    for k in range(KT):
                        act.wait_ge(t_ready, KT * r + k + 1)
                        shift = mods[:, shift_at(sub) + k:shift_at(sub) + k + 1]
                        nc.scalar.activation(a_hi[:, k, :], tmp[:, k, :], ACT.Identity, bias=shift).then_inc(h_hi, 1)
                        if mixer:
                            nc.scalar.activation(h32[:, k, :], tmp[:, k, :], ACT.Identity, bias=shift) \
                                .then_inc(h_f32, 1)

                def silu(f, n0, i):
                    act.wait_ge(panel_used[G], CREDIT + USES * l + (n0 + 1) + i)
                    act.wait_ge(glu_ready, CREDIT + f + i)
                    nc.scalar.activation(silu_g, ps[:, BK_GATE, :], ACT.Silu).then_inc(silu_ready, 1)

                def high_u(f, n0, i):
                    act.wait_ge(glu_ready, CREDIT + f + i + 1)
                    act.wait_ge(panel_used[DN], CREDIT + USES * l + n0 + i)
                    nc.scalar.activation(u_hi[:].rearrange("p k s -> p (k s)"), glu, ACT.Copy).then_inc(u_hi_ready, 1)

                def ffn(ffn_, n0):
                    f = l * (2 * NF) + ffn_ * NF
                    silu(f, n0, 0)
                    split(G, l, n0 + 1)
                    with act.Fori(0, NF - 1) as i:
                        split(DN, l, n0 + i)
                        high_u(f, n0, i)
                        split(U, l, n0 + 1 + i)
                        silu(f, n0, i + 1)
                        split(G, l, n0 + 2 + i)
                    split(DN, l, n0 + NF - 1)
                    high_u(f, n0, NF - 1)
                    split(U, l, n0 + NF)

                pre(0, False)
                ffn(0, 0)
                post(0)
                split_aq(l)
                pre(1, True)

                def evac(m, dst, func=ACT.Copy, scale=1.0, bank=None, view=None):
                    mix_used(act, l, m)
                    src = ps[:, BK_GATE + m % 2, :] if view is None else view
                    nc.scalar.activation(dst, src, func, scale=scale).then_inc(proj_read, 1)

                def next_split(m):
                    split(m % 3, l, MIX0 + m // 3)

                act.wait_ge(bias_ready, AG * (NCH + 1))
                evac(0, qT[:].rearrange("p k s -> p (k s)"))
                next_split(3)
                act.wait_ge(gates_done, CREDIT + l + 1)
                nc.scalar.activation(th[:], ps[0:2 * MH, BK_B, 0:S], ACT.Tanh, bias=gb15[:, bass.ds(l, 1)],
                                     scale=1.0 / CAP).then_inc(th_ready, 1)
                act.wait_ge(th_ready, l + 1)
                nc.scalar.activation(sp[:], th[:], ACT.Exp, scale=-CAP).then_inc(ez_ready, 1)
                act.wait_ge(ez_ready, l + 1)
                nc.scalar.activation(sp2[:], sp[:], ACT.Ln, bias=1.0).then_inc(sp_ready, 1)
                evac(1, kT[:].rearrange("p k s -> p (k s)"))
                next_split(4)
                evac(2, aqT[:].rearrange("p k s -> p (k s)"))
                next_split(5)
                evac(3, akT[:], view=ps[:, BK_UP, 0:S])
                nc.scalar.activation(av[:].rearrange("p w d -> p (w d)"), ps[:, BK_A, 0:3 * P], ACT.Copy) \
                    .then_inc(av_ready, 1)

                def floor_of(h):
                    act.wait_ge(decay_done, MH * l + h + 1)
                    act.wait_ge(hm_link, CREDIT + (MH * l + h))
                    nc.scalar.activation(floor[:], ps[:, 2, S:2 * S], ACT.Exp).then_inc(floor_ready, 1)

                def decay(h):
                    act.wait_ge(cap_ready, CREDIT + 2 * (MH * l + h + 1))
                    nc.scalar.activation(edec[:], ecap[:], ACT.Exp).then_inc(dec_ready, 1)

                def square_head(h):
                    act.wait_ge(hm_ready, CREDIT + MH * l + h + 1)
                    nc.scalar.activation(sq[:, h, :], hm[:, h, :], ACT.Square)
                    nc.scalar.activation(qe[h], qden[:, h % 2, :], ACT.Square, scale=EPS ** 0.5).then_inc(hmsq_ready, 1)

                def std_heads(b):
                    act.wait_ge(hmsum_done, 2 * l + b + 1)
                    nc.scalar.activation(tmp[:, 2 * b:2 * b + 2, :].rearrange("p k s -> p (k s)"), ps[:, b, :],
                                         ACT.Sqrt, scale=1.0 / DV).then_inc(hmstd_ready, 1)

                def high_mix(n, k0):
                    act.wait_ge(mix_f32, 4 * l + n + 1)
                    nc.scalar.activation(mix_tile("hi", k0), h32[:, k0:k0 + 2, :], ACT.Copy).then_inc(mix_hi, 1)

                floor_of(0)
                next_split(6)
                decay(0)
                evac(4, vm[:, :, 0:PC], view=ps[:, BK_GATE, :].rearrange("p (t d) -> p t d", t=2))
                floor_of(1)
                next_split(7)
                decay(1)
                act.wait_ge(smax_ready, l + 1)
                for r in range(AG * NCH):
                    nc.scalar.activation(sc[:, r, :], sc[:, r, :], ACT.Exp, bias=mx[:, 2, r:r + 1],
                                         accum_out=sums[:, 0, r:r + 1]).then_inc(probs_exp, 1)
                nc.scalar.activation(sums[:, 1, :], mx[:, 1, :], ACT.Exp).then_inc(sink_exp, 1)
                square_head(0)
                evac(5, vm[:, :, PC:2 * PC], view=ps[:, BK_UP, :].rearrange("p (t d) -> p t d", t=2))
                floor_of(2)
                next_split(8)
                decay(2)
                square_head(1)
                evac(6, cc_s.rearrange("p k s -> p (k s)"))
                floor_of(3)
                next_split(9)
                decay(3)
                square_head(2)
                for b in range(2):
                    act.wait_ge(probs_turned, 2 * l + b + 1)
                    nc.scalar.activation(pT[:, 4 * b:4 * b + 4, :].rearrange("p r q -> p (r q)"), ps[:, b, :], ACT.Copy) \
                        .then_inc(pT_ready, 1)
                next_split(10)
                square_head(3)
                std_heads(0)
                high_mix(0, 6)
                next_split(11)
                high_mix(1, 4)
                std_heads(1)
                evac(9, th_o[:, 0:2, :].rearrange("p k s -> p (k s)"), ACT.Tanh, 0.5)
                next_split(12)
                high_mix(2, 0)
                evac(10, th_o[:, 2:4, :].rearrange("p k s -> p (k s)"), ACT.Tanh, 0.5)
                high_mix(3, 2)
                for m in range(13, N_MIX + 2):
                    next_split(m)
                post(1)
                pre(2, False)
                ffn(1, FFB0)
                post(2)

            for t in range(2):
                for b in range(2):
                    act.wait_ge(o_turned, 2 * t + b + 1)
                    nc.scalar.activation(tmp[:, 4 * t + 2 * b:4 * t + 2 * b + 2, :].rearrange("p k s -> p (k s)"),
                                         ps[:, 4 + 2 * t + b, :], ACT.Copy) \
                        .then_inc(o_ready, 1)

        @block.vector
        def _(dve):
            def split(s, l, n):
                dve.wait_ge(hi_ready[s], USES * l + n + 1)
                nc.vector.tensor_tensor(lo[s][:], raw[s][:], hi[s][:].bitcast(F32), ALU.subtract) \
                    .then_inc(lo_ready[s], 1)

            def split_aq(l):
                dve.wait_ge(hi_ready[2], USES * l + MIX0 + 1)
                for g in range(AG):
                    last = nc.vector.tensor_tensor(by_group(lo, g, True), by_group(raw, g, False),
                                                   by_group(hi, g, True).bitcast(F32), ALU.subtract)
                last.then_inc(lo_ready[2], 1)

            def ada_unit(s, blk, part=None, acc=0, lag=0):
                if part != 1:
                    dve.wait_ge(ada_loaded[s], 16 * (blk - PRO_BLK + 1))
                for k in range(0 if part is None else part * UK // 2, UK if part is None else (part + 1) * UK // 2):
                    c1 = c_col[:, s * UK + k:s * UK + k + 1]
                    total = ada_acc[:, acc, :]
                    if s == 0 and k == 0:
                        dve.wait_ge(ada_turned, CREDIT + blk - lag)
                        step = nc.vector.tensor_scalar(total, ada_raw[s][:, k, :], c1, None, ALU.mult)
                    else:
                        dve.wait_ge(ada_steps, steps(blk, s, k))
                        step = nc.vector.scalar_tensor_tensor(total, ada_raw[s][:, k, :], c1, total, ALU.mult, ALU.add)
                    step.then_inc(ada_steps, 1)

            def pro_unit(s, blk):
                i = (2 * blk + s) % 4
                dve.wait_ge(pro_loaded[i], 16 * (blk // 2 + 1))
                for k in range(UK):
                    c1 = c_col[:, s * UK + k:s * UK + k + 1]
                    total = ada_acc[:, 0, :]
                    if s == 0 and k == 0:
                        dve.wait_ge(ada_turned, CREDIT + blk)
                        step = nc.vector.tensor_scalar(total, pro_raw[i][:, k, :], c1, None, ALU.mult)
                    else:
                        dve.wait_ge(ada_steps, steps(blk, s, k))
                        step = nc.vector.scalar_tensor_tensor(total, pro_raw[i][:, k, :], c1, total, ALU.mult, ALU.add)
                    step.then_inc(ada_steps, 1)

            def ada_mods(blk, bank, at, col, b_col):
                dve.wait_ge(ada_turned, CREDIT + blk + 1)
                nc.vector.tensor_tensor(mods[:, bass.ds(col, UT)], ps[:, bank, at:at + UT],
                                        adab[:, bass.ds(b_col, UT)], ALU.add).then_inc(mods_ready, 1)

            dve.sem_inc(ada_steps, 2 * UK)
            for signal in (*lo_ready, mods_ready, glu_ready, u_lo_ready, post_link, hm_link, cap_ready,
                           pm_ready, hm_ready):
                dve.sem_inc(signal, CREDIT)
            for g in range(3):
                dve.wait_ge(cols_turned, g + 1)
                n = 28 if g == 2 else 120
                nc.vector.tensor_copy(cols[:, g * P:g * P + n], ps[:, g, 0:n]).then_inc(cols_ready, 1)
            dve.wait_ge(cols_ready, 3)
            for b in range(DEPTH + 1):
                src = cols[:, (b % DEPTH) * P:(b % DEPTH) * P + 72]
                nc.vector.tensor_copy(adab[:, 72 * b:72 * b + 72], src).then_inc(prep, 1)
            dve.wait_ge(small_in, 64)
            nc.vector.tensor_scalar(gb15[:], gb[:], 1.0 / CAP, None, ALU.mult).then_inc(prep, 1)
            nc.vector.tensor_scalar(half_gain[:], cols[:, HEAD:HEAD + DEPTH * MH], 0.5, None, ALU.mult).then_inc(prep, 1)
            dve.wait_ge(prep, DEPTH + 3)
            dve.wait_ge(silu_c_ready, 1)
            for b in range(PRO_BLK):
                if b == 1:
                    for t in range(4):
                        dve.wait_ge(x_turned, t + 1)
                        nc.vector.tensor_copy(xT[:, 2 * t:2 * t + 2, :].rearrange("p k s -> p (k s)"), ps[:, t, :]) \
                            .then_inc(x_tile, 1)
                pro_unit(0, b)
                if b == PRO_BLK - 1:
                    split(G, 0, 0)
                pro_unit(1, b)
                if b == PRO_BLK - 2:
                    dve.wait_ge(t_rows, 1)
                    nc.vector.tensor_copy(trow, ps[:, 4, 0:AG * 3 * CHUNK].rearrange("p (g r) -> p g r", g=AG)) \
                        .then_inc(t_rows_out, 1)
                if b == PRO_BLK - 1:
                    split(U, 0, 0)
                ada_mods(b, BK_A, 0, WRAP + UT * b, UT * b)

            with dve.Fori(0, DEPTH) as l:
                def post(sub, w):
                    r = 3 * l + sub
                    gate = mods[:, (3 * sub + 2) * KT:(3 * sub + 3) * KT]
                    gp = cols[:, bass.ds(P + 72 + (3 * l + sub) * KT, KT)]
                    dve.wait_ge(mods_ready, CREDIT + block_no(l, sub + 1))
                    nc.vector.scalar_tensor_tensor(mod_c[:], gate, 1.0, gp, ALU.add, ALU.mult).then_inc(pre_link, 1)
                    dve.wait_ge(pre_link, 3 * r + 2)
                    nc.vector.tensor_scalar(mod_c[:], mod_c[:], w, None, ALU.mult).then_inc(pre_link, 1)
                    dve.wait_ge(ystd_ready, r + 1)
                    nc.vector.reciprocal(rstd[:], std[:]).then_inc(post_link, 1)
                    dve.wait_ge(post_link, CREDIT + r + 1)
                    dve.wait_ge(pre_link, 3 * r + 3)

                    def scale_y(b):
                        for k in (2 * b, 2 * b + 1):
                            nc.vector.scalar_tensor_tensor(tmp[:, k, :], ps[:, b, (k % 2) * S:(k % 2 + 1) * S],
                                                           mod_c[:, k:k + 1], rstd[:], ALU.mult, ALU.mult) \
                                .then_inc(y_scaled, 1)

                    scale_y(0)
                    for b in range(4):
                        if b < 3:
                            scale_y(b + 1)
                        dve.wait_ge(y_scaled, 8 * r + 2 * b + 2)
                        nc.vector.tensor_tensor(xT[:, 2 * b:2 * b + 2, :], xT[:, 2 * b:2 * b + 2, :],
                                                tmp[:, 2 * b:2 * b + 2, :], ALU.add).then_inc(x_tile, 1)

                def pre(sub):
                    r = 3 * l + sub
                    gp = cols[:, bass.ds(72 + (3 * l + sub) * KT, KT)]
                    scale = mods[:, shift_at(sub) + KT:shift_at(sub) + 2 * KT]
                    dve.wait_ge(mods_ready, CREDIT + block_no(l, sub))
                    nc.vector.scalar_tensor_tensor(mod_a[:], scale, 1.0, gp, ALU.add, ALU.mult).then_inc(pre_link, 1)
                    dve.wait_ge(xstd_ready, r + 1)
                    nc.vector.reciprocal(rstd[:], std[:]).then_inc(rx_ready, 1)
                    dve.wait_ge(rx_ready, r + 1)
                    dve.wait_ge(pre_link, 3 * r + 1)
                    def low(k):
                        shift = mods[:, shift_at(sub) + k:shift_at(sub) + k + 1]
                        dve.wait_ge(h_hi, KT * r + k + 1)
                        nc.vector.scalar_tensor_tensor(a_lo[:, k, :], tmp[:, k, :], shift,
                                                       a_hi[:, k, :].bitcast(F32), ALU.add, ALU.subtract) \
                            .then_inc(h_lo, 1)
                    for k in range(KT):
                        nc.vector.scalar_tensor_tensor(tmp[:, k, :], xT[:, k, :], mod_a[:, k:k + 1], rstd[:],
                                                       ALU.mult, ALU.mult).then_inc(t_ready, 1)
                        if k >= 2:
                            low(k - 2)
                    low(KT - 2)
                    low(KT - 1)

                def mult_up(f, n0, i):
                    dve.wait_ge(panel_used[U], CREDIT + USES * l + (n0 + 1) + i)
                    dve.wait_ge(silu_ready, CREDIT + f + i + 1)
                    dve.wait_ge(u_lo_ready, CREDIT + f + i)
                    nc.vector.tensor_tensor(glu, ps[:, BK_UP, :], silu_g, ALU.mult).then_inc(glu_ready, 1)

                def low_u(f, i):
                    dve.wait_ge(u_hi_ready, f + i + 1)
                    nc.vector.tensor_tensor(u_lo[:].rearrange("p k s -> p (k s)"), glu,
                                            u_hi[:].bitcast(F32).rearrange("p k s -> p (k s)"), ALU.subtract) \
                        .then_inc(u_lo_ready, 1)

                def third_mods(third, b, bank=BK_A, at=0):
                    ada_mods(block_no(l, third, b), bank, at, mod_col(third, b), MCOLS * l + mod_col(third, b))

                def ffn(ffn_, n0, third):
                    f = l * (2 * NF) + ffn_ * NF
                    for s in range(2):
                        ada_unit(s, block_no(l, third))
                    split(G, l, n0 + 1)
                    with dve.Fori(0, (NF - 1) // 2) as j:
                        for step in range(2):
                            i = 2 * j + step
                            blk = block_no(l, third, 1 + j)
                            if step == 1:
                                ada_unit(1, blk, 0)
                            split(DN, l, n0 + i)
                            mult_up(f, n0, i)
                            low_u(f, i)
                            split(U, l, n0 + 1 + i)
                            if step == 0:
                                third_mods(third, j)
                                ada_unit(0, blk)
                            else:
                                ada_unit(1, blk, 1)
                            split(G, l, n0 + 2 + i)
                    split(DN, l, n0 + NF - 1)
                    mult_up(f, n0, NF - 1)
                    low_u(f, NF - 1)
                    third_mods(third, THIRD - 1)
                    split(U, l, n0 + NF)

                pre(0)
                def mixer_ada(u):
                    ada_unit(u % 2, block_no(l, 1, u // 2), None, u // 2 % 2, min(u // 2, 1))

                def mixer_mods(b, bank):
                    third_mods(1, b, bank, TURN_AT if bank == 3 else 0)

                ffn(0, 0, 0)
                mixer_ada(0)
                mixer_ada(1)
                post(0, 0.5)
                split_aq(l)
                pre(1)

                def next_split(m):
                    split(m % 3, l, MIX0 + m // 3)

                next_split(3)
                dve.wait_ge(sp_ready, l + 1)
                nc.vector.tensor_tensor_scan(gsum[:], ones[0:2 * MH, :], sp2[:], 0.0, ALU.mult, ALU.subtract) \
                    .then_inc(g_ready, 1)
                mixer_ada(2)
                next_split(4)
                mixer_ada(3)
                mixer_mods(0, BK_A)
                for g in range(AG):
                    nc.vector.tensor_copy(sink8[:, g, :], sink[:, bass.ds(l, 1), g:g + 1]
                                          .rearrange("p a b -> p (a b)").to_broadcast([P, NCH])).then_inc(s_link, 1)
                dve.wait_ge(a_done, l + 1)
                nc.vector.tensor_copy(arow[:], ps[0:MH, BK_B, 0:S]).then_inc(arow_ready, 1)
                nc.vector.tensor_copy(acol[:].rearrange("p t h -> p (t h)"), ps[:, BK_B, S:S + 2 * MH]) \
                    .then_inc(arow_ready, 1)
                dve.wait_ge(arow_ready, 2 * l + 2)
                nc.vector.tensor_tensor_scan(mrow[:], arow[:], arow[:], MASKED, ALU.max, ALU.max).then_inc(m_ready, 1)
                next_split(5)
                mixer_ada(4)
                mixer_ada(5)

                def decay(h):
                    dve.wait_ge(floor_ready, CREDIT + MH * l + h + 1)
                    dve.wait_ge(dec_ready, CREDIT + MH * l + h)
                    cap = cst[:, C_CAP:C_CAP + S]
                    nc.vector.scalar_tensor_tensor(ecap[:, 0:S], ps[:, 2, 0:S], acol[:, 0, h:h + 1], cap,
                                                   ALU.add, ALU.min).then_inc(cap_ready, 1)
                    nc.vector.scalar_tensor_tensor(ecap[:, S:S + P], ps[:, 2, P:S], acol[:, 1, h:h + 1], cap[:, 0:P],
                                                   ALU.add, ALU.min).then_inc(cap_ready, 1)

                def weigh(h, blk=None):
                    dve.wait_ge(dec_ready, CREDIT + MH * l + h + 1)
                    dve.wait_ge(qk_done, MH * l + h + 1)
                    if blk is not None:
                        mixer_mods(blk, 3)
                    dve.wait_ge(num_done, CREDIT + MH * l + h)
                    nc.vector.scalar_tensor_tensor(pm[:], ps[:, 3, 0:3 * P], DQK ** -0.5, edec[:], ALU.mult, ALU.mult) \
                        .then_inc(pm_ready, 1)

                def head_out(h):
                    n = MH * l + h
                    dve.wait_ge(num_done, CREDIT + n + 1)
                    dve.wait_ge(floor_ready, CREDIT + n + 1)
                    if h >= 2:
                        dve.wait_ge(hmsq_ready, CREDIT + n - 1)
                    den = ps[:, BK_B, S:2 * S]
                    nc.vector.scalar_tensor_tensor(dd[:], den, -1.0, floor[:], ALU.mult, ALU.max).then_inc(hm_link, 1)
                    nc.vector.tensor_copy(hm[:, h, :], ps[:, BK_B, 0:S])
                    dve.wait_ge(hm_link, CREDIT + n + 1)
                    nc.vector.tensor_tensor(qden[:, h % 2, :], dd[:], den, ALU.max).then_inc(hm_ready, 1)

                def tap(t, k):
                    return cols[:, bass.ds(CONV + 6 * l + 2 * t + k, 1)]

                def conv():
                    dve.wait_ge(proj_read, N_READ * l + 7)
                    mix_used(dve, l, 7)
                    nc.vector.tensor_tensor(up_s[:, :, 2:], ps[:, BK_UP, :].rearrange("p (k s) -> p k s", k=2), cc_s,
                                            ALU.mult).then_inc(proj_read, 1)
                    dve.wait_ge(proj_read, N_READ * l + 8)
                    for k in range(2):
                        nc.vector.tensor_scalar(yc[:, k, :], up_s[:, k, 0:S], tap(0, k), None, ALU.mult) \
                            .then_inc(conv_link, 1)
                    for t in (1, 2):
                        for k in range(2):
                            dve.wait_ge(conv_link, 6 * l + 2 * (t - 1) + k + 1)
                            nc.vector.scalar_tensor_tensor(yc[:, k, :], up_s[:, k, t:t + S], tap(t, k), yc[:, k, :],
                                                           ALU.mult, ALU.add).then_inc(conv_link, 1)

                def low_mix(n, k0):
                    dve.wait_ge(mix_hi, 4 * l + n + 1)
                    nc.vector.tensor_tensor(mix_tile("lo", k0), h32[:, k0:k0 + 2, :],
                                            mix_tile("hi", k0).bitcast(F32), ALU.subtract).then_inc(mix_lo, 1)

                def norm_heads(b):
                    sl = slice(2 * b, 2 * b + 2)
                    dve.wait_ge(hmstd_ready, 2 * l + b + 1)
                    nc.vector.reciprocal(tmp[:, sl, :], tmp[:, sl, :]).then_inc(out_link, 1)
                    dve.wait_ge(out_link, 6 * l + 3 * b + 1)
                    for h in (2 * b, 2 * b + 1):
                        nc.vector.scalar_tensor_tensor(hm[:, h, :], hm[:, h, :], half_gain[:, bass.ds(MH * l + h, 1)],
                                                       tmp[:, h, :], ALU.mult, ALU.mult).then_inc(out_link, 1)

                def gate_heads(b):
                    sl = slice(2 * b, 2 * b + 2)
                    dve.wait_ge(proj_read, N_READ * l + 9 + b)
                    dve.wait_ge(out_link, 6 * l + 3 * b + 3)
                    nc.vector.scalar_tensor_tensor(h32[:, sl, :], th_o[:, sl, :], 1.0, hm[:, sl, :], ALU.add, ALU.mult) \
                        .then_inc(mix_f32, 1)

                def score_rows():
                    dve.wait_ge(bias_ready, AG * (NCH + 1))
                    dve.wait_ge(scores_done, l + 1)
                    for g in range(AG):
                        nc.vector.scalar_tensor_tensor(
                            sc[:, g * NCH:(g + 1) * NCH, :].rearrange("p j k -> p (j k)"), ps[:, g, :], DH ** -0.5,
                            bias[:, g, :, :].rearrange("p j k -> p (j k)"), ALU.mult, ALU.add).then_inc(s_link, 1)
                    base = 6 * l + 4
                    dve.wait_ge(s_link, base)
                    nc.vector.tensor_reduce(mx[:, 0, :], sc, AX_X, ALU.max).then_inc(s_link, 1)
                    dve.wait_ge(s_link, base + 1)
                    sk = sink8[:].rearrange("p g j -> p (g j)")
                    nc.vector.tensor_tensor(mx[:, 0, :], mx[:, 0, :], sk, ALU.max).then_inc(s_link, 1)
                    dve.wait_ge(s_link, base + 2)
                    nc.vector.tensor_tensor(mx[:, 1, :], sk, mx[:, 0, :], ALU.subtract).then_inc(sm_link, 1)
                    nc.vector.tensor_scalar(mx[:, 2, :], mx[:, 0, :], -1.0, None, ALU.mult).then_inc(smax_ready, 1)

                def norm_probs():
                    dve.wait_ge(probs_exp, AG * NCH * (l + 1))
                    dve.wait_ge(sink_exp, l + 1)
                    nc.vector.tensor_tensor(sums[:, 2, :], sums[:, 0, :], sums[:, 1, :], ALU.add).then_inc(pr_link, 1)
                    dve.wait_ge(pr_link, 2 * l + 1)
                    nc.vector.reciprocal(sums[:, 3, :], sums[:, 2, :]).then_inc(pr_link, 1)
                    dve.wait_ge(pr_link, 2 * l + 2)
                    nc.vector.tensor_tensor(sc, sc, sums[:, 3, :].rearrange("p (r o) -> p r o", o=1)
                                            .to_broadcast([P, AG * NCH, P]), ALU.mult).then_inc(probs_ready, 1)

                decay(0)
                next_split(6)
                weigh(0, 1)
                mixer_ada(6)
                score_rows()
                head_out(0)
                decay(1)
                next_split(7)
                weigh(1, 2)
                mixer_ada(7)
                head_out(1)
                decay(2)
                next_split(8)
                weigh(2)
                norm_probs()
                mixer_ada(8)
                head_out(2)
                decay(3)
                next_split(9)
                weigh(3, 3)
                mixer_ada(9)
                conv()
                head_out(3)
                next_split(10)
                dve.wait_ge(attn_done, l + 1)
                nc.vector.tensor_copy(h32[:, 6:8, :].rearrange("p k s -> p (k s)"), ps[:, BK_A, :]) \
                    .then_inc(mix_f32, 1)
                norm_heads(0)
                low_mix(0, 6)
                mix_used(dve, l, 8)
                dve.wait_ge(conv_link, 6 * l + 6)
                nc.vector.tensor_tensor(h32[:, 4:6, :].rearrange("p k s -> p (k s)"), ps[:, BK_GATE, :],
                                        yc.rearrange("p k s -> p (k s)"), ALU.mult).then_inc(mix_f32, 1)
                next_split(11)
                low_mix(1, 4)
                norm_heads(1)
                gate_heads(0)
                mixer_mods(4, BK_A)
                next_split(12)
                low_mix(2, 0)
                mixer_ada(10)
                gate_heads(1)
                low_mix(3, 2)
                next_split(13)
                next_split(14)
                mixer_ada(11)
                next_split(15)
                mixer_mods(THIRD - 1, BK_A)
                next_split(16)
                post(1, 1.0)
                pre(2)
                ffn(1, FFB0, 2)
                post(2, 0.5)

        @block.tensor
        def _(pe):
            def take(s, l, n):
                pe.wait_ge(lo_ready[s], CREDIT + USES * l + n + 1)

            def product(dst, w_hi, w_lo, b_hi, b_lo, first, last):
                nc.tensor.matmul(dst, w_hi, b_hi, start=first, stop=False, skip_group_check=True)
                nc.tensor.matmul(dst, w_hi, b_lo, start=False, stop=False, skip_group_check=True)
                return nc.tensor.matmul(dst, w_lo, b_hi, start=False, stop=last, skip_group_check=True)

            def ada_turn(blk, bank=BK_A, at=0, acc=0):
                pe.wait_ge(ada_steps, steps(blk, 1, UK))
                pe.wait_ge(mods_ready, CREDIT + blk)
                for j in range(UT):
                    last = nc.tensor.matmul(ps[:, bank, at + j:at + j + 1], ada_acc[:, acc, j * P:(j + 1) * P],
                                            ones[:, 0:1], start=True, stop=True)
                last.then_inc(ada_turned, 1)

            for signal in (*panel_used, ada_turned, gates_done, ysum_ready, num_done):
                pe.sem_inc(signal, CREDIT)
            pe.wait_ge(consts_in, 32)
            pe.wait_ge(c_in, 7 * 16)
            for g in range(3):
                n = 28 if g == 2 else 120
                nc.tensor.transpose(ps[:, g, 0:n], rows[0:n, g, :], ident[0:n, 0:n]).then_inc(cols_turned, 1)
            pe.wait_ge(ones_set, 4)
            pe.wait_ge(tabx_ready, 4)
            for g in range(AG):
                last = nc.tensor.matmul(ps[:, 4, g * 192:(g + 1) * 192],
                                        tabx[:, g, :, :].rearrange("b k q -> b (k q)"),
                                        cst[0:N_BUCKETS, C_HOT:C_HOT + 192], start=True, stop=True)
            last.then_inc(t_rows, 1)
            for b in range(PRO_BLK):
                ada_turn(b)
                if b == 0:
                    pe.wait_ge(x_in, 16)
                    pe.wait_ge(cols_ready, 3)
                    xt = tmp[:].rearrange("p k s -> p (k s)").rearrange("p (t d) -> p t d", t=2)
                    for k in range(KT):
                        for t in range(2):
                            last = nc.tensor.transpose(ps[:, k // 2, (k % 2) * S + t * P:(k % 2) * S + (t + 1) * P],
                                                       xt[:, t, k * P:(k + 1) * P], ident)
                        if k % 2:
                            last.then_inc(x_turned, 1)
            pe.wait_ge(t_rows_out, 1)

            with pe.Fori(0, DEPTH) as l:
                def sum_bank(bank, ready, n0, b, done=None):
                    pe.wait_ge(ready, n0 + b + 1)
                    for k in (2 * b, 2 * b + 1):
                        last = nc.tensor.matmul(ps[:, bank, 0:S], ones[:, 0:P], sq[:, k, :], start=(k == 0),
                                                stop=(k == KT - 1), skip_group_check=True)
                    if done is not None:
                        last.then_inc(done, 1)

                def keep_warm(n):
                    for _ in range(n):
                        nc.tensor.matmul(ps[:, BK_UP, 0:S], ones[:, 0:P], ones[:], start=True, stop=True)

                def pre(sub):
                    r = 3 * l + sub
                    pe.wait_ge(mods_ready, CREDIT + block_no(l, sub))
                    for b in range(4):
                        sum_bank(BK_A, xsq_ready, 4 * r, b, xsum_ready if b == 3 else None)
                    keep_warm(WARM)

                def post(sub):
                    r = 3 * l + sub
                    for b in range(4) if sub == 1 else (3,):
                        sum_bank(BK_B, ysq_ready, 4 * r, b, ysum_ready if b == 3 else None)
                    keep_warm(WARM)

                def first_panel(bank, s, r):
                    nc.tensor.matmul(ps[:, bank, 0:1], zeros[:], ones[:, 0:1], start=True, stop=False,
                                     skip_group_check=True)
                    for k in range(KT):
                        pe.wait_ge(h_lo, KT * r + k + 1)
                        for j in range(2):
                            last = product(ps[:, bank, j * S:(j + 1) * S], panel(hi, s)[:, k, j * P:(j + 1) * P],
                                           panel(lo, s)[:, k, j * P:(j + 1) * P], a_hi[:, k, :], a_lo[:, k, :],
                                           False, k == KT - 1)
                    return last

                def wide_tile(bank, s, j):
                    for k in range(KT):
                        last = product(ps[:, bank, j * S:(j + 1) * S], panel(hi, s)[:, k, j * P:(j + 1) * P],
                                       panel(lo, s)[:, k, j * P:(j + 1) * P], a_hi[:, k, :], a_lo[:, k, :],
                                       k == 0, k == KT - 1)
                    return last

                def gate(f, n0, i, r=None):
                    take(G, l, n0 + i)
                    pe.wait_ge(silu_ready, CREDIT + f + i)
                    if r is not None:
                        last = first_panel(BK_GATE, G, r)
                    else:
                        for j in range(2):
                            last = wide_tile(BK_GATE, G, j)
                    last.then_inc(panel_used[G], 1)

                def up(f, n0, i):
                    take(U, l, n0 + i)
                    pe.wait_ge(glu_ready, CREDIT + f + i)
                    for j in range(2):
                        last = wide_tile(BK_UP, U, j)
                    last.then_inc(panel_used[U], 1)

                def down(f, n0, i, final, sub=None):
                    take(DN, l, n0 + i)
                    pe.wait_ge(u_lo_ready, CREDIT + f + i + 1)
                    for m in range(KT):
                        for a in range(2):
                            last = product(ps[:, m // 2, (m % 2) * S:(m % 2 + 1) * S],
                                           rowpanel(hi, DN)[:, a, m * P:(m + 1) * P],
                                           rowpanel(lo, DN)[:, a, m * P:(m + 1) * P],
                                           u_hi[:, a, :], u_lo[:, a, :], False, final and a == 1)
                        if final and m in (1, 3, 5):
                            last.then_inc(y_done, 1)
                        if m == KT - 1:
                            last.then_inc(panel_used[DN], 1)
                        if final and m >= 5:
                            sum_bank(BK_B, ysq_ready, 4 * (3 * l + sub), m - 5)

                def ffn(n0, third, sub):
                    f = l * (2 * NF) + (0 if third == 0 else NF)
                    gate(f, n0, 0, 3 * l + sub)
                    for b in range(4):
                        nc.tensor.matmul(ps[:, b, 0:1], zeros[:], ones[:, 0:1], start=True, stop=False,
                                         skip_group_check=True)
                    with pe.Fori(0, (NF - 1) // 2) as j:
                        for step in range(2):
                            i = 2 * j + step
                            up(f, n0, i)
                            if step == 0:
                                ada_turn(block_no(l, third, j))
                            gate(f, n0, i + 1)
                            down(f, n0, i, False)
                    up(f, n0, NF - 1)
                    ada_turn(block_no(l, third, THIRD - 1))
                    down(f, n0, NF - 1, True, sub)

                def mix_take(m):
                    take(m % 3, l, MIX0 + m // 3)
                    if m >= 2:
                        pe.wait_ge(proj_read, N_READ * l + min(m - 1, 8))
                    if m == 10:
                        pe.wait_ge(mix_f32, 4 * l + 2)

                def mix_release(m, last):
                    last.then_inc(panel_used[m % 3], 1)

                def project(m, r=None):
                    mix_take(m)
                    if r is not None:
                        last = first_panel(BK_GATE + m % 2, m % 3, r)
                    else:
                        for j in range(2):
                            last = wide_tile(BK_GATE + m % 2, m % 3, j)
                    mix_release(m, last)

                def project_tokens(m):
                    mix_take(m)
                    for t in range(2):
                        for k in range(KT):
                            tok = slice(t * P, (t + 1) * P)
                            last = product(ps[:, BK_GATE + m % 2, t * PC:(t + 1) * PC], a_hi[:, k, tok], a_lo[:, k, tok],
                                           panel(hi, m % 3)[:, k, :], panel(lo, m % 3)[:, k, :], k == 0, k == KT - 1)
                    mix_release(m, last)

                def gates():
                    pe.wait_ge(wg_in, 16 * (l + 1))
                    for k in range(KT):
                        pe.wait_ge(h_f32, KT * l + k + 1)
                        last = nc.tensor.matmul(ps[0:2 * MH, BK_B, 0:S], wg[:, k, :], h32[:, k, :], start=(k == 0),
                                                stop=(k == KT - 1))
                    last.then_inc(gates_done, 1)

                def project_aq():
                    mix_take(2)
                    for g in range(AG):
                        for k in range(KT):
                            w = [panel(t, 2)[:, k, g * P:(g + 1) * P] for t in (hi, lo)]
                            last = product(ps[:, BK_GATE, g * S:(g + 1) * S], w[0], w[1], a_hi[:, k, :], a_lo[:, k, :],
                                           k == 0, k == KT - 1)
                    mix_release(2, last)

                def project_akv():
                    mix_take(3)
                    wide_tile(BK_UP, 0, 0)
                    for w in range(3):
                        tok = slice(w * CHUNK, w * CHUNK + P)
                        for k in range(KT):
                            last = product(ps[:, BK_A, w * P:(w + 1) * P], a_hi[:, k, tok], a_lo[:, k, tok],
                                           panel(hi, 0)[:, k, P:2 * P], panel(lo, 0)[:, k, P:2 * P], k == 0,
                                           k == KT - 1)
                    mix_release(3, last)

                def log_weights():
                    pe.wait_ge(g_ready, l + 1)
                    sel_i, sel_f = cst[0:2 * MH, C_SELI:C_SELI + MH], cst[0:2 * MH, C_SELF:C_SELF + MH]
                    for t in range(2):
                        o = ps[:, BK_B, S + t * MH:S + (t + 1) * MH]
                        nc.tensor.matmul(o, th[:, t * P:(t + 1) * P], sel_i, start=True, stop=False)
                        nc.tensor.matmul(o, gsum[:, t * P:(t + 1) * P], sel_f, start=False, stop=True)
                    nc.tensor.matmul(ps[0:MH, BK_B, 0:S], sel_i, th[:], start=True, stop=False)
                    nc.tensor.matmul(ps[0:MH, BK_B, 0:S], sel_f, gsum[:], start=False, stop=True).then_inc(a_done, 1)

                def scores():
                    for g in range(AG):
                        for j in range(NCH):
                            k0 = max(j - 1, 0) * CHUNK
                            for kv in range(AKV):
                                pr = slice(kv * DH, (kv + 1) * DH)
                                last = nc.tensor.matmul(ps[pr, g, j * P:(j + 1) * P],
                                                        aqT[pr, g, j * CHUNK:(j + 1) * CHUNK], akT[pr, k0:k0 + P],
                                                        start=True, stop=True)
                    last.then_inc(scores_done, 1)

                def decay_and_qk(h, blk=None):
                    pe.wait_ge(m_ready, l + 1)
                    pe.wait_ge(floor_ready, CREDIT + MH * l + h)
                    pe.wait_ge(cap_ready, CREDIT + 2 * (MH * l + h))
                    neg_m = cst[0:MH, C_NM + h * P:C_NM + (h + 1) * P]
                    neg_g = cst[0:2 * MH, C_NG + h * P:C_NG + (h + 1) * P]
                    nc.tensor.matmul(ps[:, 2, 0:S], neg_m, mrow[:], start=True, stop=True)
                    nc.tensor.matmul(ps[:, 2, S:2 * S], neg_g, gsum[:], start=True, stop=False)
                    nc.tensor.matmul(ps[:, 2, S:2 * S], neg_m, mrow[:], start=False, stop=True).then_inc(decay_done, 1)
                    pe.wait_ge(pm_ready, CREDIT + MH * l + h)
                    if blk is not None:
                        mixer_turn(blk, 3)
                    pr = slice((h % 2) * DQK, (h % 2 + 1) * DQK)
                    nc.tensor.matmul(ps[:, 3, 0:S], kT[pr, h // 2, 0:P], qT[pr, h // 2, :], start=True, stop=True)
                    nc.tensor.matmul(ps[:, 3, S:S + P], kT[pr, h // 2, P:S], qT[pr, h // 2, P:S], start=True,
                                     stop=True).then_inc(qk_done, 1)

                def numerator(h):
                    pe.wait_ge(pm_ready, CREDIT + MH * l + h + 1)
                    pe.wait_ge(hm_ready, CREDIT + MH * l + h)
                    pe.wait_ge(arow_ready, 2 * l + 2)
                    for o, w0, w1 in ((0, vm[:, 0, h * DV:(h + 1) * DV], vm[:, 1, h * DV:(h + 1) * DV]),
                                      (S, ones[:, 0:P], ones[:, 0:P])):
                        nc.tensor.matmul(ps[:, BK_B, o:o + S], w0, pm[:, 0:S], start=True, stop=False)
                        last = nc.tensor.matmul(ps[:, BK_B, o + P:o + S], w1, pm[:, S:S + P], start=False, stop=True)
                    last.then_inc(num_done, 1)

                def turn_probs():
                    pe.wait_ge(probs_ready, l + 1)
                    for r in range(AG * NCH):
                        last = nc.tensor.transpose(ps[:, r // 4, (r % 4) * P:(r % 4 + 1) * P], sc[:, r, :], ident)
                        if r % 4 == 3:
                            last.then_inc(probs_turned, 1)

                def attend():
                    pe.wait_ge(pT_ready, 2 * l + 2)
                    for g in range(AG):
                        for j in range(NCH):
                            for kv in range(AKV):
                                last = nc.tensor.matmul(
                                    ps[g * DH:(g + 1) * DH, BK_A, kv * S + j * CHUNK:kv * S + (j + 1) * CHUNK],
                                    av[:, max(j - 1, 0), kv * DH:(kv + 1) * DH],
                                    pT[:, g * NCH + j, kv * CHUNK:(kv + 1) * CHUNK], start=True, stop=True)
                    last.then_inc(attn_done, 1)

                def sum_heads(b):
                    pe.wait_ge(hmsq_ready, CREDIT + MH * l + 2 * b + 2)
                    for h in (2 * b, 2 * b + 1):
                        o = ps[:, b, (h % 2) * S:(h % 2 + 1) * S]
                        nc.tensor.matmul(o, ones[:, 0:P], sq[:, h, :], start=True, stop=False)
                        last = nc.tensor.matmul(o, ones[:, 0:P], qe[h], start=False, stop=True)
                    last.then_inc(hmsum_done, 1)

                def mixer_turn(b, bank):
                    ada_turn(block_no(l, 1, b), bank, TURN_AT if bank == 3 else 0, b % 2)

                def mix_out(b):
                    m = N_IN + b
                    take(m % 3, l, MIX0 + m // 3)
                    order = [(j, k) for ks in ((6, 7, 4, 5, 0, 1), (2, 3)) for j in range(2) for k in ks] if b == 0 \
                        else [(j, k) for j in range(2) for k in range(KT)]
                    if b == 0:
                        nc.tensor.matmul(ps[:, b, 0:1], zeros[:], ones[:, 0:1], start=True, stop=False,
                                         skip_group_check=True)
                    seen = set()
                    for j, k in order:
                        if b == 0 and k // 2 not in seen:
                            seen.add(k // 2)
                            pe.wait_ge(mix_lo, 4 * l + len(seen))
                        last = product(ps[:, b, j * S:(j + 1) * S], panel(hi, m % 3)[:, k, j * P:(j + 1) * P],
                                       panel(lo, m % 3)[:, k, j * P:(j + 1) * P],
                                       mix_tile("hi", k - k % 2)[:, k % 2, :], mix_tile("lo", k - k % 2)[:, k % 2, :],
                                       b > 0 and k == 0, k == (3 if b == 0 else KT - 1))
                    mix_release(m, last)

                pre(0)
                ffn(0, 0, 0)
                post(0)
                pre(1)
                project(0, 3 * l + 1)
                gates()
                project(1)
                mixer_turn(0, BK_A)
                project_aq()
                log_weights()
                pe.wait_ge(mods_ready, CREDIT + block_no(l, 1, 1))
                project_akv()
                decay_and_qk(0, 1)
                pe.wait_ge(proj_read, N_READ * l + 4)
                project_tokens(4)
                scores()
                pe.wait_ge(proj_read, N_READ * l + 5)
                numerator(0)
                decay_and_qk(1, 2)
                project_tokens(5)
                numerator(1)
                decay_and_qk(2)
                project(6)
                pe.wait_ge(proj_read, N_READ * l + 6)
                numerator(2)
                decay_and_qk(3, 3)
                turn_probs()
                project(7)
                numerator(3)
                attend()
                sum_heads(0)
                project(8)
                sum_heads(1)
                project(9)
                pe.wait_ge(mix_f32, 4 * l + 1)
                mixer_turn(4, BK_A)
                project(10)
                pe.wait_ge(hmstd_ready, 2 * l + 2)
                for b in range(N_OUT):
                    mix_out(b)
                    if b == 2:
                        mixer_turn(THIRD - 1, BK_A)
                post(1)
                pre(2)
                ffn(FFB0, 2, 2)
                post(2)

            pe.wait_ge(mods_ready, CREDIT + block_no(DEPTH, 0))
            pe.wait_ge(ystd_ready, 3 * DEPTH)
            for b in range(4):
                pe.wait_ge(x_tile, 4 * (3 * DEPTH + 1))
                t = b // 2
                for k in range(4 * (b % 2), 4 * (b % 2) + 4):
                    last = nc.tensor.transpose(ps[:, 4 + b, (k % 4) * P:(k % 4 + 1) * P], xT[:, k, t * P:(t + 1) * P],
                                               ident)
                last.then_inc(o_turned, 1)


_INS = ["x", "c", "ada_w", "ada_b", "norm_pre", "norm_post", "ffn_w_gate", "ffn_w_up", "ffn_w_down", "w_in",
        "mlstm_igate_bias", "mlstm_fgate_bias", "mlstm_head_norm", "conv_w", "attn_sinks", "rel_bias_table", "w_out"]


def kernel(**inputs):
    import concourse.bacc as bacc
    from concourse.bass_utils import run_bass_kernel_spmd

    nc = bacc.Bacc("TRN2", target_bir_lowering=False, num_devices=1)
    arrays, args = {}, []
    for name in _INS + ["constants"]:
        a = constant_table() if name == "constants" else np.ascontiguousarray(inputs[name])
        arrays[f"in_{name}"] = a
        args.append(nc.dram_tensor(f"in_{name}", a.shape, mybir.dt.from_np(a.dtype), kind="ExternalInput").ap())
    args.append(nc.dram_tensor("out_x", (1, S, D), F32, kind="ExternalOutput").ap())
    build(nc, *args)
    r = run_bass_kernel_spmd(nc, [arrays], core_ids=[0])
    return r.results[0]["out_x"]
```

```python
from contextlib import ExitStack

import numpy as np

import concourse.bass as bass
from concourse import mybir

F32 = mybir.dt.float32
F32R = mybir.dt.float32r
ALU = mybir.AluOpType
ACT = mybir.ActivationFunctionType
AX_X = mybir.AxisListType.X

P = 128
D = 1024
S = 256
DEPTH = 2
KT = D // P
D_FF = 2816
PC = 256
NF = D_FF // PC
N_SUB = 3
EPS = 1e-6
CAP = 15.0
MH, DQK, DV = 4, 64, 128
AH, AKV, AG, DH = 4, 2, 2, 64
CHUNK = 64
NCH = S // CHUNK
N_BUCKETS, MAX_DISTANCE = 32, 128
P_IN = 2824
COL_GATES = 1024
MASKED = -1e30
CREDIT = 1

IN_COLS = dict(mq=0, mk=256, aq=2312, akv=2568, mv0=512, mv1=768, mo0=1032, mo1=1288, cc=1800, cx=2056, cb=1544)
IN_ORDER = ["mq", "mk", "aq", "akv", "mv0", "mv1", "cc", "cx", "cb", "mo0", "mo1"]
N_IN = len(IN_ORDER)
N_OUT = D // PC
N_READ = N_IN - 1
N_MIX = N_IN + N_OUT
MIX_USES = N_MIX // 3
USES = 2 * NF + MIX_USES
MIX0 = NF
FFB0 = NF + MIX_USES
G, U, DN = 0, 1, 2

UK, UC = KT // 2, 512
UT = UC // P
N_BLK = 3 * N_SUB * D // UC
PRO_BLK, THIRD = 2 * D // UC, N_BLK // 3
IN_FFN, BRIDGE = 3, 3
MCOLS = 3 * N_SUB * KT
WRAP = MCOLS

BK_GATE, BK_UP, BK_B, BK_A = 4, 5, 6, 7
BK_X, BK_Y = BK_B, BK_A
BK_OUT = (6, 7, 5, 4)
WARM_POST, WARM_PRE = 10, 8
TURN_AT = 400

C_ID, C_CAP, C_HOT, C_SELI, C_SELF, C_NM, C_NG = 0, 128, 384, 576, 580, 584, 1096
C_ALL = 1608


def constant_table():
    c = np.zeros((P, C_ALL), np.float32)
    c[:, C_ID:C_ID + P] = np.eye(P)
    c[:, C_CAP:C_CAP + P] = np.where(np.arange(P)[:, None] <= np.arange(P)[None, :], 0.0, MASKED)
    rel = np.arange(3 * CHUNK - 1) - (2 * CHUNK - 1)
    nb = N_BUCKETS // 2
    exact = nb // 2
    n = np.abs(rel)
    large = exact + (np.log(np.maximum(n, 1) / exact) / np.log(MAX_DISTANCE / exact) * (nb - exact)).astype(np.int32)
    bucket = (rel > 0).astype(np.int32) * nb + np.where(n < exact, n, np.minimum(large, nb - 1))
    c[bucket, C_HOT + np.arange(rel.size)] = 1.0
    for h in range(MH):
        c[h, C_SELI + h] = CAP
        c[MH + h, C_SELF + h] = -1.0
        c[h, C_NM + h * P:C_NM + (h + 1) * P] = -1.0
        c[MH + h, C_NG + h * P:C_NG + (h + 1) * P] = -1.0
    return c


def build(nc, x, c, ada_w, ada_b, norm_pre, norm_post, w_gate, w_up, w_down, w_in, ig_b, fg_b, head_norm,
          conv_w, sinks, rel_table, w_out, consts, out):
    gate_rows = w_gate.rearrange("l s d f -> (l s d) f")
    up_rows = w_up.rearrange("l s d f -> (l s d) f")
    down_rows = w_down.rearrange("l s f d -> (l s f) d")
    in_rows = w_in.rearrange("l d f -> (l d) f")
    out_rows = w_out.rearrange("l d f -> (l d) f")
    ada_rows = ada_w.rearrange("l d f -> (l d) f")
    skew = nc.dram_tensor("skew", (P, AG * 3 * CHUNK), F32, kind="Internal").ap()

    with ExitStack() as ctx:
        def sb(name, shape, dt=F32):
            return ctx.enter_context(nc.sbuf_tensor(name, shape, dt))

        def sem(name):
            return ctx.enter_context(nc.semaphore(name))

        ps = ctx.enter_context(nc.psum_tensor("ps", [P, 8, 512], F32))

        raw = [sb(f"raw{s}", [P, KT * PC]) for s in range(3)]
        hi = [sb(f"hi{s}", [P, KT * PC], F32R) for s in range(3)]
        lo = [sb(f"lo{s}", [P, KT * PC], F32R) for s in range(3)]
        ada_raw = [sb(f"ada_raw{s}", [P, UK, UC]) for s in range(2)]
        ada_acc = sb("ada_acc", [P, THIRD, UC])
        xT = sb("xT", [P, KT, S])
        inv = sb("inv", [P, S])
        o_scale = sb("o_scale", [P, 2])
        a_hi = sb("a_hi", [P, KT, S], F32R)
        a_lo = sb("a_lo", [P, KT, S], F32R)
        sq = sb("sq", [P, KT, S])
        tmp = sb("tmp", [P, KT, S])
        h32 = sb("h32", [P, KT, S])
        std = sb("std", [P, S])
        rstd = sb("rstd", [P, S])
        ffn_tmp = sb("ffn_tmp", [P, 2, 2 * S])
        silu_g, glu = ffn_tmp[:, 0, :], ffn_tmp[:, 1, :]
        u_hi = sb("u_hi", [P, 2, S], F32R)
        u_lo = sb("u_lo", [P, 2, S], F32R)
        cst = sb("cst", [P, C_ALL])
        ones = sb("ones", [P, S])
        zeros = sb("zeros", [P, P])
        m_hi = sb("m_hi", [P, KT - 2, S], F32R)
        m_lo = sb("m_lo", [P, KT - 2, S], F32R)
        eps = sb("eps", [P, 1])
        cols = sb("cols", [P, 3 * P])
        adab = sb("adab", [P, (DEPTH + 1) * 72])
        c_col = sb("c_col", [P, KT])
        mods = sb("mods", [P, WRAP + 2 * KT])
        warm = sb("warm", [P, 1])
        mod_a = sb("mod_a", [P, KT])
        mod_c = sb("mod_c", [P, KT])
        tab = sb("tab", [N_BUCKETS, AH])
        bias = sb("bias", [P, AG, NCH, 2 * CHUNK])
        sink = sb("sink", [P, DEPTH, AG])
        sink8 = sb("sink8", [P, AG, NCH])
        half_gain = sb("half_gain", [P, DEPTH * MH])
        gb = sb("gb", [2 * MH, DEPTH])
        gb15 = sb("gb15", [2 * MH, DEPTH])
        wg = sb("wg", [P, KT, 2 * MH])
        vm = ada_acc[:, 2:4, :]
        qT, kT = (ada_acc[:, b, :].rearrange("p (k s) -> p k s", k=2) for b in (4, 5))
        aqT = sb("aqT", [P, AG, S])
        akT = sb("akT", [P, S])
        av = sb("av", [P, 3, P])
        th_o, yc, cc_s = h32[:, 0:4, :], h32[:, 4:6, :], sq[:, 4:6, :]
        avT = h32[:, 4, :]
        hm, sc = tmp[:, 4:8, :], tmp[:, 0:4, :].rearrange("p k s -> p (k s)").rearrange("p (r n) -> p r n", n=P)
        qe = [sq[:, 6, :], sq[:, 7, :], std[:], rstd[:]]
        o_rows = [h32[:, 2 * n:2 * n + 2, :].rearrange("p k s -> p (k s)") for n in range(4)]
        pT = ffn_tmp[:].rearrange("p k s -> p (k s)").rearrange("p (r n) -> p r n", n=P)
        th = sb("th", [2 * MH, S])
        sp = sb("sp", [2 * MH, S])
        sp2 = sb("sp2", [2 * MH, S])
        gsum = sb("gsum", [2 * MH, S])
        arow = sb("arow", [MH, S])
        mrow = sb("mrow", [MH, S])
        acol = sb("acol", [P, 2, MH])
        floor = sb("floor", [P, S])
        trow = av[:].rearrange("p w d -> p (w d)").rearrange("p (g r) -> p g r", g=AG)
        bias1 = floor[:].rearrange("p (g r) -> p g r", g=AG)
        ecap = sb("ecap", [P, 3 * P])
        edec = sb("edec", [P, 3 * P])
        tabx = ecap[0:N_BUCKETS, 0:AG * AKV * CHUNK].rearrange("b (g k q) -> b g k q", g=AG, k=AKV)
        rows = edec[:].rearrange("p (g r) -> p g r", g=3)
        pm = sb("pm", [P, 3 * P])
        dd = sb("dd", [P, S])
        eps_std = dd
        qden = sb("qden", [P, 2, S])
        mx = sb("mx", [P, 3, AG * NCH])
        sums = sb("sums", [P, 4, AG * NCH])
        up_s = sb("up_s", [P, 2, S + 2])

        ident = cst[:, C_ID:C_ID + P]
        pre_col = P + 72
        HEAD, CONV, CC = 2 * P, 2 * P + 8, 2 * P + 20

        def mix_tile(parts, k0):
            if k0 == 4:
                return (u_hi if parts == "hi" else u_lo)[:]
            t = m_hi if parts == "hi" else m_lo
            k1 = k0 if k0 < 4 else k0 - 2
            return t[:, k1:k1 + 2, :]

        raw_loaded = [sem(f"raw_loaded{s}") for s in range(3)]
        hi_ready = [sem(f"hi_ready{s}") for s in range(3)]
        lo_ready = [sem(f"lo_ready{s}") for s in range(3)]
        panel_used = [sem(f"panel_used{s}") for s in range(3)]
        ada_loaded = [sem(f"ada_loaded{s}") for s in range(2)]
        ada_steps = sem("ada_steps")
        ada_turned = sem("ada_turned")
        mods_ready = sem("mods_ready")
        warmed = sem("warmed")
        consts_in, c_in, x_in, small_in, ones_set, tab_in = (sem(n) for n in
            ("consts_in", "c_in", "x_in", "small_in", "ones_set", "tab_in"))
        cols_turned, cols_ready, silu_c_ready, x_turned, x_ready = (sem(n) for n in
            ("cols_turned", "cols_ready", "silu_c_ready", "x_turned", "x_ready"))
        prep, tabx_ready, t_rows, t_rows_out, skew_out, skew_in, bias_ready = (sem(n) for n in
            ("prep", "tabx_ready", "t_rows", "t_rows_out", "skew_out", "skew_in", "bias_ready"))
        y_done, ysq_ready, ysum_ready, ystd_ready, post_link, x_tile, xsq_ready, xsum_ready, xstd_ready = (
            sem(n) for n in ("y_done", "ysq_ready", "ysum_ready", "ystd_ready", "post_link", "x_tile",
                             "xsq_ready", "xsum_ready", "xstd_ready"))
        pre_link, t_ready, h_hi, h_lo, h_f32 = (sem(n) for n in ("pre_link", "t_ready", "h_hi", "h_lo", "h_f32"))
        y_gained, q_ready, e_ready = sem("y_gained"), sem("q_ready"), sem("e_ready")
        z_scaled, rx_ready, sm_link, pr_link = (sem(n) for n in ("z_scaled", "rx_ready", "sm_link", "pr_link"))
        silu_ready, glu_ready, u_hi_ready, u_lo_ready = (sem(n) for n in (
            "silu_ready", "glu_ready", "u_hi_ready", "u_lo_ready"))
        wg_in = sem("wg_in")
        gates_done, th_ready, ez_ready, sp_ready, g_ready, a_done, arow_ready, m_ready = (sem(n) for n in (
            "gates_done", "th_ready", "ez_ready", "sp_ready", "g_ready", "a_done", "arow_ready", "m_ready"))
        proj_read = sem("proj_read")
        av_turned, av_ready = sem("av_turned"), sem("av_ready")
        scores_done, s_link, smax_ready, probs_exp, sink_exp, probs_ready = (sem(n) for n in (
            "scores_done", "s_link", "smax_ready", "probs_exp", "sink_exp", "probs_ready"))
        probs_turned, pT_ready, attn_done, attn_read = (sem(n) for n in (
            "probs_turned", "pT_ready", "attn_done", "attn_read"))
        decay_done, qk_done, floor_ready, cap_ready, dec_ready, pm_ready, num_done, hm_link, hm_ready, hmsq_ready = (
            sem(n) for n in ("decay_done", "qk_done", "floor_ready", "cap_ready", "dec_ready", "pm_ready",
                             "num_done", "hm_link", "hm_ready", "hmsq_ready"))
        hmsum_done, hmstd_ready, out_link, mix_f32, mix_hi, mix_lo, conv_link = (sem(n) for n in (
            "hmsum_done", "hmstd_ready", "out_link", "mix_f32", "mix_hi", "mix_lo", "conv_link"))
        o_std_turned, o_scale_ready = sem("o_std_turned"), sem("o_scale_ready")
        o_turned, o_ready, o_last_ready, out_stored = (sem(n) for n in
            ("o_turned", "o_ready", "o_last_ready", "out_stored"))

        pro_loaded = [sem(f"pro_loaded{s}") for s in range(4)]
        block = ctx.enter_context(nc.Block())
        pro_raw = [ada_raw[0][:], ada_raw[1][:], raw[DN][:].rearrange("p (k n) -> p k n", n=UC),
                   h32[:].rearrange("p k s -> p (k s)").rearrange("p (k n) -> p k n", n=UC)]

        def panel(t, s):
            return t[s][:].rearrange("p (k n) -> p k n", n=PC)

        def rowpanel(t, s):
            return t[s][:].rearrange("p (k n) -> p k n", n=D)

        def by_group(t, g, turned):
            v = panel(t, 2)
            if turned:
                return v.rearrange("p k (g v d) -> p k g v d", v=AKV, g=AG)[:, :, g, :, :]
            return v.rearrange("p k (v g d) -> p k v g d", v=AKV, g=AG)[:, :, :, g, :]

        def block_no(l, third, b=0):
            return N_BLK * l + (PRO_BLK + THIRD * third) + b

        def shift_at(sub):
            return WRAP if sub == 0 else 3 * sub * KT

        def steps(blk, s, k):
            return (2 * UK) * (blk + 1) + (UK * s + k)

        def mod_col(third, b):
            return PRO_BLK * UT + THIRD * UT * third + UT * b

        def mix_used(eng, l, m):
            eng.wait_ge(panel_used[m % 3], CREDIT + USES * l + (MIX0 + m // 3 + 1))

        @block.sync
        def _(sp_e):
            def load(s, l, n, dst, src):
                sp_e.wait_ge(lo_ready[s], CREDIT + USES * l + n)
                sp_e.dma_start(dst, src).then_inc(raw_loaded[s], 16)

            def wide(rows_, r0, c0):
                return rows_[bass.ds(r0, D), bass.ds(c0, PC)].rearrange("(k p) n -> p k n", p=P)

            def load_gate(l, ffn, n0, i, now=None):
                src = wide(gate_rows, l * (2 * D) + ffn * D, i * PC)
                load(G, l if now is None else now, n0 + i if now is None else USES, panel(raw, G), src)

            def load_up(l, ffn, n0, i, now=None):
                src = wide(up_rows, l * (2 * D) + ffn * D, i * PC)
                load(U, l if now is None else now, n0 + i if now is None else USES, panel(raw, U), src)

            def load_down(l, ffn, n0, i):
                src = down_rows[bass.ds(l * (2 * D_FF) + ffn * D_FF + i * PC, PC), :].rearrange("(k p) n -> p k n", p=P)
                load(DN, l, n0 + i, rowpanel(raw, DN), src)

            def load_ada(s, blk, layer, c):
                sp_e.wait_ge(ada_steps, steps(blk - 1, s, UK))
                src = ada_rows[bass.ds(layer * D + s * (UK * P), UK * P), bass.ds(c, UC)]
                sp_e.dma_start(ada_raw[s][:], src.rearrange("(k p) n -> p k n", p=P)).then_inc(ada_loaded[s], 16)

            sp_e.dma_start(rows[0:72, 0, :], ada_b[0].rearrange("(r n) -> r n", n=P)).then_inc(c_in, 16)
            sp_e.dma_start(rows[72:120, 0, :], norm_pre.rearrange("l s (r n) -> (l s r) n", n=P)).then_inc(c_in, 16)
            sp_e.dma_start(rows[0:72, 1, :], ada_b[1].rearrange("(r n) -> r n", n=P)).then_inc(c_in, 16)
            sp_e.dma_start(rows[72:120, 1, :], norm_post.rearrange("l s (r n) -> (l s r) n", n=P)).then_inc(c_in, 16)
            sp_e.dma_start(rows[0:8, 2, :], head_norm.rearrange("l (r n) -> (l r) n", n=P)).then_inc(c_in, 16)
            sp_e.dma_start(rows[8:20, 2, :], conv_w.rearrange("l k (r n) -> (l k r) n", n=P)).then_inc(c_in, 16)
            sp_e.dma_start(rows[20:28, 2, :], c.rearrange("b (r n) -> (b r) n", n=P)).then_inc(c_in, 16)
            sp_e.dma_start(cst[:, 0:C_HOT], consts[:, 0:C_HOT]).then_inc(consts_in, 16)
            sp_e.dma_start(cst[0:N_BUCKETS, C_HOT:], consts[0:N_BUCKETS, C_HOT:]).then_inc(consts_in, 16)
            xv = x.rearrange("b (t p) d -> (b p) t d", p=P)
            for n in range(2 * PRO_BLK):
                b, s, i = n // 2, n % 2, n % 4
                if n >= 4:
                    sp_e.wait_ge(ada_steps, steps(b - 2, s, UK))
                src = ada_rows[s * UK * P:(s + 1) * UK * P, b * UC:(b + 1) * UC].rearrange("(k p) n -> p k n", p=P)
                sp_e.dma_start(pro_raw[i], src).then_inc(pro_loaded[i], 16)
                if n == 2:
                    sp_e.dma_start(tmp[:].rearrange("p k s -> p (k s)").rearrange("p (t d) -> p t d", t=2), xv) \
                        .then_inc(x_in, 16)
                if n == 4:
                    sp_e.dma_start(panel(raw, G), wide(gate_rows, 0, 0)).then_inc(raw_loaded[G], 16)
                if n == 6:
                    sp_e.dma_start(panel(raw, U), wide(up_rows, 0, 0)).then_inc(raw_loaded[U], 16)

            with sp_e.Fori(0, DEPTH) as l:
                after = (l + 1) % DEPTH

                def ffn_loads(ffn, n0, third):
                    for s in range(2):
                        load_ada(s, block_no(l, third), l, (PRO_BLK + THIRD * third) * UC)
                    if third == 2:
                        two_steps(ffn, n0, third, 0, l, (PRO_BLK + THIRD * third + 1) * UC)
                        with sp_e.Fori(1, (NF - 1) // 2) as j:
                            two_steps(ffn, n0, third, j, after, (j - 1) * UC)
                    else:
                        with sp_e.Fori(0, (NF - 1) // 2) as j:
                            two_steps(ffn, n0, third, j, l, j * UC + (PRO_BLK + THIRD * third + 1) * UC)

                def two_steps(ffn, n0, third, j, layer, c):
                    for step in range(2):
                        i = 2 * j + step
                        load_gate(l, ffn, n0, i + 1)
                        load_down(l, ffn, n0, i)
                        load_up(l, ffn, n0, i + 1)
                        load_ada(step, block_no(l, third, 1 + j), layer, c)

                def load_mix(m):
                    src = wide(in_rows, l * D, IN_COLS[IN_ORDER[m]]) if m < N_IN else \
                        wide(out_rows, l * D, (m - N_IN) * PC)
                    load(m % 3, l, MIX0 + m // 3, panel(raw, m % 3), src)

                def mixer_ada(u):
                    b, s = u // 2, u % 2
                    load_ada(s, block_no(l, 1, b), l, (PRO_BLK + THIRD + b) * UC)

                ffn_loads(0, 0, 0)
                load_mix(0)
                load_down(l, 0, 0, NF - 1)
                mixer_ada(0)
                load_mix(1)
                mixer_ada(1)
                load_mix(2)
                sp_e.wait_ge(gates_done, CREDIT + l)
                sp_e.dma_start(wg[:], in_rows[bass.ds(l * D, D), COL_GATES:COL_GATES + 2 * MH]
                               .rearrange("(k p) n -> p k n", p=P)).then_inc(wg_in, 16)
                mixer_ada(2)
                mixer_ada(3)
                between = {6: (4,), 7: (5,), 8: (6, 7), 10: (8, 9), 12: (10, 11)}
                for m in range(3, N_MIX):
                    load_mix(m)
                    for u in between.get(m, ()):
                        mixer_ada(u)
                load_gate(l, 1, FFB0, 0)
                load_up(l, 1, FFB0, 0)
                ffn_loads(1, FFB0, 2)
                load_gate(after, 0, 0, 0, l)
                load_down(l, 1, FFB0, NF - 1)
                load_up(after, 0, 0, 0, l)
            for n in range(4):
                if n < 3:
                    sp_e.wait_ge(o_ready, n + 1)
                else:
                    sp_e.wait_ge(o_last_ready, 1)
                h, t = n // 2, n % 2
                sp_e.dma_start(out[0, t * P:(t + 1) * P, h * (D // 2):(h + 1) * (D // 2)], o_rows[n]) \
                    .then_inc(out_stored, 16)
            sp_e.wait_ge(out_stored, 64)
            for s in (G, U):
                sp_e.wait_ge(raw_loaded[s], 16 * (DEPTH * USES + 1))

        @block.gpsimd
        def _(pool):
            nc.gpsimd.memset(ones[:], 1.0).then_inc(ones_set, 1)
            nc.gpsimd.memset(zeros[:], 0.0).then_inc(ones_set, 1)
            nc.gpsimd.memset(eps[:], EPS).then_inc(ones_set, 1)
            nc.gpsimd.memset(up_s[:], 0.0).then_inc(ones_set, 1)
            nc.gpsimd.memset(inv[:], 1.0).then_inc(ones_set, 1)
            nc.gpsimd.memset(eps_std[:], KT * EPS).then_inc(ones_set, 1)
            pool.dma_start(tab[:], rel_table).then_inc(tab_in, 16)
            with nc.allow_non_contiguous_dma(reason="a few words of gate biases and sinks"):
                pool.dma_start(gb[0:MH, :], ig_b.rearrange("l h -> h l")).then_inc(small_in, 16)
                pool.dma_start(gb[MH:2 * MH, :], fg_b.rearrange("l h -> h l")).then_inc(small_in, 16)
                for kv in range(AKV):
                    pool.dma_start(sink[kv * CHUNK:(kv + 1) * CHUNK, :, :],
                                   sinks[:, kv * AG:(kv + 1) * AG].rearrange("(o l) g -> o l g", o=1)
                                   .to_broadcast([CHUNK, DEPTH, AG])).then_inc(small_in, 16)
            pool.wait_ge(tab_in, 16)
            for g in range(AG):
                for kv in range(AKV):
                    nc.gpsimd.tensor_copy(tabx[:, g, kv, :], tab[:, kv * AG + g:kv * AG + g + 1]
                                          .to_broadcast([N_BUCKETS, CHUNK])).then_inc(tabx_ready, 1)
            pool.wait_ge(t_rows_out, 1)
            pool.dma_start(skew.rearrange("p (g r) -> p g r", g=AG), trow).then_inc(skew_out, 16)
            pool.wait_ge(skew_out, 16)
            W = AG * 3 * CHUNK
            for kv in range(AKV):
                o = kv * CHUNK * W + CHUNK - 1
                src = skew.rearrange("p r -> (p r)")[o:o + CHUNK * (W - 1)] if o + CHUNK * (W - 1) <= P * W else None
                v = src.rearrange("(q r) -> q r", r=W - 1)
                for g in range(AG):
                    pool.dma_start(bias1[kv * CHUNK:(kv + 1) * CHUNK, g, :],
                                   v[:, g * 3 * CHUNK:g * 3 * CHUNK + 2 * CHUNK]).then_inc(skew_in, 16)
            pool.wait_ge(raw_loaded[U], 16)
            nc.gpsimd.tensor_copy(hi[U][:], raw[U][:]).then_inc(hi_ready[U], 1)
            pool.wait_ge(hi_ready[U], 1)
            nc.gpsimd.tensor_tensor(lo[U][:], raw[U][:], hi[U][:].bitcast(F32), ALU.subtract).then_inc(lo_ready[U], 1)
            pool.wait_ge(skew_in, 64)
            for g in range(AG):
                for j in range(1, NCH):
                    nc.gpsimd.tensor_copy(bias[:, g, j, :], bias1[:, g, :]).then_inc(bias_ready, 1)
                nc.gpsimd.tensor_copy(bias[:, g, 0, 0:CHUNK], bias1[:, g, CHUNK:]).then_inc(bias_ready, 1)
                nc.gpsimd.memset(bias[:, g, 0, CHUNK:], MASKED).then_inc(bias_ready, 1)

        @block.scalar
        def _(act):
            def split(s, l, n):
                act.wait_ge(raw_loaded[s], 16 * (USES * l + n + 1))
                act.wait_ge(panel_used[s], CREDIT + USES * l + n)
                nc.scalar.activation(hi[s][:], raw[s][:], ACT.Copy).then_inc(hi_ready[s], 1)

            def split_aq(l):
                act.wait_ge(raw_loaded[2], 16 * (USES * l + MIX0 + 1))
                act.wait_ge(panel_used[2], CREDIT + USES * l + MIX0)
                for g in range(AG):
                    last = nc.scalar.activation(by_group(hi, g, True), by_group(raw, g, False), ACT.Copy)
                last.then_inc(hi_ready[2], 1)

            act.wait_ge(ones_set, 6)
            for signal in (silu_ready, floor_ready, dec_ready, warmed, hmsq_ready, e_ready):
                act.sem_inc(signal, CREDIT)
            act.wait_ge(cols_ready, 3)
            nc.scalar.activation(c_col[:], cols[:, CC:CC + KT], ACT.Silu).then_inc(silu_c_ready, 1)
            for b in range(4):
                act.wait_ge(x_turned, b + 1)
                nc.scalar.activation(xT[:, 2 * b:2 * b + 2, :].rearrange("p k s -> p (k s)"), ps[:, b, :], ACT.Copy) \
                    .then_inc(x_tile, 1)
            split(G, 0, 0)

            def load_sqrt(n):
                act.wait_ge(warmed, n)
                nc.scalar.activation(warm[:], eps[:], ACT.Sqrt).then_inc(warmed, 1)

            with act.Fori(0, DEPTH) as l:
                def post(sub):
                    r = 3 * l + sub
                    load_sqrt(4 * l + sub + 2)
                    for b in range(4):
                        if sub == 1:
                            if b < 3:
                                split((14 + b) % 3, l, MIX0 + (14 + b) // 3)
                            mix_used(act, l, N_IN + b)
                        elif b < 3:
                            act.wait_ge(y_done, 3 * (2 * l + sub // 2) + b + 1)
                        else:
                            act.wait_ge(panel_used[DN], CREDIT + USES * l + (NF if sub == 0 else USES))
                        nc.scalar.activation(sq[:, 2 * b:2 * b + 2, :].rearrange("p k s -> p (k s)"), ps[:, b, :],
                                             ACT.Square).then_inc(ysq_ready, 1)
                        act.wait_ge(pre_link, 3 * r + 3)
                        for k in (2 * b, 2 * b + 1):
                            nc.scalar.activation(tmp[:, k, :], ps[:, b, (k % 2) * S:(k % 2 + 1) * S], ACT.Identity,
                                                 scale=mod_c[:, k:k + 1]).then_inc(y_gained, 1)
                    act.wait_ge(ysum_ready, CREDIT + r + 1)
                    act.wait_ge(rx_ready, r + 1)
                    nc.scalar.activation(std[:], ps[:, BK_Y, 0:S], ACT.Sqrt, bias=eps[:], scale=1.0 / D) \
                        .then_inc(ystd_ready, 1)
                    act.wait_ge(ystd_ready, r + 1)
                    nc.scalar.activation(eps_std[:], std[:], ACT.Square, scale=(KT * EPS) ** 0.5).then_inc(e_ready, 1)

                def pre(sub, mixer):
                    r = 3 * l + sub
                    if sub == 0:
                        load_sqrt(4 * l + 1)
                    for b in range(4):
                        act.wait_ge(x_tile, 4 * r + b + 1)
                        act.wait_ge(ysum_ready, CREDIT + r)
                        nc.scalar.activation(sq[:, 2 * b:2 * b + 2, :], xT[:, 2 * b:2 * b + 2, :], ACT.Square) \
                            .then_inc(xsq_ready, 1)
                    act.wait_ge(xsum_ready, r + 1)
                    act.wait_ge(post_link, CREDIT + r)
                    nc.scalar.activation(std[:], ps[:, BK_X, 0:S], ACT.Sqrt, scale=1.0 / D) \
                        .then_inc(xstd_ready, 1)
                    for k in range(KT):
                        act.wait_ge(t_ready, KT * r + k + 1)
                        shift = mods[:, shift_at(sub) + k:shift_at(sub) + k + 1]
                        nc.scalar.activation(a_hi[:, k, :], tmp[:, k, :], ACT.Identity, bias=shift).then_inc(h_hi, 1)
                        if mixer:
                            nc.scalar.activation(h32[:, k, :], tmp[:, k, :], ACT.Identity, bias=shift) \
                                .then_inc(h_f32, 1)

                def silu(f, n0, i):
                    act.wait_ge(panel_used[G], CREDIT + USES * l + (n0 + 1) + i)
                    act.wait_ge(glu_ready, CREDIT + f + i)
                    nc.scalar.activation(silu_g, ps[:, BK_GATE, :], ACT.Silu).then_inc(silu_ready, 1)

                def high_u(f, n0, i):
                    act.wait_ge(glu_ready, CREDIT + f + i + 1)
                    act.wait_ge(panel_used[DN], CREDIT + USES * l + n0 + i)
                    nc.scalar.activation(u_hi[:].rearrange("p k s -> p (k s)"), glu, ACT.Copy).then_inc(u_hi_ready, 1)

                def ffn(ffn_, n0):
                    f = l * (2 * NF) + ffn_ * NF
                    silu(f, n0, 0)
                    split(G, l, n0 + 1)
                    with act.Fori(0, NF - 1) as i:
                        split(DN, l, n0 + i)
                        high_u(f, n0, i)
                        split(U, l, n0 + 1 + i)
                        silu(f, n0, i + 1)
                        split(G, l, n0 + 2 + i)
                    split(DN, l, n0 + NF - 1)
                    high_u(f, n0, NF - 1)
                    split(U, l, n0 + NF)

                pre(0, False)
                ffn(0, 0)
                post(0)
                split_aq(l)
                pre(1, True)

                def evac(m, dst, func=ACT.Copy, scale=1.0, bank=None, view=None):
                    mix_used(act, l, m)
                    src = ps[:, BK_GATE + m % 2, :] if view is None else view
                    nc.scalar.activation(dst, src, func, scale=scale).then_inc(proj_read, 1)

                def next_split(m):
                    split(m % 3, l, MIX0 + m // 3)

                act.wait_ge(bias_ready, AG * (NCH + 1))
                evac(0, qT.rearrange("p k s -> p (k s)"))
                next_split(3)
                act.wait_ge(gates_done, CREDIT + l + 1)
                nc.scalar.activation(th[:], ps[0:2 * MH, BK_B, 0:S], ACT.Tanh, bias=gb15[:, bass.ds(l, 1)],
                                     scale=1.0 / CAP).then_inc(th_ready, 1)
                act.wait_ge(th_ready, l + 1)
                nc.scalar.activation(sp[:], th[:], ACT.Exp, scale=-CAP).then_inc(ez_ready, 1)
                act.wait_ge(ez_ready, l + 1)
                nc.scalar.activation(sp2[:], sp[:], ACT.Ln, bias=1.0).then_inc(sp_ready, 1)
                evac(1, kT.rearrange("p k s -> p (k s)"))
                next_split(4)
                evac(2, aqT[:].rearrange("p k s -> p (k s)"))
                next_split(5)
                mix_used(act, l, 3)
                nc.scalar.activation(avT, ps[:, BK_UP, S:2 * S], ACT.Copy)
                evac(3, akT[:], view=ps[:, BK_UP, 0:S])

                def floor_of(h):
                    act.wait_ge(decay_done, MH * l + h + 1)
                    act.wait_ge(hm_link, CREDIT + (MH * l + h))
                    nc.scalar.activation(floor[:], ps[:, 2, S:2 * S], ACT.Exp).then_inc(floor_ready, 1)

                def decay(h):
                    act.wait_ge(cap_ready, CREDIT + 2 * (MH * l + h + 1))
                    nc.scalar.activation(edec[:], ecap[:], ACT.Exp).then_inc(dec_ready, 1)

                def square_head(h):
                    act.wait_ge(hm_ready, CREDIT + MH * l + h + 1)
                    nc.scalar.activation(sq[:, h, :], hm[:, h, :], ACT.Square)
                    nc.scalar.activation(qe[h], qden[:, h % 2, :], ACT.Square, scale=EPS ** 0.5).then_inc(hmsq_ready, 1)

                def std_heads(b):
                    act.wait_ge(hmsum_done, 2 * l + b + 1)
                    nc.scalar.activation(tmp[:, 2 * b:2 * b + 2, :].rearrange("p k s -> p (k s)"), ps[:, b, :],
                                         ACT.Sqrt, scale=1.0 / DV).then_inc(hmstd_ready, 1)

                def high_mix(n, k0):
                    act.wait_ge(mix_f32, 4 * l + n + 1)
                    nc.scalar.activation(mix_tile("hi", k0), h32[:, k0:k0 + 2, :], ACT.Copy).then_inc(mix_hi, 1)

                floor_of(0)
                next_split(6)
                decay(0)
                evac(4, vm[:, :, 0:PC], view=ps[:, BK_GATE, :].rearrange("p (t d) -> p t d", t=2))
                act.wait_ge(av_turned, l + 1)
                nc.scalar.activation(av[:].rearrange("p w d -> p (w d)"), ps[:, BK_A, 0:3 * P], ACT.Copy) \
                    .then_inc(av_ready, 1)
                floor_of(1)
                next_split(7)
                decay(1)
                act.wait_ge(smax_ready, l + 1)
                for r in range(AG * NCH):
                    nc.scalar.activation(sc[:, r, :], sc[:, r, :], ACT.Exp, bias=mx[:, 2, r:r + 1],
                                         accum_out=sums[:, 0, r:r + 1]).then_inc(probs_exp, 1)
                nc.scalar.activation(sums[:, 1, :], mx[:, 1, :], ACT.Exp).then_inc(sink_exp, 1)
                square_head(0)
                evac(5, vm[:, :, PC:2 * PC], view=ps[:, BK_UP, :].rearrange("p (t d) -> p t d", t=2))
                floor_of(2)
                next_split(8)
                decay(2)
                square_head(1)
                evac(6, cc_s.rearrange("p k s -> p (k s)"))
                floor_of(3)
                next_split(9)
                decay(3)
                square_head(2)
                for b in range(2):
                    act.wait_ge(probs_turned, 2 * l + b + 1)
                    nc.scalar.activation(pT[:, 4 * b:4 * b + 4, :].rearrange("p r q -> p (r q)"), ps[:, b, :], ACT.Copy) \
                        .then_inc(pT_ready, 1)
                next_split(10)
                square_head(3)
                std_heads(0)
                high_mix(0, 6)
                next_split(11)
                high_mix(1, 4)
                std_heads(1)
                evac(9, th_o[:, 0:2, :].rearrange("p k s -> p (k s)"), ACT.Tanh, 0.5)
                next_split(12)
                high_mix(2, 0)
                evac(10, th_o[:, 2:4, :].rearrange("p k s -> p (k s)"), ACT.Tanh, 0.5)
                high_mix(3, 2)
                next_split(13)
                post(1)
                pre(2, False)
                ffn(1, FFB0)
                post(2)

            act.wait_ge(o_scale_ready, 1)
            for n in range(3):
                act.wait_ge(o_turned, n // 2 + 1)
                nc.scalar.activation(o_rows[n], ps[:, BK_OUT[n], :], ACT.Copy, scale=o_scale[:, n % 2:n % 2 + 1]).then_inc(o_ready, 1)

        @block.vector
        def _(dve):
            def split(s, l, n):
                dve.wait_ge(hi_ready[s], USES * l + n + 1)
                nc.vector.tensor_tensor(lo[s][:], raw[s][:], hi[s][:].bitcast(F32), ALU.subtract) \
                    .then_inc(lo_ready[s], 1)

            def split_aq(l):
                dve.wait_ge(hi_ready[2], USES * l + MIX0 + 1)
                for g in range(AG):
                    last = nc.vector.tensor_tensor(by_group(lo, g, True), by_group(raw, g, False),
                                                   by_group(hi, g, True).bitcast(F32), ALU.subtract)
                last.then_inc(lo_ready[2], 1)

            def ada_unit(s, blk, free_at, total, part=None):
                if part != 1:
                    dve.wait_ge(ada_loaded[s], 16 * (blk - PRO_BLK + 1))
                for k in range(0 if part is None else part * UK // 2, UK if part is None else (part + 1) * UK // 2):
                    c1 = c_col[:, s * UK + k:s * UK + k + 1]
                    if s == 0 and k == 0:
                        dve.wait_ge(ada_turned, CREDIT + free_at)
                        step = nc.vector.tensor_scalar(total, ada_raw[s][:, k, :], c1, None, ALU.mult)
                    else:
                        dve.wait_ge(ada_steps, steps(blk, s, k))
                        step = nc.vector.scalar_tensor_tensor(total, ada_raw[s][:, k, :], c1, total, ALU.mult, ALU.add)
                    step.then_inc(ada_steps, 1)

            def pro_unit(s, blk, acc):
                i = (2 * blk + s) % 4
                dve.wait_ge(pro_loaded[i], 16 * (blk // 2 + 1))
                for k in range(UK):
                    c1 = c_col[:, s * UK + k:s * UK + k + 1]
                    total = ada_acc[:, acc, :]
                    if s == 0 and k == 0:
                        if acc == 0:
                            dve.wait_ge(ada_turned, CREDIT + blk)
                        step = nc.vector.tensor_scalar(total, pro_raw[i][:, k, :], c1, None, ALU.mult)
                    else:
                        dve.wait_ge(ada_steps, steps(blk, s, k))
                        step = nc.vector.scalar_tensor_tensor(total, pro_raw[i][:, k, :], c1, total, ALU.mult, ALU.add)
                    step.then_inc(ada_steps, 1)

            def ada_mods(blk, bank, at, col, b_col, n=1):
                dve.wait_ge(ada_turned, CREDIT + blk + n)
                nc.vector.tensor_tensor(mods[:, col:col + n * UT], ps[:, bank, at:at + n * UT],
                                        adab[:, bass.ds(b_col, n * UT)], ALU.add).then_inc(mods_ready, n)

            dve.sem_inc(ada_steps, 2 * UK)
            for signal in (*lo_ready, mods_ready, glu_ready, u_lo_ready, post_link, hm_link, cap_ready,
                           pm_ready, hm_ready):
                dve.sem_inc(signal, CREDIT)
            for g in range(3):
                dve.wait_ge(cols_turned, g + 1)
                n = 28 if g == 2 else 120
                nc.vector.tensor_copy(cols[:, g * P:g * P + n], ps[:, g, 0:n]).then_inc(cols_ready, 1)
            dve.wait_ge(cols_ready, 3)
            for b in range(DEPTH + 1):
                src = cols[:, (b % DEPTH) * P:(b % DEPTH) * P + 72]
                nc.vector.tensor_copy(adab[:, 72 * b:72 * b + 72], src).then_inc(prep, 1)
            nc.vector.tensor_scalar(half_gain[:], cols[:, HEAD:HEAD + DEPTH * MH], 0.5, None, ALU.mult).then_inc(prep, 1)
            dve.wait_ge(prep, DEPTH + 2)
            dve.wait_ge(silu_c_ready, 1)
            for b in range(PRO_BLK):
                acc = 0 if b < PRO_BLK - 1 else THIRD - 1
                pro_unit(0, b, acc)
                pro_unit(1, b, acc)
                if b == PRO_BLK - 2:
                    dve.wait_ge(t_rows, 1)
                    nc.vector.tensor_copy(trow, ps[:, 4, 0:AG * 3 * CHUNK].rearrange("p (g r) -> p g r", g=AG)) \
                        .then_inc(t_rows_out, 1)
                if b == PRO_BLK - 2:
                    split(G, 0, 0)
                if b < PRO_BLK - 1:
                    ada_mods(b, BK_A, 0, WRAP + UT * b, UT * b)
            dve.wait_ge(small_in, 64)
            nc.vector.tensor_scalar(gb15[:], gb[:], 1.0 / CAP, None, ALU.mult).then_inc(prep, 1)

            with dve.Fori(0, DEPTH) as l:
                def third_mods(third, b, bank=BK_A, at=0, n=1):
                    ada_mods(block_no(l, third, b), bank, at, mod_col(third, b), MCOLS * l + mod_col(third, b), n)

                def post_gain(sub, w):
                    r = 3 * l + sub
                    gate = mods[:, (3 * sub + 2) * KT:(3 * sub + 3) * KT]
                    gp = cols[:, bass.ds(P + 72 + (3 * l + sub) * KT, KT)]
                    dve.wait_ge(mods_ready, CREDIT + block_no(l, sub, 2))
                    nc.vector.scalar_tensor_tensor(mod_c[:], gate, 1.0, gp, ALU.add, ALU.mult).then_inc(pre_link, 1)
                    dve.wait_ge(pre_link, 3 * r + 2)
                    nc.vector.tensor_scalar(mod_c[:], mod_c[:], w, None, ALU.mult).then_inc(pre_link, 1)

                def post(sub):
                    r = 3 * l + sub
                    dve.wait_ge(ystd_ready, r + 1)
                    dve.wait_ge(post_link, CREDIT + r)
                    nc.vector.tensor_tensor(rstd[:], inv[:], std[:], ALU.mult).then_inc(q_ready, 1)
                    dve.wait_ge(q_ready, r + 1)

                    def rescale(b):
                        two = xT[:, 2 * b:2 * b + 2, :]
                        nc.vector.tensor_tensor(two, two, rstd[:].rearrange("p (o s) -> p o s", o=1)
                                                .to_broadcast([P, 2, S]), ALU.mult).then_inc(z_scaled, 1)

                    rescale(0)
                    for b in range(4):
                        if b < 3:
                            rescale(b + 1)
                        dve.wait_ge(z_scaled, 4 * r + b + 1)
                        dve.wait_ge(y_gained, 8 * r + 2 * b + 2)
                        nc.vector.tensor_tensor(xT[:, 2 * b:2 * b + 2, :], xT[:, 2 * b:2 * b + 2, :],
                                                tmp[:, 2 * b:2 * b + 2, :], ALU.add).then_inc(x_tile, 1)
                    nc.vector.reciprocal(inv[:], std[:]).then_inc(post_link, 1)
                    if sub != 1:
                        third_mods(sub, IN_FFN, BK_GATE, n=THIRD - IN_FFN - sub // 2)

                def pre(sub):
                    r = 3 * l + sub
                    gp = cols[:, bass.ds(72 + (3 * l + sub) * KT, KT)]
                    scale = mods[:, shift_at(sub) + KT:shift_at(sub) + 2 * KT]
                    if sub > 0:
                        dve.wait_ge(mods_ready, CREDIT + block_no(l, sub))
                        nc.vector.scalar_tensor_tensor(mod_a[:], scale, 1.0, gp, ALU.add, ALU.mult).then_inc(pre_link, 1)
                    dve.wait_ge(xstd_ready, r + 1)
                    nc.vector.reciprocal(rstd[:], std[:]).then_inc(rx_ready, 1)
                    if sub == 0:
                        col = (PRO_BLK - 1) * UT
                        ada_mods(block_no(l, 0) - 1, BK_A, 0, WRAP + col, MCOLS * l + col)
                        dve.wait_ge(mods_ready, CREDIT + block_no(l, sub))
                        nc.vector.scalar_tensor_tensor(mod_a[:], scale, 1.0, gp, ALU.add, ALU.mult).then_inc(pre_link, 1)
                    dve.wait_ge(rx_ready, r + 1)
                    dve.wait_ge(pre_link, 3 * r + 1)
                    def low(k):
                        shift = mods[:, shift_at(sub) + k:shift_at(sub) + k + 1]
                        dve.wait_ge(h_hi, KT * r + k + 1)
                        nc.vector.scalar_tensor_tensor(a_lo[:, k, :], tmp[:, k, :], shift,
                                                       a_hi[:, k, :].bitcast(F32), ALU.add, ALU.subtract) \
                            .then_inc(h_lo, 1)
                    for k in range(KT):
                        nc.vector.scalar_tensor_tensor(tmp[:, k, :], xT[:, k, :], mod_a[:, k:k + 1], rstd[:],
                                                       ALU.mult, ALU.mult).then_inc(t_ready, 1)
                        if k >= 2:
                            low(k - 2)
                    low(KT - 2)
                    low(KT - 1)

                def mult_up(f, n0, i):
                    dve.wait_ge(panel_used[U], CREDIT + USES * l + (n0 + 1) + i)
                    dve.wait_ge(silu_ready, CREDIT + f + i + 1)
                    dve.wait_ge(u_lo_ready, CREDIT + f + i)
                    nc.vector.tensor_tensor(glu, ps[:, BK_UP, :], silu_g, ALU.mult).then_inc(glu_ready, 1)

                def low_u(f, i):
                    dve.wait_ge(u_hi_ready, f + i + 1)
                    nc.vector.tensor_tensor(u_lo[:].rearrange("p k s -> p (k s)"), glu,
                                            u_hi[:].bitcast(F32).rearrange("p k s -> p (k s)"), ALU.subtract) \
                        .then_inc(u_lo_ready, 1)

                def ffn(ffn_, n0, third):
                    f = l * (2 * NF) + ffn_ * NF
                    all_read = block_no(l, third)
                    for s in range(2):
                        ada_unit(s, block_no(l, third), all_read, ada_acc[:, 0, :])
                    split(G, l, n0 + 1)
                    with dve.Fori(0, (NF - 1) // 2) as j:
                        total = ada_acc[:, bass.ds(1 + j, 1), :].rearrange("p b n -> p (b n)")
                        for step in range(2):
                            i = 2 * j + step
                            blk = block_no(l, third, 1 + j)
                            if step == 1:
                                ada_unit(1, blk, all_read, total, 0)
                            split(DN, l, n0 + i)
                            mult_up(f, n0, i)
                            low_u(f, i)
                            split(U, l, n0 + 1 + i)
                            if step == 0:
                                ada_unit(0, blk, all_read, total)
                            else:
                                ada_unit(1, blk, all_read, total, 1)
                            split(G, l, n0 + 2 + i)
                    split(DN, l, n0 + NF - 1)
                    mult_up(f, n0, NF - 1)
                    low_u(f, NF - 1)
                    third_mods(third, 0, n=IN_FFN)
                    post_gain(third, 0.5)
                    split(U, l, n0 + NF)

                pre(0)

                def mixer_ada(u):
                    b = u // 2
                    ada_unit(u % 2, block_no(l, 1, b), block_no(l, 0, 2) if b < 2 else block_no(l, 1, b - 1),
                             ada_acc[:, b % 2, :])

                def mixer_mods(b, bank):
                    third_mods(1, b, bank, TURN_AT if bank == 3 else 0)

                ffn(0, 0, 0)
                mixer_ada(0)
                mixer_ada(1)
                post(0)
                split_aq(l)
                pre(1)

                def next_split(m):
                    split(m % 3, l, MIX0 + m // 3)

                next_split(3)
                dve.wait_ge(sp_ready, l + 1)
                nc.vector.tensor_tensor_scan(gsum[:], ones[0:2 * MH, :], sp2[:], 0.0, ALU.mult, ALU.subtract) \
                    .then_inc(g_ready, 1)
                mixer_ada(2)
                next_split(4)
                mixer_ada(3)
                mixer_mods(0, BK_A)
                for g in range(AG):
                    nc.vector.tensor_copy(sink8[:, g, :], sink[:, bass.ds(l, 1), g:g + 1]
                                          .rearrange("p a b -> p (a b)").to_broadcast([P, NCH])).then_inc(s_link, 1)
                dve.wait_ge(a_done, l + 1)
                nc.vector.tensor_copy(arow[:], ps[0:MH, BK_B, 0:S]).then_inc(arow_ready, 1)
                nc.vector.tensor_copy(acol[:].rearrange("p t h -> p (t h)"), ps[:, BK_B, S:S + 2 * MH]) \
                    .then_inc(arow_ready, 1)
                dve.wait_ge(arow_ready, 2 * l + 2)
                nc.vector.tensor_tensor_scan(mrow[:], arow[:], arow[:], MASKED, ALU.max, ALU.max).then_inc(m_ready, 1)
                next_split(5)
                mixer_ada(4)
                mixer_ada(5)

                def decay(h):
                    dve.wait_ge(floor_ready, CREDIT + MH * l + h + 1)
                    dve.wait_ge(dec_ready, CREDIT + MH * l + h)
                    cap = cst[:, C_CAP:C_CAP + S]
                    nc.vector.scalar_tensor_tensor(ecap[:, 0:S], ps[:, 2, 0:S], acol[:, 0, h:h + 1], cap,
                                                   ALU.add, ALU.min).then_inc(cap_ready, 1)
                    nc.vector.scalar_tensor_tensor(ecap[:, S:S + P], ps[:, 2, P:S], acol[:, 1, h:h + 1], cap[:, 0:P],
                                                   ALU.add, ALU.min).then_inc(cap_ready, 1)

                def weigh(h, blk=None):
                    dve.wait_ge(dec_ready, CREDIT + MH * l + h + 1)
                    dve.wait_ge(qk_done, MH * l + h + 1)
                    if blk is not None:
                        mixer_mods(blk, 3)
                    dve.wait_ge(num_done, CREDIT + MH * l + h)
                    nc.vector.scalar_tensor_tensor(pm[:], ps[:, 3, 0:3 * P], DQK ** -0.5, edec[:], ALU.mult, ALU.mult) \
                        .then_inc(pm_ready, 1)

                def head_out(h):
                    n = MH * l + h
                    dve.wait_ge(num_done, CREDIT + n + 1)
                    dve.wait_ge(floor_ready, CREDIT + n + 1)
                    if h >= 2:
                        dve.wait_ge(hmsq_ready, CREDIT + n - 1)
                    den = ps[:, BK_B, S:2 * S]
                    nc.vector.scalar_tensor_tensor(dd[:], den, -1.0, floor[:], ALU.mult, ALU.max).then_inc(hm_link, 1)
                    nc.vector.tensor_copy(hm[:, h, :], ps[:, BK_B, 0:S])
                    dve.wait_ge(hm_link, CREDIT + n + 1)
                    nc.vector.tensor_tensor(qden[:, h % 2, :], dd[:], den, ALU.max).then_inc(hm_ready, 1)

                def tap(t, k):
                    return cols[:, bass.ds(CONV + 6 * l + 2 * t + k, 1)]

                def conv():
                    dve.wait_ge(proj_read, N_READ * l + 7)
                    mix_used(dve, l, 7)
                    nc.vector.tensor_tensor(up_s[:, :, 2:], ps[:, BK_UP, :].rearrange("p (k s) -> p k s", k=2), cc_s,
                                            ALU.mult).then_inc(proj_read, 1)
                    dve.wait_ge(proj_read, N_READ * l + 8)
                    for k in range(2):
                        nc.vector.tensor_scalar(yc[:, k, :], up_s[:, k, 0:S], tap(0, k), None, ALU.mult) \
                            .then_inc(conv_link, 1)
                    for t in (1, 2):
                        for k in range(2):
                            dve.wait_ge(conv_link, 6 * l + 2 * (t - 1) + k + 1)
                            nc.vector.scalar_tensor_tensor(yc[:, k, :], up_s[:, k, t:t + S], tap(t, k), yc[:, k, :],
                                                           ALU.mult, ALU.add).then_inc(conv_link, 1)

                def low_mix(n, k0):
                    dve.wait_ge(mix_hi, 4 * l + n + 1)
                    nc.vector.tensor_tensor(mix_tile("lo", k0), h32[:, k0:k0 + 2, :],
                                            mix_tile("hi", k0).bitcast(F32), ALU.subtract).then_inc(mix_lo, 1)

                def norm_heads(b):
                    sl = slice(2 * b, 2 * b + 2)
                    dve.wait_ge(hmstd_ready, 2 * l + b + 1)
                    nc.vector.reciprocal(tmp[:, sl, :], tmp[:, sl, :]).then_inc(out_link, 1)
                    dve.wait_ge(out_link, 6 * l + 3 * b + 1)
                    for h in (2 * b, 2 * b + 1):
                        nc.vector.scalar_tensor_tensor(hm[:, h, :], hm[:, h, :], half_gain[:, bass.ds(MH * l + h, 1)],
                                                       tmp[:, h, :], ALU.mult, ALU.mult).then_inc(out_link, 1)

                def gate_heads(b):
                    sl = slice(2 * b, 2 * b + 2)
                    dve.wait_ge(proj_read, N_READ * l + 9 + b)
                    dve.wait_ge(out_link, 6 * l + 3 * b + 3)
                    nc.vector.scalar_tensor_tensor(h32[:, sl, :], th_o[:, sl, :], 1.0, hm[:, sl, :], ALU.add, ALU.mult) \
                        .then_inc(mix_f32, 1)

                def score_rows():
                    dve.wait_ge(bias_ready, AG * (NCH + 1))
                    dve.wait_ge(scores_done, l + 1)
                    for g in range(AG):
                        nc.vector.scalar_tensor_tensor(
                            sc[:, g * NCH:(g + 1) * NCH, :].rearrange("p j k -> p (j k)"), ps[:, g, :], DH ** -0.5,
                            bias[:, g, :, :].rearrange("p j k -> p (j k)"), ALU.mult, ALU.add).then_inc(s_link, 1)
                    base = 6 * l + 4
                    dve.wait_ge(s_link, base)
                    nc.vector.tensor_reduce(mx[:, 0, :], sc, AX_X, ALU.max).then_inc(s_link, 1)
                    dve.wait_ge(s_link, base + 1)
                    sk = sink8[:].rearrange("p g j -> p (g j)")
                    nc.vector.tensor_tensor(mx[:, 0, :], mx[:, 0, :], sk, ALU.max).then_inc(s_link, 1)
                    dve.wait_ge(s_link, base + 2)
                    nc.vector.tensor_tensor(mx[:, 1, :], sk, mx[:, 0, :], ALU.subtract).then_inc(sm_link, 1)
                    nc.vector.tensor_scalar(mx[:, 2, :], mx[:, 0, :], -1.0, None, ALU.mult).then_inc(smax_ready, 1)

                def norm_probs():
                    dve.wait_ge(probs_exp, AG * NCH * (l + 1))
                    dve.wait_ge(sink_exp, l + 1)
                    nc.vector.tensor_tensor(sums[:, 2, :], sums[:, 0, :], sums[:, 1, :], ALU.add).then_inc(pr_link, 1)
                    dve.wait_ge(pr_link, 2 * l + 1)
                    nc.vector.reciprocal(sums[:, 3, :], sums[:, 2, :]).then_inc(pr_link, 1)
                    dve.wait_ge(pr_link, 2 * l + 2)
                    nc.vector.tensor_tensor(sc, sc, sums[:, 3, :].rearrange("p (r o) -> p r o", o=1)
                                            .to_broadcast([P, AG * NCH, P]), ALU.mult).then_inc(probs_ready, 1)

                decay(0)
                next_split(6)
                weigh(0, 1)
                mixer_ada(6)
                score_rows()
                head_out(0)
                decay(1)
                next_split(7)
                weigh(1, 2)
                mixer_ada(7)
                head_out(1)
                decay(2)
                next_split(8)
                weigh(2)
                norm_probs()
                mixer_ada(8)
                head_out(2)
                decay(3)
                next_split(9)
                weigh(3, 3)
                mixer_ada(9)
                conv()
                head_out(3)
                next_split(10)
                dve.wait_ge(attn_done, l + 1)
                nc.vector.tensor_copy(h32[:, 6:8, :].rearrange("p k s -> p (k s)"), ps[:, BK_A, :]) \
                    .then_inc(mix_f32, 1)
                norm_heads(0)
                low_mix(0, 6)
                mix_used(dve, l, 8)
                dve.wait_ge(conv_link, 6 * l + 6)
                nc.vector.tensor_tensor(h32[:, 4:6, :].rearrange("p k s -> p (k s)"), ps[:, BK_GATE, :],
                                        yc.rearrange("p k s -> p (k s)"), ALU.mult).then_inc(mix_f32, 1)
                next_split(11)
                low_mix(1, 4)
                norm_heads(1)
                gate_heads(0)
                mixer_mods(4, BK_A)
                next_split(12)
                low_mix(2, 0)
                mixer_ada(10)
                gate_heads(1)
                low_mix(3, 2)
                post_gain(1, 1.0)
                next_split(13)
                next_split(14)
                mixer_ada(11)
                next_split(15)
                mixer_mods(THIRD - 1, BK_GATE)
                next_split(16)
                post(1)
                pre(2)
                ffn(1, FFB0, 2)
                post(2)

            dve.wait_ge(o_std_turned, 1)
            nc.vector.reciprocal(o_scale[:], ps[:, BK_UP, 0:2 * P].rearrange("p (t s) -> p t s", t=2)[:, :, 0:1]
                                 .rearrange("p t s -> p (t s)")).then_inc(o_scale_ready, 1)
            dve.wait_ge(o_scale_ready, 1)
            dve.wait_ge(o_turned, 2)
            nc.vector.tensor_scalar(o_rows[3], ps[:, BK_OUT[3], :], o_scale[:, 1:2], None, ALU.mult).then_inc(o_last_ready, 1)

        @block.tensor
        def _(pe):
            def take(s, l, n):
                pe.wait_ge(lo_ready[s], CREDIT + USES * l + n + 1)

            def product(dst, w_hi, w_lo, b_hi, b_lo, first, last):
                nc.tensor.matmul(dst, w_hi, b_hi, start=first, stop=False, skip_group_check=True)
                nc.tensor.matmul(dst, w_hi, b_lo, start=False, stop=False, skip_group_check=True)
                return nc.tensor.matmul(dst, w_lo, b_hi, start=False, stop=last, skip_group_check=True)

            def keep_warm(n, bank=BK_UP):
                for _ in range(n):
                    nc.tensor.matmul(ps[:, bank, 0:S], ones[:, 0:P], ones[:], start=True, stop=True)

            def ada_turn(blk, bank=BK_A, at=0, acc=0):
                pe.wait_ge(ada_steps, steps(blk, 1, UK))
                if bank != BK_GATE:
                    pe.wait_ge(mods_ready, CREDIT + blk - (at // UT if bank == BK_A else 0))
                for j in range(UT):
                    last = nc.tensor.matmul(ps[:, bank, at + j:at + j + 1], ada_acc[:, acc, j * P:(j + 1) * P],
                                            ones[:, 0:1], start=True, stop=True)
                last.then_inc(ada_turned, 1)

            for signal in (*panel_used, ada_turned, gates_done, ysum_ready, num_done):
                pe.sem_inc(signal, CREDIT)
            pe.wait_ge(consts_in, 32)
            pe.wait_ge(c_in, 7 * 16)
            for g in range(3):
                n = 28 if g == 2 else 120
                nc.tensor.transpose(ps[:, g, 0:n], rows[0:n, g, :], ident[0:n, 0:n]).then_inc(cols_turned, 1)
            pe.wait_ge(ones_set, 6)
            pe.wait_ge(tabx_ready, 4)
            for g in range(AG):
                last = nc.tensor.matmul(ps[:, 4, g * 192:(g + 1) * 192],
                                        tabx[:, g, :, :].rearrange("b k q -> b (k q)"),
                                        cst[0:N_BUCKETS, C_HOT:C_HOT + 192], start=True, stop=True)
            last.then_inc(t_rows, 1)
            for b in range(PRO_BLK - 1):
                if b > 0:
                    keep_warm(WARM_PRE)
                ada_turn(b)
                if b == 0:
                    pe.wait_ge(x_in, 16)
                    pe.wait_ge(cols_ready, 3)
                    xt = tmp[:].rearrange("p k s -> p (k s)").rearrange("p (t d) -> p t d", t=2)
                    for k in range(KT):
                        for t in range(2):
                            last = nc.tensor.transpose(ps[:, k // 2, (k % 2) * S + t * P:(k % 2) * S + (t + 1) * P],
                                                       xt[:, t, k * P:(k + 1) * P], ident)
                        if k % 2:
                            last.then_inc(x_turned, 1)
            pe.wait_ge(t_rows_out, 1)

            with pe.Fori(0, DEPTH) as l:
                def sum_bank(bank, ready, n0, b, done=None):
                    pe.wait_ge(ready, n0 + b + 1)
                    for k in (2 * b, 2 * b + 1):
                        last = nc.tensor.matmul(ps[:, bank, 0:S], ones[:, 0:P], sq[:, k, :], start=(k == 0 and bank == BK_Y),
                                                stop=(k == KT - 1), skip_group_check=True)
                    if done is not None:
                        last.then_inc(done, 1)

                def pre(sub):
                    r = 3 * l + sub
                    pe.wait_ge(e_ready, CREDIT + r)
                    nc.tensor.matmul(ps[:, BK_X, 0:S], ones[:, 0:P], eps_std[:], start=True, stop=False,
                                     skip_group_check=True)
                    for b in range(4):
                        sum_bank(BK_X, xsq_ready, 4 * r, b, xsum_ready if b == 3 else None)
                    if sub == 0:
                        ada_turn(block_no(l, 0) - 1, BK_A, 0, THIRD - 1)
                    keep_warm(WARM_PRE)

                def post(sub):
                    r = 3 * l + sub
                    sum_bank(BK_Y, ysq_ready, 4 * r, 3, ysum_ready)
                    if sub != 1:
                        keep_warm(1)
                        for b in range(IN_FFN, THIRD if sub == 0 else THIRD - 1):
                            ada_turn(block_no(l, sub, b), BK_GATE, (b - IN_FFN) * UT, b)
                            keep_warm(2)
                    keep_warm(WARM_POST if sub == 1 else 0)

                def first_panel(bank, s, sub):
                    r = 3 * l + sub
                    pe.wait_ge(mods_ready, CREDIT + block_no(l, sub))
                    nc.tensor.matmul(ps[:, bank, 0:1], zeros[:], ones[:, 0:1], start=True, stop=False,
                                     skip_group_check=True)
                    for k in range(KT):
                        pe.wait_ge(h_lo, KT * r + k + 1)
                        for j in range(2):
                            last = product(ps[:, bank, j * S:(j + 1) * S], panel(hi, s)[:, k, j * P:(j + 1) * P],
                                           panel(lo, s)[:, k, j * P:(j + 1) * P], a_hi[:, k, :], a_lo[:, k, :],
                                           False, k == KT - 1)
                    return last

                def wide_tile(bank, s, j):
                    for k in range(KT):
                        last = product(ps[:, bank, j * S:(j + 1) * S], panel(hi, s)[:, k, j * P:(j + 1) * P],
                                       panel(lo, s)[:, k, j * P:(j + 1) * P], a_hi[:, k, :], a_lo[:, k, :],
                                       k == 0, k == KT - 1)
                    return last

                def gate(f, n0, i, sub=None):
                    take(G, l, n0 + i)
                    pe.wait_ge(silu_ready, CREDIT + f + i)
                    if sub is not None:
                        last = first_panel(BK_GATE, G, sub)
                    else:
                        for j in range(2):
                            last = wide_tile(BK_GATE, G, j)
                    last.then_inc(panel_used[G], 1)

                def up(f, n0, i):
                    take(U, l, n0 + i)
                    pe.wait_ge(glu_ready, CREDIT + f + i)
                    for j in range(2):
                        last = wide_tile(BK_UP, U, j)
                    last.then_inc(panel_used[U], 1)

                def down(f, n0, i, final, sub=None):
                    take(DN, l, n0 + i)
                    pe.wait_ge(u_lo_ready, CREDIT + f + i + 1)
                    for m in range(KT):
                        for a in range(2):
                            last = product(ps[:, m // 2, (m % 2) * S:(m % 2 + 1) * S],
                                           rowpanel(hi, DN)[:, a, m * P:(m + 1) * P],
                                           rowpanel(lo, DN)[:, a, m * P:(m + 1) * P],
                                           u_hi[:, a, :], u_lo[:, a, :], False, final and a == 1)
                        if final and m in (1, 3, 5):
                            last.then_inc(y_done, 1)
                        if m == KT - 1:
                            last.then_inc(panel_used[DN], 1)
                        if final and m == 5:
                            pe.wait_ge(mods_ready, CREDIT + block_no(l, sub, IN_FFN))
                        if final and m >= 5:
                            sum_bank(BK_Y, ysq_ready, 4 * (3 * l + sub), m - 5)

                def ffn(n0, third, sub):
                    f = l * (2 * NF) + (0 if third == 0 else NF)
                    gate(f, n0, 0, sub)
                    for b in range(4):
                        nc.tensor.matmul(ps[:, b, 0:1], zeros[:], ones[:, 0:1], start=True, stop=False,
                                         skip_group_check=True)
                    with pe.Fori(0, (NF - 1) // 2) as j:
                        for step in range(2):
                            i = 2 * j + step
                            up(f, n0, i)
                            gate(f, n0, i + 1)
                            down(f, n0, i, False)
                    for b in range(IN_FFN):
                        if b == IN_FFN - BRIDGE:
                            up(f, n0, NF - 1)
                        else:
                            keep_warm(1, BK_X)
                        ada_turn(block_no(l, third, b), BK_A, b * UT, b)
                    down(f, n0, NF - 1, True, sub)

                def mix_take(m):
                    take(m % 3, l, MIX0 + m // 3)
                    if m >= 2:
                        pe.wait_ge(proj_read, N_READ * l + min(m - 1, 8))
                    if m == 10:
                        pe.wait_ge(mix_f32, 4 * l + 2)

                def mix_release(m, last):
                    last.then_inc(panel_used[m % 3], 1)

                def project(m, sub=None):
                    mix_take(m)
                    if sub is not None:
                        last = first_panel(BK_GATE + m % 2, m % 3, sub)
                    else:
                        for j in range(2):
                            last = wide_tile(BK_GATE + m % 2, m % 3, j)
                    mix_release(m, last)

                def project_tokens(m):
                    mix_take(m)
                    for t in range(2):
                        for k in range(KT):
                            tok = slice(t * P, (t + 1) * P)
                            last = product(ps[:, BK_GATE + m % 2, t * PC:(t + 1) * PC], a_hi[:, k, tok], a_lo[:, k, tok],
                                           panel(hi, m % 3)[:, k, :], panel(lo, m % 3)[:, k, :], k == 0, k == KT - 1)
                    mix_release(m, last)

                def gates():
                    pe.wait_ge(wg_in, 16 * (l + 1))
                    for k in range(KT):
                        pe.wait_ge(h_f32, KT * l + k + 1)
                        last = nc.tensor.matmul(ps[0:2 * MH, BK_B, 0:S], wg[:, k, :], h32[:, k, :], start=(k == 0),
                                                stop=(k == KT - 1))
                    last.then_inc(gates_done, 1)

                def project_aq():
                    mix_take(2)
                    for g in range(AG):
                        for k in range(KT):
                            w = [panel(t, 2)[:, k, g * P:(g + 1) * P] for t in (hi, lo)]
                            last = product(ps[:, BK_GATE, g * S:(g + 1) * S], w[0], w[1], a_hi[:, k, :], a_lo[:, k, :],
                                           k == 0, k == KT - 1)
                    mix_release(2, last)

                def turn_values():
                    for w in range(3):
                        last = nc.tensor.transpose(ps[:, BK_A, w * P:(w + 1) * P], avT[:, w * CHUNK:w * CHUNK + P], ident)
                    last.then_inc(av_turned, 1)

                def log_weights():
                    pe.wait_ge(g_ready, l + 1)
                    sel_i, sel_f = cst[0:2 * MH, C_SELI:C_SELI + MH], cst[0:2 * MH, C_SELF:C_SELF + MH]
                    for t in range(2):
                        o = ps[:, BK_B, S + t * MH:S + (t + 1) * MH]
                        nc.tensor.matmul(o, th[:, t * P:(t + 1) * P], sel_i, start=True, stop=False)
                        nc.tensor.matmul(o, gsum[:, t * P:(t + 1) * P], sel_f, start=False, stop=True)
                    nc.tensor.matmul(ps[0:MH, BK_B, 0:S], sel_i, th[:], start=True, stop=False)
                    nc.tensor.matmul(ps[0:MH, BK_B, 0:S], sel_f, gsum[:], start=False, stop=True).then_inc(a_done, 1)

                def scores():
                    for g in range(AG):
                        for j in range(NCH):
                            k0 = max(j - 1, 0) * CHUNK
                            for kv in range(AKV):
                                pr = slice(kv * DH, (kv + 1) * DH)
                                last = nc.tensor.matmul(ps[pr, g, j * P:(j + 1) * P],
                                                        aqT[pr, g, j * CHUNK:(j + 1) * CHUNK], akT[pr, k0:k0 + P],
                                                        start=True, stop=True)
                    last.then_inc(scores_done, 1)

                def decay_and_qk(h, blk=None):
                    pe.wait_ge(m_ready, l + 1)
                    pe.wait_ge(floor_ready, CREDIT + MH * l + h)
                    pe.wait_ge(cap_ready, CREDIT + 2 * (MH * l + h))
                    neg_m = cst[0:MH, C_NM + h * P:C_NM + (h + 1) * P]
                    neg_g = cst[0:2 * MH, C_NG + h * P:C_NG + (h + 1) * P]
                    nc.tensor.matmul(ps[:, 2, 0:S], neg_m, mrow[:], start=True, stop=True)
                    nc.tensor.matmul(ps[:, 2, S:2 * S], neg_g, gsum[:], start=True, stop=False)
                    nc.tensor.matmul(ps[:, 2, S:2 * S], neg_m, mrow[:], start=False, stop=True).then_inc(decay_done, 1)
                    pe.wait_ge(pm_ready, CREDIT + MH * l + h)
                    if blk is not None:
                        mixer_turn(blk, 3)
                    pr = slice((h % 2) * DQK, (h % 2 + 1) * DQK)
                    nc.tensor.matmul(ps[:, 3, 0:S], kT[pr, h // 2, 0:P], qT[pr, h // 2, :], start=True, stop=True)
                    nc.tensor.matmul(ps[:, 3, S:S + P], kT[pr, h // 2, P:S], qT[pr, h // 2, P:S], start=True,
                                     stop=True).then_inc(qk_done, 1)

                def numerator(h):
                    pe.wait_ge(pm_ready, CREDIT + MH * l + h + 1)
                    pe.wait_ge(hm_ready, CREDIT + MH * l + h)
                    pe.wait_ge(arow_ready, 2 * l + 2)
                    for o, w0, w1 in ((0, vm[:, 0, h * DV:(h + 1) * DV], vm[:, 1, h * DV:(h + 1) * DV]),
                                      (S, ones[:, 0:P], ones[:, 0:P])):
                        nc.tensor.matmul(ps[:, BK_B, o:o + S], w0, pm[:, 0:S], start=True, stop=False)
                        last = nc.tensor.matmul(ps[:, BK_B, o + P:o + S], w1, pm[:, S:S + P], start=False, stop=True)
                    last.then_inc(num_done, 1)

                def turn_probs():
                    pe.wait_ge(probs_ready, l + 1)
                    for r in range(AG * NCH):
                        last = nc.tensor.transpose(ps[:, r // 4, (r % 4) * P:(r % 4 + 1) * P], sc[:, r, :], ident)
                        if r % 4 == 3:
                            last.then_inc(probs_turned, 1)

                def attend():
                    pe.wait_ge(pT_ready, 2 * l + 2)
                    for g in range(AG):
                        for j in range(NCH):
                            for kv in range(AKV):
                                last = nc.tensor.matmul(
                                    ps[g * DH:(g + 1) * DH, BK_A, kv * S + j * CHUNK:kv * S + (j + 1) * CHUNK],
                                    av[:, max(j - 1, 0), kv * DH:(kv + 1) * DH],
                                    pT[:, g * NCH + j, kv * CHUNK:(kv + 1) * CHUNK], start=True, stop=True)
                    last.then_inc(attn_done, 1)

                def sum_heads(b):
                    pe.wait_ge(hmsq_ready, CREDIT + MH * l + 2 * b + 2)
                    for h in (2 * b, 2 * b + 1):
                        o = ps[:, b, (h % 2) * S:(h % 2 + 1) * S]
                        nc.tensor.matmul(o, ones[:, 0:P], sq[:, h, :], start=True, stop=False)
                        last = nc.tensor.matmul(o, ones[:, 0:P], qe[h], start=False, stop=True)
                    last.then_inc(hmsum_done, 1)

                def mixer_turn(b, bank):
                    ada_turn(block_no(l, 1, b), bank, TURN_AT if bank == 3 else 0, b % 2)

                def mix_out(b, groups):
                    m = N_IN + b
                    if groups[0] == 0:
                        take(m % 3, l, MIX0 + m // 3)
                        nc.tensor.matmul(ps[:, b, 0:1], zeros[:], ones[:, 0:1], start=True, stop=False,
                                         skip_group_check=True)
                    for n in groups:
                        k0 = (6, 4, 0, 2)[n]
                        if b == 0:
                            pe.wait_ge(mix_lo, 4 * l + n + 1)
                        for k in (k0, k0 + 1):
                            for j in range(2):
                                last = product(ps[:, b, j * S:(j + 1) * S], panel(hi, m % 3)[:, k, j * P:(j + 1) * P],
                                               panel(lo, m % 3)[:, k, j * P:(j + 1) * P], mix_tile("hi", k0)[:, k - k0, :],
                                               mix_tile("lo", k0)[:, k - k0, :], False, k == 3)
                    if groups[-1] == 3:
                        mix_release(m, last)

                pre(0)
                ffn(0, 0, 0)
                post(0)
                pre(1)
                project(0, 1)
                gates()
                project(1)
                mixer_turn(0, BK_A)
                project_aq()
                log_weights()
                project(3)
                decay_and_qk(0, 1)
                pe.wait_ge(proj_read, N_READ * l + 4)
                project_tokens(4)
                pe.wait_ge(mods_ready, CREDIT + block_no(l, 1, 1))
                turn_values()
                scores()
                pe.wait_ge(proj_read, N_READ * l + 5)
                numerator(0)
                decay_and_qk(1, 2)
                project_tokens(5)
                numerator(1)
                decay_and_qk(2)
                project(6)
                pe.wait_ge(proj_read, N_READ * l + 6)
                numerator(2)
                decay_and_qk(3, 3)
                turn_probs()
                project(7)
                numerator(3)
                attend()
                sum_heads(0)
                project(8)
                sum_heads(1)
                project(9)
                pe.wait_ge(mix_f32, 4 * l + 1)
                mixer_turn(4, BK_A)
                project(10)
                pe.wait_ge(hmstd_ready, 2 * l + 2)
                for b in range(2):
                    mix_out(b, (0, 1, 2))
                for b in range(2):
                    mix_out(b, (3,))
                mix_out(2, range(4))
                pe.wait_ge(mods_ready, CREDIT + block_no(l, 1, THIRD - 1))
                for b in range(2):
                    sum_bank(BK_Y, ysq_ready, 4 * (3 * l + 1), b)
                mixer_turn(THIRD - 1, BK_GATE)
                mix_out(3, (0, 1))
                sum_bank(BK_Y, ysq_ready, 4 * (3 * l + 1), 2)
                mix_out(3, (2, 3))
                post(1)
                pre(2)
                ffn(FFB0, 2, 2)
                post(2)

            pe.wait_ge(ystd_ready, 3 * DEPTH)
            for t in range(2):
                last = nc.tensor.transpose(ps[:, BK_UP, t * P:(t + 1) * P], std[:, t * P:(t + 1) * P], ident)
            last.then_inc(o_std_turned, 1)
            for b in range(4):
                pe.wait_ge(x_tile, 4 * (3 * DEPTH) + b + 1)
                for k in (2 * b, 2 * b + 1):
                    for t in range(2):
                        n = 2 * (k // 4) + t
                        if n == 2 and k == 4:
                            pe.wait_ge(o_scale_ready, 1)
                        if n == 3 and k == 4:
                            pe.wait_ge(mods_ready, CREDIT + (block_no(DEPTH, 0) - 1))
                        last = nc.tensor.transpose(ps[:, BK_OUT[n], (k % 4) * P:(k % 4 + 1) * P],
                                                   xT[:, k, t * P:(t + 1) * P], ident)
                if b % 2:
                    last.then_inc(o_turned, 1)


_INS = ["x", "c", "ada_w", "ada_b", "norm_pre", "norm_post", "ffn_w_gate", "ffn_w_up", "ffn_w_down", "w_in",
        "mlstm_igate_bias", "mlstm_fgate_bias", "mlstm_head_norm", "conv_w", "attn_sinks", "rel_bias_table", "w_out"]


def kernel(**inputs):
    import concourse.bacc as bacc
    from concourse.bass_utils import run_bass_kernel_spmd

    nc = bacc.Bacc("TRN2", target_bir_lowering=False, num_devices=1)
    arrays, args = {}, []
    for name in _INS + ["constants"]:
        a = constant_table() if name == "constants" else np.ascontiguousarray(inputs[name])
        arrays[f"in_{name}"] = a
        args.append(nc.dram_tensor(f"in_{name}", a.shape, mybir.dt.from_np(a.dtype), kind="ExternalInput").ap())
    args.append(nc.dram_tensor("out_x", (1, S, D), F32, kind="ExternalOutput").ap())
    build(nc, *args)
    r = run_bass_kernel_spmd(nc, [arrays], core_ids=[0])
    return r.results[0]["out_x"]
```
